# Optimizing a Trainium2 kernel written in Bass

```python
import math
import jax
import jax.numpy as jnp
from jax import lax
import numpy as np

D_MODEL = 1024
BATCH = 1
SEQ = 256
DEPTH = 2

CTX_LEN = 256
GRID_W = 64
N_EVEN = (DEPTH + 1) // 2
N_ODD = DEPTH // 2
EPS = 1e-6

MLA_HEADS = 8
QK_NOPE = 64
QK_ROPE = 32
QK_HEAD = QK_NOPE + QK_ROPE
V_HEAD = 64
Q_LORA = 256
KV_LORA = 128
MLA_WIDTH = MLA_HEADS * V_HEAD
ROPE_BASE = 10000.0
ATTN_BLOCK = 128

S5_WIDTH = 512
S5_GROUP = 16
S5_GROUPS = S5_WIDTH // S5_GROUP
S5_STATE = 64
S5_MIN_STEP = 1e-3
S5_MAX_STEP = 1e-1

EVEN_IN = Q_LORA + KV_LORA + QK_ROPE + S5_WIDTH
EVEN_OUT = MLA_WIDTH + S5_WIDTH

HY_WIDTH = D_MODEL
FILT_EMB = 33
FILT_BANDS = (FILT_EMB - 1) // 2
FILT_HIDDEN = 64
SHORT_CONV = 3
HY_MIN_DECAY = -math.log(1e-2) / 1.5
HY_MAX_DECAY = -math.log(1e-2) / 0.3

N_EXPERTS = 64
TOP_K = 6
EXPERT_FF = 256
SHARED_FF = 256
ROUTE_SCALE = 2.5
MOE_BLOCK = 256

kernel_name = 'hybrid_mla_s5_hyena_moe_prefix_dit'

def rmsnorm(x, g=None):
    xf = x.astype(jnp.float32)
    y = xf * lax.rsqrt(jnp.mean(xf * xf, axis=-1, keepdims=True) + EPS)
    if g is not None:
        y = y * g.astype(jnp.float32)
    return y.astype(x.dtype)

def modulate(h, shift, scale):
    return h * (1.0 + scale) + shift

def axial_rope_tables(rows):
    t = jnp.arange(rows * GRID_W)
    row = (t // GRID_W).astype(jnp.float32)
    col = (t % GRID_W).astype(jnp.float32)
    n_freq = QK_ROPE // 4
    inv = ROPE_BASE ** (-jnp.arange(n_freq, dtype=jnp.float32) / n_freq)
    ang = jnp.concatenate([row[:, None] * inv, col[:, None] * inv], axis=-1)
    return jnp.cos(ang), jnp.sin(ang)

def apply_rope(x, cos, sin):
    xf = x.astype(jnp.float32).reshape(x.shape[:-1] + (QK_ROPE // 2, 2))
    xr, xi = xf[..., 0], xf[..., 1]
    cs, sn = cos[:, None, :], sin[:, None, :]
    out = jnp.stack([xr * cs - xi * sn, xr * sn + xi * cs], axis=-1)
    return out.reshape(x.shape).astype(x.dtype)

def rope_tail(t, cos, sin):
    return jnp.concatenate([t[..., :QK_NOPE], apply_rope(t[..., QK_NOPE:], cos, sin)], axis=-1)

def mla_keys_values(part, kv_norm, w_ukv, k_qk, cos, sin):
    B, L, _ = part.shape
    c_kv = rmsnorm(part[..., :KV_LORA], kv_norm)
    kv = (c_kv @ w_ukv).reshape(B, L, MLA_HEADS, QK_NOPE + V_HEAD)
    k_r = jnp.broadcast_to(part[..., None, KV_LORA:KV_LORA + QK_ROPE], (B, L, MLA_HEADS, QK_ROPE))
    k = rmsnorm(jnp.concatenate([kv[..., :QK_NOPE], k_r], axis=-1), k_qk)
    if cos is not None:
        k = rope_tail(k, cos, sin)
    return k, kv[..., QK_NOPE:]

def attend_blocked(q, k, v):
    B, L, H, Dk = q.shape
    nb = L // ATTN_BLOCK
    qb = q.reshape(B, nb, ATTN_BLOCK, H, Dk).transpose(1, 0, 2, 3, 4)
    scale = QK_HEAD ** -0.5

    def one_block(q_blk):
        s = jnp.einsum('bqhd,bkhd->bhqk', q_blk, k, preferred_element_type=jnp.float32) * scale
        p = jax.nn.softmax(s, axis=-1)
        return jnp.einsum('bhqk,bkhd->bqhd', p.astype(v.dtype), v)

    o = lax.map(one_block, qb)
    return o.transpose(1, 0, 2, 3, 4).reshape(B, L, H * v.shape[-1])

def _ssm_combine(left, right):
    a_l, b_l = left
    a_r, b_r = right
    return a_r * a_l, a_r * b_l + b_r

def s5_scan(u, lam_bar, b_bar, s0=None):
    bu = jnp.einsum('blgh,gph->blgp', u.astype(jnp.complex64), b_bar)
    if s0 is not None:
        bu = bu.at[:, 0].add(lam_bar * s0)
    a = jnp.broadcast_to(lam_bar, bu.shape)
    _, states = lax.associative_scan(_ssm_combine, (a, bu), axis=1)
    return states

def s5_mixer(u, u_ctx, lam_re, lam_im, log_step, b_re, b_im, c_re, c_im, d_skip, glu_w, glu_b):
    B, L, _ = u.shape
    Lc = u_ctx.shape[1]
    ug = u.astype(jnp.float32).reshape(B, L, S5_GROUPS, S5_GROUP)
    ugc = u_ctx.astype(jnp.float32).reshape(B, Lc, S5_GROUPS, S5_GROUP)
    y = ug * d_skip.astype(jnp.float32).reshape(S5_GROUPS, S5_GROUP)
    for direction in range(2):
        lam = lax.complex(jnp.minimum(lam_re[direction].astype(jnp.float32), -1e-4),
                          lam_im[direction].astype(jnp.float32))
        step = jnp.exp(log_step[direction].astype(jnp.float32))[:, None]
        lam_bar = jnp.exp(lam * step)
        b_mat = lax.complex(b_re[direction].astype(jnp.float32), b_im[direction].astype(jnp.float32))
        b_bar = ((lam_bar - 1.0) / lam)[..., None] * b_mat
        c_mat = lax.complex(c_re[direction].astype(jnp.float32), c_im[direction].astype(jnp.float32))
        if direction == 0:
            uc, ul = ugc, ug
        else:
            uc, ul = ugc[:, ::-1], ug[:, ::-1]
        ctx_final = s5_scan(uc, lam_bar, b_bar)[:, -1]
        states = s5_scan(ul, lam_bar, b_bar, ctx_final)
        yd = jnp.einsum('blgp,ghp->blgh', states, c_mat).real
        y = y + (yd if direction == 0 else yd[:, ::-1])
    y = y.reshape(B, L, S5_WIDTH)
    z = jax.nn.gelu(y)
    out = z * jax.nn.sigmoid(z @ glu_w.astype(jnp.float32) + glu_b.astype(jnp.float32))
    return out.astype(u.dtype)

def even_mixer(h, h_ctx, cos, sin, w_in, q_norm, w_uq, kv_norm, w_ukv, q_qk, k_qk,
               lam_re, lam_im, log_step, b_re, b_im, c_re, c_im, d_skip, glu_w, glu_b, w_out):
    B, L, _ = h.shape
    proj = h @ w_in
    proj_ctx = h_ctx @ w_in[:, Q_LORA:]
    q = (rmsnorm(proj[..., :Q_LORA], q_norm) @ w_uq).reshape(B, L, MLA_HEADS, QK_HEAD)
    q = rope_tail(rmsnorm(q, q_qk), cos, sin)
    k_lat, v_lat = mla_keys_values(proj[..., Q_LORA:], kv_norm, w_ukv, k_qk, cos, sin)
    k_ctx, v_ctx = mla_keys_values(proj_ctx, kv_norm, w_ukv, k_qk, None, None)
    attn = attend_blocked(q, jnp.concatenate([k_lat, k_ctx], axis=1),
                          jnp.concatenate([v_lat, v_ctx], axis=1))
    s5 = s5_mixer(proj[..., Q_LORA + KV_LORA + QK_ROPE:], proj_ctx[..., KV_LORA + QK_ROPE:],
                  lam_re, lam_im, log_step, b_re, b_im, c_re, c_im, d_skip, glu_w, glu_b)
    return jnp.concatenate([attn, s5], axis=-1) @ w_out

def hyena_filter(L, w1, b1, w2, b2, w3, freq):
    f32 = jnp.float32
    t = jnp.linspace(0.0, 1.0, L, dtype=f32)[:, None]
    ang = 2.0 * math.pi * jnp.arange(L, dtype=f32)[:, None] / L
    bands = jnp.linspace(1e-4, FILT_BANDS - 1, FILT_BANDS, dtype=f32)
    z = jnp.concatenate([t, jnp.cos(bands * ang), -jnp.sin(bands * ang)], axis=-1)
    fr = freq.astype(f32)
    hid = jnp.sin(fr * (z @ w1.astype(f32) + b1.astype(f32)))
    hid = jnp.sin(fr * (hid @ w2.astype(f32) + b2.astype(f32)))
    hf = (hid @ w3.astype(f32)).reshape(L, 2, HY_WIDTH)
    deltas = jnp.linspace(HY_MIN_DECAY, HY_MAX_DECAY, HY_WIDTH, dtype=f32)
    hf = hf * jnp.exp(-t * deltas)[:, None, :]
    hf = hf * lax.rsqrt(jnp.sum(hf * hf, axis=(0, 1), keepdims=True) + EPS)
    return hf[:, 0], hf[:, 1]

def bidir_long_conv(z, h_fwd, h_bwd):
    B, L, Dh = z.shape
    zeros = jnp.zeros((L, Dh), jnp.float32)
    circ = (jnp.concatenate([h_fwd, zeros], axis=0)
            + jnp.concatenate([h_bwd[:1], zeros, h_bwd[:0:-1]], axis=0))
    zf = jnp.fft.rfft(z.astype(jnp.float32), n=2 * L, axis=1)
    cf = jnp.fft.rfft(circ, axis=0)
    return jnp.fft.irfft(zf * cf[None], n=2 * L, axis=1)[:, :L]

def hyena_mixer(h, w_in, conv_w, conv_b, f_w1, f_b1, f_w2, f_b2, f_w3, f_freq, bias, w_out):
    B, L, _ = h.shape
    p = h @ w_in
    pad = SHORT_CONV // 2
    pp = jnp.pad(p, ((0, 0), (pad, pad), (0, 0)))
    p = sum(pp[:, j:j + L] * conv_w[j] for j in range(SHORT_CONV)) + conv_b
    x0, x1, v = jnp.split(p, 3, axis=-1)
    h_fwd, h_bwd = hyena_filter(L, f_w1, f_b1, f_w2, f_b2, f_w3, f_freq)
    z = (v * x1).astype(jnp.float32)
    z = bidir_long_conv(z, h_fwd, h_bwd) + bias.astype(jnp.float32) * z
    y = x0 * z.astype(x0.dtype)
    return y @ w_out

def moe(h, router_w, router_b, w_gate, w_up, w_down, sh_gate, sh_up, sh_down):
    B, L, Dm = h.shape
    xf = h.reshape(B * L, Dm)
    T = B * L
    TK = T * TOP_K
    scores = jax.nn.sigmoid(jnp.einsum('td,de->te', xf, router_w, preferred_element_type=jnp.float32))
    _, idx = lax.top_k(scores + router_b.astype(jnp.float32), TOP_K)
    sel = jnp.take_along_axis(scores, idx, axis=-1)
    wts = sel / jnp.sum(sel, axis=-1, keepdims=True) * ROUTE_SCALE
    flat_e = idx.reshape(TK)
    order = jnp.argsort(flat_e)
    sorted_e = flat_e[order]
    counts = jnp.bincount(flat_e, length=N_EXPERTS)
    padded = (counts + MOE_BLOCK - 1) // MOE_BLOCK * MOE_BLOCK
    pad_end = jnp.cumsum(padded)
    pad_start = pad_end - padded
    start = jnp.cumsum(counts) - counts
    dest = pad_start[sorted_e] + jnp.arange(TK, dtype=jnp.int32) - start[sorted_e]
    n_blocks = -(-TK // MOE_BLOCK) + N_EXPERTS
    n_rows = n_blocks * MOE_BLOCK
    row_tok = jnp.zeros((n_rows,), jnp.int32).at[dest].set((order // TOP_K).astype(jnp.int32))
    row_w = jnp.zeros((n_rows,), jnp.float32).at[dest].set(wts.reshape(TK)[order])
    block_start = jnp.arange(n_blocks, dtype=jnp.int32) * MOE_BLOCK
    block_e = jnp.minimum(jnp.searchsorted(pad_end, block_start, side='right'), N_EXPERTS - 1)

    def expert_block(args):
        toks, w, e = args
        xb = xf[toks]
        hid = jax.nn.silu(xb @ w_gate[e]) * (xb @ w_up[e])
        return (hid @ w_down[e]) * w[:, None].astype(xb.dtype)

    ys = lax.map(expert_block, (row_tok.reshape(n_blocks, MOE_BLOCK),
                                row_w.reshape(n_blocks, MOE_BLOCK), block_e))
    routed = jnp.zeros_like(xf).at[row_tok].add(ys.reshape(n_rows, Dm))
    shared = (jax.nn.silu(xf @ sh_gate) * (xf @ sh_up)) @ sh_down
    return (routed + shared).reshape(B, L, Dm)

def setup_inputs(seed: int = 0) -> dict:
    key = jax.random.key(seed)
    ks = iter(jax.random.split(key, 64))
    f32 = jnp.float32
    D = D_MODEL

    def nrm(shape, s):
        return jax.random.normal(next(ks), shape, f32) * s

    n_idx = jnp.arange(S5_STATE, dtype=f32)
    s5_shape = (N_EVEN, 2, S5_GROUPS, S5_STATE)
    return {
        'x': nrm((BATCH, SEQ, D), 1.0),
        'c': nrm((BATCH, D), 1.0),
        'ctx': nrm((BATCH, CTX_LEN, D), 1.0),
        'c_ctx': nrm((D,), 1.0),
        'ada_w': nrm((DEPTH, D, 6 * D), 0.5 * D ** -0.5),
        'ada_b': nrm((DEPTH, 6 * D), 0.02),
        'ev_w_in': nrm((N_EVEN, D, EVEN_IN), D ** -0.5),
        'mla_q_norm': 1.0 + nrm((N_EVEN, Q_LORA), 0.05),
        'mla_w_uq': nrm((N_EVEN, Q_LORA, MLA_HEADS * QK_HEAD), Q_LORA ** -0.5),
        'mla_kv_norm': 1.0 + nrm((N_EVEN, KV_LORA), 0.05),
        'mla_w_ukv': nrm((N_EVEN, KV_LORA, MLA_HEADS * (QK_NOPE + V_HEAD)), KV_LORA ** -0.5),
        'mla_q_qknorm': 1.0 + nrm((N_EVEN, QK_HEAD), 0.05),
        'mla_k_qknorm': 1.0 + nrm((N_EVEN, QK_HEAD), 0.05),
        's5_lam_re': -0.5 * jnp.exp(nrm(s5_shape, 0.05)),
        's5_lam_im': math.pi * n_idx + nrm(s5_shape, 0.05),
        's5_log_step': jax.random.uniform(next(ks), (N_EVEN, 2, S5_GROUPS), f32,
                                          math.log(S5_MIN_STEP), math.log(S5_MAX_STEP)),
        's5_b_re': nrm((N_EVEN, 2, S5_GROUPS, S5_STATE, S5_GROUP), (2.0 * S5_GROUP) ** -0.5),
        's5_b_im': nrm((N_EVEN, 2, S5_GROUPS, S5_STATE, S5_GROUP), (2.0 * S5_GROUP) ** -0.5),
        's5_c_re': nrm((N_EVEN, 2, S5_GROUPS, S5_GROUP, S5_STATE), 0.5 ** 0.5),
        's5_c_im': nrm((N_EVEN, 2, S5_GROUPS, S5_GROUP, S5_STATE), 0.5 ** 0.5),
        's5_d': nrm((N_EVEN, S5_WIDTH), 1.0),
        's5_glu_w': nrm((N_EVEN, S5_WIDTH, S5_WIDTH), S5_WIDTH ** -0.5),
        's5_glu_b': nrm((N_EVEN, S5_WIDTH), 0.02),
        'ev_w_out': nrm((N_EVEN, EVEN_OUT, D), EVEN_OUT ** -0.5),
        'hy_w_in': nrm((N_ODD, D, 3 * HY_WIDTH), D ** -0.5),
        'hy_conv_w': nrm((N_ODD, SHORT_CONV, 3 * HY_WIDTH), SHORT_CONV ** -0.5),
        'hy_conv_b': nrm((N_ODD, 3 * HY_WIDTH), 0.02),
        'hy_f_w1': nrm((N_ODD, FILT_EMB, FILT_HIDDEN), FILT_EMB ** -0.5),
        'hy_f_b1': nrm((N_ODD, FILT_HIDDEN), 0.02),
        'hy_f_w2': nrm((N_ODD, FILT_HIDDEN, FILT_HIDDEN), FILT_HIDDEN ** -0.5),
        'hy_f_b2': nrm((N_ODD, FILT_HIDDEN), 0.02),
        'hy_f_w3': nrm((N_ODD, FILT_HIDDEN, 2 * HY_WIDTH), FILT_HIDDEN ** -0.5),
        'hy_f_freq': 1.0 + nrm((N_ODD, FILT_HIDDEN), 0.05),
        'hy_bias': nrm((N_ODD, HY_WIDTH), 1.0),
        'hy_w_out': nrm((N_ODD, HY_WIDTH, D), HY_WIDTH ** -0.5),
        'moe_router_w': nrm((DEPTH, D, N_EXPERTS), D ** -0.5),
        'moe_router_b': nrm((DEPTH, N_EXPERTS), 0.01),
        'moe_w_gate': nrm((DEPTH, N_EXPERTS, D, EXPERT_FF), D ** -0.5),
        'moe_w_up': nrm((DEPTH, N_EXPERTS, D, EXPERT_FF), D ** -0.5),
        'moe_w_down': nrm((DEPTH, N_EXPERTS, EXPERT_FF, D), EXPERT_FF ** -0.5),
        'moe_sh_gate': nrm((DEPTH, D, SHARED_FF), D ** -0.5),
        'moe_sh_up': nrm((DEPTH, D, SHARED_FF), D ** -0.5),
        'moe_sh_down': nrm((DEPTH, SHARED_FF, D), SHARED_FF ** -0.5),
    }

def reference(x, c, ctx, c_ctx, ada_w, ada_b,
              ev_w_in, mla_q_norm, mla_w_uq, mla_kv_norm, mla_w_ukv, mla_q_qknorm, mla_k_qknorm,
              s5_lam_re, s5_lam_im, s5_log_step, s5_b_re, s5_b_im, s5_c_re, s5_c_im, s5_d,
              s5_glu_w, s5_glu_b, ev_w_out,
              hy_w_in, hy_conv_w, hy_conv_b, hy_f_w1, hy_f_b1, hy_f_w2, hy_f_b2, hy_f_w3, hy_f_freq,
              hy_bias, hy_w_out,
              moe_router_w, moe_router_b, moe_w_gate, moe_w_up, moe_w_down,
              moe_sh_gate, moe_sh_up, moe_sh_down):
    B, L, D = x.shape
    rows = L // GRID_W
    cos, sin = axial_rope_tables(rows)
    sc = jax.nn.silu(c)
    sc_ctx = jax.nn.silu(c_ctx)
    for li in range(DEPTH):
        mod = sc @ ada_w[li] + ada_b[li]
        sh1, sc1, g1, sh2, sc2, g2 = jnp.split(mod[:, None, :], 6, axis=-1)
        h = modulate(rmsnorm(x), sh1, sc1)
        if li % 2 == 0:
            e = li // 2
            mod_ctx = sc_ctx @ ada_w[li][:, :2 * D] + ada_b[li][:2 * D]
            h_ctx = modulate(rmsnorm(ctx), mod_ctx[:D], mod_ctx[D:])
            mix = even_mixer(h, h_ctx, cos, sin, ev_w_in[e], mla_q_norm[e], mla_w_uq[e], mla_kv_norm[e],
                             mla_w_ukv[e], mla_q_qknorm[e], mla_k_qknorm[e],
                             s5_lam_re[e], s5_lam_im[e], s5_log_step[e], s5_b_re[e], s5_b_im[e],
                             s5_c_re[e], s5_c_im[e], s5_d[e], s5_glu_w[e], s5_glu_b[e], ev_w_out[e])
        else:
            o = li // 2
            mix = hyena_mixer(h, hy_w_in[o], hy_conv_w[o], hy_conv_b[o], hy_f_w1[o], hy_f_b1[o],
                              hy_f_w2[o], hy_f_b2[o], hy_f_w3[o], hy_f_freq[o], hy_bias[o], hy_w_out[o])
        x = x + g1 * mix
        h = modulate(rmsnorm(x), sh2, sc2)
        x = x + g2 * moe(h, moe_router_w[li], moe_router_b[li], moe_w_gate[li], moe_w_up[li],
                         moe_w_down[li], moe_sh_gate[li], moe_sh_up[li], moe_sh_down[li])
    return x


_drawn_inputs = setup_inputs


def setup_inputs(seed=0):
    import zlib

    import numpy as np

    out = dict(_drawn_inputs(seed))
    spreads = {}
    factors = {'mla_q_norm': 3.634,
     'mla_q_qknorm': 3.599,
     'mla_k_qknorm': 6.802,
     's5_lam_re': 3.107,
     's5_glu_b': 6.479}
    for name, (base, spread) in spreads.items():
        noise = np.random.default_rng([zlib.crc32(name.encode()), seed]).standard_normal(out[name].shape)
        drawn = base * np.exp(spread * noise) if base else spread * noise
        out[name] = jnp.asarray(drawn.astype(out[name].dtype))
    for name, factor in factors.items():
        out[name] = (out[name] * factor).astype(out[name].dtype)
    return out
```

```python
import math
from contextlib import ExitStack

import numpy as np
import concourse.bass as bass
from concourse import mybir

F32 = mybir.dt.float32
ALU = mybir.AluOpType
ACT = mybir.ActivationFunctionType
AX = mybir.AxisListType

P = 128
D = 1024
KD = D // P
L = 256
EPS = 1e-6
HEADS, NOPE, ROPE, VH = 8, 64, 32, 64
QKH = NOPE + ROPE
QL, KVL = 256, 128
G5, C5, N5 = 32, 16, 64
T5 = 8
NCH = 2 * L // T5
XCH = L // T5
NT5 = G5
GP = G5 // 2
TW = T5 * C5
UOFF = QL + KVL + ROPE
EVIN = UOFF + G5 * C5
NE, TOPK, FF = 64, 6, 256
ROUTE_SCALE = 2.5
HYW = 1024
FH, FE = 64, 33
RING = 4
WEXP = KD * FF * 2 + (FF // P) * D
ADC = 512
NADC = 2 * 6 * D // ADC
TWO_PI = 2.0 * math.pi
PI_HI = 6.28125
PI_LO = TWO_PI - PI_HI
ROUND = 12582912.0
PI_SAFE = 3.1415925


def offsets(widths):
    out, at = {}, 0
    for name, width in widths:
        out[name] = (at, width)
        at += width
    return out, at


COLS, NCOLS = offsets((("ada_b", 2 * 48 * 2), ("c", KD * 2), ("qn", 2), ("kvn", 1), ("qqk", 1), ("kqk", 1),
                       ("glub", 4), ("convw", 3 * 24), ("convb", 24), ("hybias", 8), ("fb1", 1), ("fb2", 1),
                       ("freq", 1), ("s5d", GP)))
S5P, NS5P = offsets((("lre", NT5), ("lim", NT5), ("lst", NT5), ("br", NT5 * C5), ("bi", NT5 * C5),
                     ("cr", NT5 * C5), ("ci", NT5 * C5)))
CST, NCST = offsets((("ident", P), ("cos", L), ("sin", L), ("swap", QKH), ("eye16", C5)))
HCST, NHCST = offsets((("fc", 2 * L), ("fs", 2 * L), ("ic", 2 * L), ("is", 2 * L), ("decay", 2 * HYW), ("zemb", L)))


class Chain:

    def __init__(self, eng, semaphore, sem):
        self.eng, self.own, self.sem, self.n, self.counts = eng, semaphore, sem, 0, {}

    def __call__(self, ins):
        self.n += 1
        ins.then_inc(self.own, 1)
        self.eng.wait_ge(self.own, self.n)

    def then(self, ins, name):
        self.counts[name] = self.counts.get(name, 0) + 1
        ins.then_inc(self.sem(name), 1)
        self.eng.wait_ge(self.sem(name), self.counts[name])


def program(nc, A):
    with ExitStack() as ctx:
        sems = {}

        def sem(name):
            if name not in sems:
                sems[name] = ctx.enter_context(nc.semaphore(name))
            return sems[name]

        NAR = 53100
        ar = ctx.enter_context(nc.sbuf_tensor("arena", [P, NAR], F32))
        ps = ctx.enter_context(nc.psum_tensor("ps", [P, 8, 512], F32))
        scr = {n: nc.dram_tensor(n, sh, F32, kind="Internal").ap()
               for n, sh in (("u_scr", [G5 * C5, T5, NCH]), ("k_scr", [2 * C5, GP, 15 * C5]),
                             ("y_scr", [TW, G5, XCH]), ("w_scr", [2, NE, L]))}
        top = [0]

        def region(width):
            a = top[0]
            top[0] += width
            assert top[0] <= NAR, top
            return a

        def at(a, width, rows=P):
            return ar[0:rows, a:a + width]

        r_cst, r_cols, r_x, r_h = region(NCST), region(NCOLS), region(KD * L), region(2 * KD * L)
        r_mod, r_ones, r_row, r_sc = region(192), region(P), region(1024), region(16)
        r_eps, r_st = region(1), region(34)
        r_free = top[0]
        ident = at(r_cst, P)
        ones = at(r_ones, P)

        def cst(name, rows=P):
            a, w = CST[name]
            return at(r_cst + a, w, rows)

        def col(name, i=0, n=1, rows=P):
            return at(r_cols + COLS[name][0] + i, n, rows)

        def tiles(a, k, n, rows=P):
            return at(a, k * n, rows).rearrange("p (k t) -> p k t", k=k)

        xT = tiles(r_x, KD, L)
        hT = tiles(r_h, KD, 2 * L)
        hX = tiles(r_h, KD, L)
        sqX = tiles(r_h + KD * L, KD, L)
        mod = at(r_mod, 192).rearrange("p (l j k m) -> p l j k m", l=2, j=6, k=KD)
        modc = at(r_mod, 192).rearrange("p (c m) -> p c m", m=2)
        sc = at(r_sc, 16).rearrange("p (k m) -> p k m", m=2)
        adrow = at(r_row, 1024, 2).rearrange("p (b n) -> p b n", b=2)
        rsx = at(r_row, 512)
        stx = at(r_row + 512, 512)

        r1 = region(8192)
        r2 = region(2 * NT5 * 144)
        r3 = region(8192)
        r4 = region(4096)
        r6 = region(35 * 64)
        r7 = region(4096)
        r8 = region(2560)
        r9 = region(NS5P)
        r10 = region(3000)

        adw = at(r1, 8192).rearrange("p (b k n) -> p b k n", b=2, k=KD)
        w_in = tiles(r1, KD, EVIN)
        kh = tiles(r1, HEADS, 2 * L, QKH)
        qh = tiles(r1 + 4096, HEADS, L, QKH)
        vt = tiles(r1 + 6144, 4, 512)
        glu_w = tiles(r1, 4, 512)
        ctr = at(r2, NT5 * 144).rearrange("p (g d j c) -> p g d j c", d=2, j=9, c=C5)
        ctn = at(r2 + NT5 * 144, NT5 * 144).rearrange("p (g d j c) -> p g d j c", d=2, j=9, c=C5)
        bm = at(r3, 8192).rearrange("p (t r m) -> p t r m", t=NT5, r=2)
        sqk = tiles(r3, HEADS, 2 * L, QKH)
        sqq = tiles(r3 + 4096, HEADS, L, QKH)
        w_out = tiles(r3, KD, D)
        toep = tiles(r4, G5, TW)
        st = at(r6, 35 * 64).rearrange("p (s r t) -> p s r t", r=2, t=NT5)
        bt = at(r7, 4096).rearrange("p (b r t m) -> p b r t m", b=2, r=2, t=8)
        U = tiles(r7, G5, NCH)
        u_sb = at(r7 + 2048, 2048).rearrange("p (i t c) -> p i t c", i=4, t=T5)
        prob = tiles(r7 + 2048, 2, 512)
        att = tiles(r7 + 3072, 4, L)
        ysb = tiles(r3, G5, XCH)
        w_uq = tiles(r8, 2, 768)
        w_ukv = at(r8 + 1536, 1024)
        cx = tiles(r9, KD, L)
        pT = at(r9, 2048).rearrange("p (b k t) -> p b k t", b=2, k=4)
        kvl, krl, ql = at(r9, 512), at(r9 + 512, 512, QKH), tiles(r9 + 1024, 2, L)
        kk = at(r_h, GP * 240, 2 * C5).rearrange("p (g j c) -> p g j c", j=15, c=C5)
        est = at(r_h, 4096).rearrange("p (s r t) -> p s r t", r=2, t=NT5)
        sql = tiles(r_h, 3, 512)
        yT = at(r10 + 0, 1024).rearrange("p (i t c) -> p i t c", i=4, t=T5)
        zT = tiles(r10 + 1024, 4, L)

        def s5(name):
            a, w = S5P[name]
            v = at(r9 + a, w)
            return v if w == NT5 else v.rearrange("p (t c) -> p t c", c=C5)

        def sm(i, n=1):
            return at(r10 + NT5 * i, NT5 * n)
        pw = at(r10 + NT5 * 30, 18 * NT5).rearrange("p (r j t) -> p r j t", r=2, j=9)
        fb = at(r10 + NT5 * 48, 2 * NT5 * C5).rearrange("p (r t c) -> p r t c", r=2, c=C5)
        tmp5 = r10 + NT5 * 81
        bdr = at(r4, NT5 * 32).rearrange("p (t m) -> p t m", m=32)
        bdi = at(r4 + NT5 * 32, NT5 * 32).rearrange("p (t m) -> p t m", m=32)
        big = at(r3, 4096)
        r11 = region(4 * TW)

        m1 = r_free
        wring = at(m1, RING * WEXP).rearrange("p (b n) -> p b n", b=RING)
        wbc = tiles(m1 + RING * WEXP, 2, L)
        sg = tiles(m1 + RING * WEXP + 512, 2, 512)
        hh = tiles(m1 + RING * WEXP + 1536, 2, 512)
        rw = tiles(m1 + RING * WEXP + 2560, KD, NE)
        rtb = m1 + RING * WEXP + 3072
        assert rtb + 24 * 64 <= NAR

        def wg(slot, k, f):
            a = k * FF + f * P
            return wring[:, slot, a:a + P]

        def wu(slot, k, f):
            a = KD * FF + k * FF + f * P
            return wring[:, slot, a:a + P]

        def wd(slot, f, j):
            a = 2 * KD * FF + f * D + j * P
            return wring[:, slot, a:a + P]

        hyw = at(m1, 3 * 4096).rearrange("p (b k n) -> p b k n", b=3, k=KD)
        hyo = tiles(m1, KD, D)
        hc0 = m1 + 3 * 4096
        xc = tiles(hc0 + NHCST, 24, L)
        ff0 = hc0 + NHCST + 24 * L
        pp = at(ff0, 2 * 4 * L).rearrange("p (b i t) -> p b i t", b=2, i=4)
        zt = tiles(ff0 + 2048, KD, L)
        zs = tiles(ff0 + 4096, 2, HYW)
        hf = tiles(ff0 + 6144, 4, HYW)
        HR, HS = tiles(ff0 + 10240, 2, HYW), tiles(ff0 + 12288, 2, HYW)
        f_w3 = at(ff0 + 14336, 2048, FH)
        f_w1 = at(ff0 + 16384, FH, FE)
        f_w2 = at(ff0 + 16384 + FH, FH, FH)
        hid = tiles(ff0 + 16512, 2, L, FH)
        hsc = ff0 + 17024
        hns = at(hsc + 1024, 8)
        YR, YS = tiles(ff0 + 6144, 2, HYW), tiles(ff0 + 8192, 2, HYW)
        ytmp = tiles(ff0 + 4096, 2, HYW)
        assert hsc + 1040 <= NAR, hsc

        def hcst(name, k=2, rows=P):
            a, w = HCST[name]
            v = at(hc0 + a, w, rows)
            return v if k == 1 else v.rearrange("p (k t) -> p k t", k=k)

        def scol(li, j, k, m=0):
            return mod[:, li, j, k, m:m + 1]

        def ada_turn(pe, i):
            pe.wait_ge(sem("adrow_ready"), i + 1)
            if i >= 1:
                pe.wait_ge(sem("modc_ready"), i)
            for j in range(4):
                last = pe.matmul(ps[:, 2, 2 * j:2 * j + 2], adrow[:, i % 2, j * P:(j + 1) * P], ident[0:2, 0:2], start=True, stop=True)
            last.then_inc(sem("ada_turned"), 1)

        def turned(act, f, ch, n):
            h, t = n // 2, n % 2
            act.wait_ge(sem("pT_mm"), n + 1)
            if h >= 2:
                act.wait_ge(sem("pv_mm"), h - 1)
            ch.then(f(pT[:, h % 2, :, t * P:(t + 1) * P], ps[:, 2 + n % 2, :].rearrange("p (k q) -> p k q", k=4), ACT.Copy), "pT_ready")

        def attend_out(dve, ch, h):
            dve.wait_ge(sem("pv_mm"), h + 1)
            rows = slice((h % 2) * VH, (h % 2 + 1) * VH)
            ch.then(dve.tensor_copy(att[rows, h // 2], ps[rows, 4 if h % 2 == 0 else 7, 0:L]), "att_ready")

        block = ctx.enter_context(nc.Block())

        @block.sync
        def _(sp):
            def load(dst, src, name, n=16):
                sp.dma_start(dst, src).then_inc(sem(name), 16)

            load(at(r_cols, NCOLS), A["cols"], "cols_in")
            load(at(r9, NS5P), A["s5p"], "s5p_in")
            load(at(r_cst, NCST), A["cst"], "cst_in")
            load(w_uq, A["w_uq"], "wuq_in")
            load(w_ukv, A["w_ukv"], "wukv_in")
            for i in range(NADC):
                if i >= 2:
                    sp.wait_ge(sem("ada_mm"), i - 1)
                load(adw[:, i % 2], A["ada_w"][i], f"ada_in{i % 2}")
            load(xT, A["xT"], "x_in")
            sp.wait_ge(sem("s5_params_used"), 1)
            load(cx, A["ctxT"], "ctx_in")
            sp.wait_ge(sem("ada_mm"), NADC)
            load(w_in, A["w_in"], "win_in")
            sp.wait_ge(sem("kk_ready"), 1)
            load(scr["k_scr"], kk.rearrange("p g j c -> p g (j c)"), "kscr_out")
            sp.wait_ge(sem("kscr_out"), 16)
            sp.wait_ge(sem("bd_used"), 1)
            for t in range(T5):
                for g2 in range(2):
                    load(toep[t * C5:(t + 1) * C5].rearrange("p (g b) m -> p g b m", b=2)[:, :, g2],
                         scr["k_scr"][g2 * C5:(g2 + 1) * C5, :, (T5 - 1 - t) * C5:(2 * T5 - 1 - t) * C5], "toep_in")
            sp.wait_ge(sem("u_evicted"), 4)
            load(scr["u_scr"].rearrange("(i p) t c -> p i (t c)", p=P), u_sb.rearrange("p i t c -> p i (t c)"), "uscr_out")
            sp.wait_ge(sem("uscr_out"), 16)
            for t in range(T5):
                load(U[t * C5:(t + 1) * C5], scr["u_scr"][:, t].rearrange("(g p) c -> p g c", p=C5), "U_in")
            sp.wait_ge(sem("scores_done"), 2 * HEADS)
            load(glu_w, A["glu_w"], "glu_in")
            sp.wait_ge(sem("y_evicted"), 2)
            load(scr["y_scr"], ysb, "yscr_out")
            sp.wait_ge(sem("yscr_out"), 16)
            for g8 in range(8):
                for i in range(4):
                    load(yT[g8 * C5:(g8 + 1) * C5, i],
                         scr["y_scr"].rearrange("(t p) g c -> p t g c", p=C5)[:, :, i * 8 + g8], "yT_in")
            load(w_out, A["ev_w_out"], "wout_in")

            def moe_loads(li):
                sp.wait_ge(sem("x_mixed"), li * 1 + 1)
                load(rw, A["router_w"][li], "rw_in")
                load(at(rtb, NE), A["router_b"][li:li + 1].broadcast_to([P, NE]), "rw_in")
                load(wring[:, 0], A["w_shared"][li], "w_slot0")
                for e in range(RING - 1):
                    load(wring[:, e + 1], A["w_experts"][li, e], f"w_slot{e + 1}")
                sp.wait_ge(sem("wT_ready"), li * 1 + 1)
                load(scr["w_scr"][li], at(rtb + 16 * 64, L, NE), "wscr_out")
                sp.wait_ge(sem("wscr_out"), li * 16 + 16)
                wsrc = scr["w_scr"]

                def weights_row(n, e):
                    load(wbc[:, n % 2], wsrc[li, e].rearrange("(a t) -> a t", a=1).broadcast_to([P, L]), f"wbc_in{n % 2}")
                weights_row(1, 0)
                weights_row(2, 1)
                for n in range(3, 5):
                    if n == 4:
                        sp.wait_ge(sem("down"), li * (NE + 1) + n - RING + 1)
                        load(wring[:, n % RING], A["w_experts"][li, n - 1], f"w_slot{n % RING}")
                    sp.wait_ge(sem("h_done"), li * (NE + 1) + n - 1)
                    weights_row(n, n - 1)
                with sp.Fori(0, (NE - RING) // RING) as i:
                    for q in range(RING):
                        n = 5 + q
                        sp.wait_ge(sem("down"), li * (NE + 1) + i * RING + (n - RING + 1))
                        sp.dma_start(wring[:, n % RING], A["w_experts"][li, i * RING + (n - 1)]).then_inc(sem(f"w_slot{n % RING}"), 16)
                        sp.wait_ge(sem("h_done"), li * (NE + 1) + i * RING + (n - 1))
                        sp.dma_start(wbc[:, n % 2], wsrc[li, i * RING + (n - 1)].rearrange("(a t) -> a t", a=1).broadcast_to([P, L])).then_inc(sem(f"wbc_in{n % 2}"), 16)

            moe_loads(0)
            sp.wait_ge(sem("moe_x"), 1)
            load(at(hc0, NHCST), A["hcst"], "hcst_in")
            load(f_w1, A["f_w1"], "fw_in")
            load(f_w2, A["f_w2"], "fw_in")
            load(f_w3, A["f_w3"], "fw_in")
            for i in range(6):
                if i >= 3:
                    sp.wait_ge(sem("hy_proj"), i - 2)
                load(hyw[:, i % 3], A["hy_w_in"][i], f"hyw_in{i % 3}")
            sp.wait_ge(sem("hy_proj"), 6)
            load(hyo, A["hy_w_out"], "hyo_in")
            moe_loads(1)
            sp.wait_ge(sem("moe_x"), 2)
            load(A["out"], xT, "out_done")
            sp.wait_ge(sem("out_done"), 16)

        @block.gpsimd
        def _(pool):
            ch = Chain(pool, sem("pool_chain"), sem)
            ch.then(pool.memset(ones, 1.0), "ones_ready")
            ch(pool.memset(st[:, 0], 0.0))
            lam8 = pw[:, :, 8]
            A8, B8 = tiles(tmp5, 2, NT5), tiles(tmp5 + 64, 2, NT5)
            t1, t2 = tiles(tmp5 + 128, 2, NT5), tiles(tmp5 + 192, 2, NT5)
            pool.wait_ge(sem("lam8_ready"), 1)
            pool.wait_ge(sem("est_ready"), 8)
            for k in range(NCH):
                a = k % 2 if k < NCH // 2 else 2 + k - NCH // 2
                b = (k + 1) % 2 if k + 1 < NCH // 2 else 2 + k + 1 - NCH // 2
                ins = pool.tensor_tensor(t1, A8, st[:, a], ALU.mult)
                ch(ins)
                ch(pool.tensor_tensor(t2, B8, st[:, a, ::-1], ALU.mult))
                ch(pool.tensor_tensor(t1, t1, est[:, k], ALU.add))
                ch(pool.tensor_tensor(st[:, b], t1, t2, ALU.add))
            ch.then(pool.memset(t1, 0.0), "scan_done")

        @block.tensor
        def _(pe):
            def mm(out, lhsT, rhs, start, stop, skip=False):
                return pe.matmul(out, lhsT, rhs, start=start, stop=stop, skip_group_check=skip)

            def sum_squares(src, bank, n):
                for k in range(KD):
                    last = mm(ps[:, bank, 0:n], ones, src[:, k], k == 0, k == KD - 1)
                return last

            pe.wait_ge(sem("sc_ready"), 1)
            pe.wait_ge(sem("cst_in"), 16)
            for i in range(NADC):
                pe.wait_ge(sem(f"ada_in{i % 2}"), 16 * (i // 2 + 1))
                if i >= 2:
                    pe.wait_ge(sem("adrow_ready"), i - 1)
                for k in range(KD):
                    last = mm(ps[0:2, i % 2, :], sc[:, k], adw[:, i % 2, k], k == 0, k == KD - 1)
                last.then_inc(sem("ada_mm"), 1)
                if i >= 1:
                    ada_turn(pe, i - 1)
            ada_turn(pe, NADC - 1)
            pe.wait_ge(sem("ctab_ready"), 1)
            for t in range(NT5):
                g, d = t // 2, t % 2
                bank, off = 3 + (t % 16) // 4, (t % 4) * TW
                if t == 16:
                    pe.wait_ge(sem("kk_half"), 1)
                o = ps[0:2 * C5, bank, off:off + TW]
                j0 = 0 if d == 0 else 1
                mm(o, bdr[:, t], ctr[:, g, d, j0:j0 + T5].rearrange("p j c -> p (j c)"), True, False)
                last = mm(o, bdi[:, t], ctn[:, g, d, j0:j0 + T5].rearrange("p j c -> p (j c)"), False, True)
                if t == 15:
                    last.then_inc(sem("kk_mm"), 1)
            last.then_inc(sem("kk_mm"), 1)
            for q in range(4):
                pe.wait_ge(sem("bt_ready"), q + 1)
                for r in range(2):
                    for hb in range(2):
                        n = 4 * q + 2 * r + hb
                        if n >= 2:
                            pe.wait_ge(sem("bm_evicted"), n - 1)
                        for t in range(4):
                            last = pe.transpose(ps[:, n % 2, t * P:(t + 1) * P], bt[:, q % 2, r, hb * 4 + t], ident)
                        last.then_inc(sem("bt_turned"), 1)
            pe.wait_ge(sem("sq0"), 2)
            pe.wait_ge(sem("ones_ready"), 1)
            sum_squares(hT, 7, 512).then_inc(sem("norm_mm"), 1)
            pe.wait_ge(sem("win_in"), 16)
            pe.wait_ge(sem("h_ready"), 1)
            pe.wait_ge(sem("bm_evicted"), 16)
            for bank, c0, m, tok in ((0, QL, P, 0), (1, QL + KVL - NOPE, QKH, 0)):
                for k in range(KD):
                    last = mm(ps[0:m, bank, :], w_in[:, k, c0:c0 + m], hT[:, k], k == 0, k == KD - 1)
                last.then_inc(sem("proj_mm"), 1)
            for i in range(2):
                for k in range(KD):
                    last = mm(ps[:, 2, i * L:(i + 1) * L], w_in[:, k, i * P:(i + 1) * P], hT[:, k, L:2 * L], k == 0, k == KD - 1)
            last.then_inc(sem("proj_mm"), 1)
            for i in range(4):
                for k in range(KD):
                    last = mm(ps[:, 3 + i, :], w_in[:, k, UOFF + i * P:UOFF + (i + 1) * P], hT[:, k], k == 0, k == KD - 1)
                last.then_inc(sem("proj_mm"), 1)
            pe.wait_ge(sem("sql_ready"), 2)
            pe.wait_ge(sem("kvl_evicted"), 3)
            mm(ps[:, 7, :], ones, sql[:, 0], True, True).then_inc(sem("lat_mm"), 1)
            for i in range(2):
                last = mm(ps[:, 0, 0:L], ones, sql[:, 1, i * L:(i + 1) * L], i == 0, i == 1)
            last.then_inc(sem("lat_mm"), 1)
            pe.wait_ge(sem("ql_normed"), 1)
            pe.wait_ge(sem("u_evicted"), 4)
            pe.wait_ge(sem("wuq_in"), 16)
            pe.wait_ge(sem("wukv_in"), 16)
            for h in range(HEADS):
                for k in range(2):
                    last = mm(ps[0:QKH, 3 + h // 2, (h % 2) * L:(h % 2 + 1) * L], w_uq[:, k, h * QKH:(h + 1) * QKH], ql[:, k], k == 0, k == 1)
                if h % 2:
                    last.then_inc(sem("qh_mm"), 1)
            kbank = (0, 1, 2, 7)
            for h in range(HEADS):
                if h >= 4:
                    pe.wait_ge(sem("kh_evicted"), h - 3)
                mm(ps[0:NOPE, kbank[h % 4], :], w_ukv[:, h * P:h * P + NOPE], kvl, True, True).then_inc(sem("kh_mm"), 1)
            for t in range(4):
                pe.wait_ge(sem("qh_evicted"), t + 1)
                mm(ps[:, 3 + t, :], kvl[:, t * P:(t + 1) * P],
                   w_ukv.rearrange("p (h n) -> p h n", h=HEADS)[:, :, NOPE:P], True, True).then_inc(sem("v_mm"), 1)
            pe.wait_ge(sem("U_in"), 16 * T5)
            pe.wait_ge(sem("kh_evicted"), 8)
            pe.wait_ge(sem("vt_evicted"), 4)
            for b in range(8):
                for t in range(8):
                    tile, r = (b // 2) * 8 + t, b % 2
                    for g2 in range(2):
                        last = mm(ps[g2 * N5:(g2 + 1) * N5, b, t * NCH:(t + 1) * NCH], bm[:, tile, r, g2 * N5:(g2 + 1) * N5],
                                  U[:, 2 * (tile // 2) + g2], True, True)
                last.then_inc(sem("est_mm"), 1)
            pe.wait_ge(sem("sqq_ready"), 1)
            for h in range(HEADS):
                if h % 2 == 0:
                    pe.wait_ge(sem("est_ready"), 8)
                last = mm(ps[0:QKH, h // 2, (h % 2) * L:(h % 2 + 1) * L], ones[0:QKH, 0:QKH], sqq[:, h], True, True)
                if h % 2:
                    last.then_inc(sem("qn_mm"), 1)
            pe.wait_ge(sem("sqk_ready"), 1)
            for h in range(HEADS):
                if h >= 4:
                    pe.wait_ge(sem("krms"), h - 3)
                mm(ps[0:QKH, 4 + h % 4, :], ones[0:QKH, 0:QKH], sqk[:, h], True, True).then_inc(sem("kn_mm"), 1)
            pe.wait_ge(sem("qrms"), 4)
            pe.wait_ge(sem("qh_normed"), 1)
            for b in range(4):
                mm(ps[0:QKH, b, :], cst("swap", QKH), qh[:, 2 * b:2 * b + 2].rearrange("p h t -> p (h t)"), True, True).then_inc(sem("qswap_mm"), 1)
            pe.wait_ge(sem("krms"), 8)
            pe.wait_ge(sem("kh_normed"), 1)
            for b in range(4):
                mm(ps[0:QKH, 4 + b, :], cst("swap", QKH), kh[:, 2 * b:2 * b + 2, L:2 * L], True, True).then_inc(sem("kswap_mm"), 1)
            pe.wait_ge(sem("rope_done"), 2)

            def scores(n):
                h, t = n // 2, n % 2
                if n >= 2:
                    pe.wait_ge(sem("exp_done"), n - 1)
                mm(ps[:, n % 2, :], qh[:, h, t * P:(t + 1) * P], kh[:, h], True, True).then_inc(sem("scores_done"), 1)
            scores(0)
            for n in range(2 * HEADS):
                h, t = n // 2, n % 2
                if n + 1 < 2 * HEADS:
                    scores(n + 1)
                pe.wait_ge(sem("prob_ready"), n + 1)
                if n >= 2:
                    pe.wait_ge(sem("pT_ready"), n - 1)
                for k in range(4):
                    last = pe.transpose(ps[:, 2 + n % 2, k * P:(k + 1) * P], prob[:, n % 2, k * P:(k + 1) * P], ident)
                last.then_inc(sem("pT_mm"), 1)
                if t == 1:
                    pe.wait_ge(sem("pT_ready"), n + 1)
                    if h >= 2:
                        pe.wait_ge(sem("att_ready"), h - 1)
                    o = ps[(h % 2) * VH:(h % 2 + 1) * VH, 4 if h % 2 == 0 else 7, 0:L]
                    for k in range(4):
                        last = mm(o, vt[:, k, h * VH:(h + 1) * VH], pT[:, h % 2, k], k == 0, k == 3)
                    last.then_inc(sem("pv_mm"), 1)
            pe.wait_ge(sem("scan_done"), 1)
            pe.wait_ge(sem("toep_in"), 16 * 2 * T5)
            for g in range(G5):
                o = ps[:, 5 + g % 2, (g // 2) * XCH:(g // 2 + 1) * XCH]
                rows = slice((g % 2) * N5, (g % 2 + 1) * N5)
                mm(o, toep[:, g], U[:, g, XCH:2 * XCH], True, False)
                for d in range(2):
                    sl = st[rows, 2:2 + XCH] if d == 0 else st[rows, 1 + XCH:1:-1]
                    j0 = 1 - d
                    for r, tab in ((0, ctr), (1, ctn)):
                        last = mm(o, tab[rows, g // 2, d, j0:j0 + T5].rearrange("p j c -> p (j c)"),
                                  sl[:, :, r, (g // 2) * 2 + d], False, d == 1 and r == 1)
            last.then_inc(sem("y_mm"), 1)
            pe.wait_ge(sem("z_ready"), 1)
            pe.wait_ge(sem("glu_in"), 16)
            for j in range(4):
                for k in range(4):
                    last = mm(ps[:, 5 + j // 2, (j % 2) * L:(j % 2 + 1) * L], glu_w[:, k, j * P:(j + 1) * P], zT[:, k], k == 0, k == 3)
                last.then_inc(sem("glu_mm"), 1)
            pe.wait_ge(sem("att_ready"), HEADS)
            pe.wait_ge(sem("s5_out"), 4)
            pe.wait_ge(sem("wout_in"), 16)
            for j in range(KD):
                for k in range(KD):
                    rhs = att[:, k] if k < 4 else zT[:, k - 4]
                    last = mm(ps[:, j // 2, (j % 2) * L:(j % 2 + 1) * L], w_out[:, k, j * P:(j + 1) * P], rhs, k == 0, k == KD - 1)
                last.then_inc(sem("mix_mm0"), 1)

            def moe_pe(li):
                pe.wait_ge(sem("moe_sq"), li * 1 + 1)
                sum_squares(sqX, 6, L).then_inc(sem("norm_mm"), 1)
                pe.wait_ge(sem("moe_h"), li * 1 + 1)
                pe.wait_ge(sem("rw_in"), li * 32 + 32)
                for t in range(2):
                    for k in range(KD):
                        last = mm(ps[:, 7, t * NE:(t + 1) * NE], hX[:, k, t * P:(t + 1) * P], rw[:, k], k == 0, k == KD - 1)
                last.then_inc(sem("logits"), 1)

                def gate_up(n, i=None):
                    b = 4 + 2 * (n % 2)
                    for f in range(2):
                        for k in range(KD):
                            mm(ps[:, b, f * L:(f + 1) * L], wg(n % RING, k, f), hX[:, k], k == 0, k == KD - 1)
                    for f in range(2):
                        for k in range(KD):
                            last = mm(ps[:, b + 1, f * L:(f + 1) * L], wu(n % RING, k, f), hX[:, k], k == 0, k == KD - 1)
                    last.then_inc(sem("gu"), 1)

                def down(n, first=False, end=False):
                    for f in range(2):
                        for j in range(KD):
                            last = mm(ps[:, j // 2, (j % 2) * L:(j % 2 + 1) * L], wd(n % RING, f, j), hh[:, n % 2, f * L:(f + 1) * L],
                                      first and f == 0 and j % 2 == 0, end and f == 1, skip=True)
                    last.then_inc(sem("down"), 1)

                pe.wait_ge(sem("w_slot0"), 16 * (17 * li + 1))
                gate_up(0)
                pe.wait_ge(sem("route"), li * 2 + 2)
                for t in range(2):
                    last = pe.transpose(ps[0:NE, 6, t * P:(t + 1) * P], at(rtb + 14 * 64 + t * 64, NE), ident)
                last.then_inc(sem("wT_mm"), 1)
                pe.wait_ge(sem("wT_ready"), li * 1 + 1)
                for n in range(1, 5):
                    pe.wait_ge(sem(f"w_slot{n % RING}"), 16 * li * (NE // RING + (n % RING == 0)) + 16 * (n // RING + 1))
                    if n >= 2:
                        pe.wait_ge(sem("h_done"), li * (NE + 1) + n - 1)
                    gate_up(n)
                    pe.wait_ge(sem("h_done"), li * (NE + 1) + n)
                    down(n - 1, first=(n == 1))
                with pe.Fori(0, (NE - RING) // RING) as i:
                    for q in range(RING):
                        n = 5 + q
                        pe.wait_ge(sem(f"w_slot{n % RING}"), 16 * li * (NE // RING + (n % RING == 0)) + i * 16 + 16 * (n // RING + 1))
                        gate_up(n)
                        pe.wait_ge(sem("h_done"), li * (NE + 1) + i * RING + n)
                        down(n - 1)
                pe.wait_ge(sem("h_done"), li * (NE + 1) + NE + 1)
                down(NE, end=True)

            moe_pe(0)
            pe.wait_ge(sem("hcst_in"), 16)
            pe.wait_ge(sem("fw_in"), 48)
            mm(ps[0:FH, 4, 0:L], f_w1, hcst("zemb", 1, FE), True, True).then_inc(sem("hid_mm"), 1)
            pe.wait_ge(sem("hid_ready"), 1)
            mm(ps[0:FH, 5, 0:L], f_w2, hid[:, 0], True, True).then_inc(sem("hid_mm"), 1)
            pe.wait_ge(sem("hid_ready"), 2)
            for t in range(2):
                for j in range(4):
                    mm(ps[:, (t * 4 + j) % 8, :], hid[:, 1, t * P:(t + 1) * P], f_w3[:, j * 512:(j + 1) * 512], True, True).then_inc(sem("hf_mm"), 1)
            pe.wait_ge(sem("hf_sq"), 1)
            for j in range(8):
                for k in range(4):
                    last = mm(ps[:, 0, j:j + 1], tiles(ff0, 4, HYW)[:, k, j * P:(j + 1) * P], ones[:, 0:1], k == 0, k == 3)
            last.then_inc(sem("hn_mm"), 1)
            pe.wait_ge(sem("hf_comb"), 1)
            for w, (mat, src) in enumerate((("fc", 0), ("fs", 2))):
                for m in range(2):
                    for c in range(2):
                        n = w * 4 + m * 2 + c
                        if n == 0:
                            pe.wait_ge(sem("hn_read"), 1)
                        for k in range(2):
                            last = mm(ps[:, n, :], hcst(mat)[:, k, m * P:(m + 1) * P], hf[:, src + k, c * 512:(c + 1) * 512], k == 0, k == 1)
                        last.then_inc(sem("H_mm"), 1)
            pe.wait_ge(sem("hy_sq"), 1)
            pe.wait_ge(sem("H_evicted"), 8)
            sum_squares(sqX, 6, L).then_inc(sem("norm_mm"), 1)
            pe.wait_ge(sem("hy_h"), 1)
            for i in range(6):
                pe.wait_ge(sem(f"hyw_in{i % 3}"), 16 * (i // 3 + 1))
                if i >= 2:
                    pe.wait_ge(sem("hyp_evicted"), i - 1)
                for j in range(4):
                    for k in range(KD):
                        last = mm(ps[:, 2 * (i % 2) + j // 2, (j % 2) * L:(j % 2 + 1) * L], hyw[:, i % 3, k, j * P:(j + 1) * P], hX[:, k], k == 0, k == KD - 1)
                last.then_inc(sem("hy_proj"), 1)
            pe.wait_ge(sem("z_conv"), 1)
            for t in range(2):
                for hb in range(2):
                    for j in range(4):
                        last = pe.transpose(ps[:, 4 + 2 * t + hb, j * P:(j + 1) * P], zt[:, hb * 4 + j, t * P:(t + 1) * P], ident)
                    last.then_inc(sem("zs_mm"), 1)
            pe.wait_ge(sem("zs_ready"), 4)
            for w, mat in enumerate(("fc", "fs")):
                for m in range(2):
                    for c in range(2):
                        n = w * 4 + m * 2 + c
                        for k in range(2):
                            last = mm(ps[:, n, :], hcst(mat)[:, k, m * P:(m + 1) * P], zs[:, k, c * 512:(c + 1) * 512], k == 0, k == 1)
                        last.then_inc(sem("Z_mm"), 1)
            pe.wait_ge(sem("Y_ready"), 1)
            for j in range(KD):
                for w, (mat, src) in enumerate((("ic", YR), ("is", YS))):
                    for k in range(2):
                        last = mm(ps[:, j // 2, (j % 2) * L:(j % 2 + 1) * L], src[:, k, j * P:(j + 1) * P], hcst(mat)[:, k], w == 0 and k == 0, w == 1 and k == 1)
                last.then_inc(sem("conv_mm"), 1)
            pe.wait_ge(sem("yh_ready"), 8)
            pe.wait_ge(sem("hyo_in"), 16)
            for j in range(KD):
                for k in range(KD):
                    last = mm(ps[:, 4 + j // 2, (j % 2) * L:(j % 2 + 1) * L], hyo[:, k, j * P:(j + 1) * P], zt[:, k], k == 0, k == KD - 1)
                last.then_inc(sem("mix_mm1"), 1)
            moe_pe(1)

        @block.scalar
        def _(act):
            ch = Chain(act, sem("act_chain"), sem)

            def f(out, in_, func, **kw):
                return act.activation(out, in_, func, **kw)

            act.wait_ge(sem("cols_in"), 16)
            ch.then(f(sc, col("c", 0, 16).rearrange("p (k m) -> p k m", m=2), ACT.Silu), "sc_ready")
            act.wait_ge(sem("s5p_in"), 16)
            ch.then(f(sm(0), s5("lst"), ACT.Exp), "s5_step")
            act.wait_ge(sem("s5_arg"), 1)
            ch(f(sm(4), sm(1), ACT.Exp))
            ch(f(sm(5), sm(2), ACT.Sin))
            ch.then(f(sm(6), sm(3), ACT.Sin), "s5_trig")
            for i in range(NADC):
                act.wait_ge(sem("ada_mm"), i + 1)
                if i >= 2:
                    act.wait_ge(sem("ada_turned"), i - 1)
                ch.then(f(adrow[:, i % 2], ps[0:2, i % 2, :], ACT.Copy), "adrow_ready")
                if i >= 1:
                    act.wait_ge(sem("ada_turned"), i)
                    ch.then(f(modc[:, 4 * (i - 1):4 * i].rearrange("p c m -> p (c m)"), ps[:, 2, 0:8], ACT.Copy), "modc_ready")
            act.wait_ge(sem("ada_turned"), NADC)
            ch.then(f(modc[:, 4 * (NADC - 1):4 * NADC].rearrange("p c m -> p (c m)"), ps[:, 2, 0:8], ACT.Copy), "modc_ready")
            for n in range(16):
                act.wait_ge(sem("bt_turned"), n + 1)
                q, r, hb = n // 4, n // 2 % 2, n % 2
                if n == 0:
                    act.wait_ge(sem("kk_ready"), 1)
                ch.then(f(bm[:, 8 * q + 4 * hb:8 * q + 4 * hb + 4, r], ps[:, n % 2, :].rearrange("p (t m) -> p t m", t=4), ACT.Copy), "bm_evicted")
            act.wait_ge(sem("x_in"), 16)
            act.wait_ge(sem("kscr_out"), 16)
            act.wait_ge(sem("ctx_in"), 16)
            ch.then(f(hT[:, :, 0:L], cx, ACT.Square), "sq0")
            ch.then(f(hT[:, :, L:2 * L], xT, ACT.Square), "sq0")

            def rms(bank, n, count, name, rows=P, width=D, out=None):
                act.wait_ge(sem(name), count)
                return f(out if out is not None else stx[:, 0:n], ps[0:rows, bank, 0:n], ACT.Sqrt, scale=1.0 / width, bias=at(r_eps, 1, rows))

            act.wait_ge(sem("eps_ready"), 1)
            ch.then(rms(7, 512, 1, "norm_mm"), "rms_ready")
            for i in range(4):
                act.wait_ge(sem("proj_mm"), 4 + i)
                ch.then(f(u_sb[:, i], ps[:, 3 + i, :].rearrange("p (c t) -> p t c", t=T5), ACT.Copy), "u_evicted")
            act.wait_ge(sem("kvl_evicted"), 3)
            ch.then(f(sql[:, 0], kvl, ACT.Square), "sql_ready")
            ch.then(f(sql[:, 1], ql.rearrange("p k t -> p (k t)"), ACT.Square), "sql_ready")
            act.wait_ge(sem("h_ready"), 1)
            ch.then(rms(7, 512, 1, "lat_mm", width=KVL), "lrms_ready")
            act.wait_ge(sem("kvl_normed"), 1)
            ch.then(rms(0, L, 2, "lat_mm", width=QL), "lrms_ready")
            for b in range(4):
                act.wait_ge(sem("qh_mm"), b + 1)
                if b == 0:
                    act.wait_ge(sem("kvl_evicted"), 3)
                ch.then(f(qh[:, 2 * b:2 * b + 2].rearrange("p h t -> p (h t)"), ps[0:QKH, 3 + b, :], ACT.Copy), "qh_evicted")
            for t in range(4):
                act.wait_ge(sem("v_mm"), t + 1)
                ch.then(f(vt[:, t], ps[:, 3 + t, :], ACT.Copy), "vt_evicted")
            for b in range(8):
                act.wait_ge(sem("est_mm"), b + 1)
                r, g0 = b % 2, (b // 2) * 8
                src = ps[:, b, :].rearrange("p (g d c) -> p g d c", d=2, c=NCH)
                dst = est[:, :, r, g0:g0 + 8].rearrange("p s (g d) -> p g d s", d=2)
                ch(f(dst[:, :, 0], src[:, :, 0], ACT.Copy))
                ch(f(dst[:, :, 1, 0:XCH], src[:, :, 1, XCH - 1::-1], ACT.Copy))
                ch.then(f(dst[:, :, 1, XCH:NCH], src[:, :, 1, NCH - 1:XCH - 1:-1], ACT.Copy), "est_ready")
            act.wait_ge(sem("est_mm"), 8)
            ch.then(f(sqq, qh, ACT.Square), "sqq_ready")
            act.wait_ge(sem("kh_evicted"), 8)
            act.wait_ge(sem("kr_copied"), 1)
            ch.then(f(sqk, kh, ACT.Square), "sqk_ready")
            for b in range(4):
                act.wait_ge(sem("qn_mm"), b + 1)
                ch.then(f(sqq[:, 2 * b:2 * b + 2].rearrange("p h t -> p (h t)"), ps[0:QKH, b, :], ACT.Sqrt, scale=1.0 / QKH, bias=at(r_eps, 1, QKH)), "qrms")
            for h in range(HEADS):
                act.wait_ge(sem("kn_mm"), h + 1)
                ch.then(f(sqk[:, h], ps[0:QKH, 4 + h % 4, :], ACT.Sqrt, scale=1.0 / QKH, bias=at(r_eps, 1, QKH)), "krms")
            for n in range(2 * HEADS):
                act.wait_ge(sem("max_done"), n + 1)
                if n >= 2:
                    act.wait_ge(sem("pT_mm"), n - 1)
                ch.then(f(prob[:, n % 2], ps[:, n % 2, :], ACT.Exp, scale=QKH ** -0.5, bias=at(r_st + n, 1), accum_out=at(r_st + 16 + n, 1)), "exp_done")
                if n >= 1:
                    turned(act, f, ch, n - 1)
            turned(act, f, ch, 2 * HEADS - 1)
            act.wait_ge(sem("pv_mm"), HEADS)
            act.wait_ge(sem("yT_in"), 16 * 32)
            ch.then(f(zT.rearrange("p i (c t) -> p i t c", t=T5), yT, ACT.Gelu_apprx_tanh), "z_ready")
            for j in range(4):
                act.wait_ge(sem("glu_mm"), j // 2 * 2 + 2)
                ch.then(f(yT.rearrange("p i t c -> p i (t c)")[:, j], ps[:, 5 + j // 2, (j % 2) * L:(j % 2 + 1) * L], ACT.Sigmoid, bias=col("glub", j)), "glu_sig")

            def moe_act(li):
                act.wait_ge(sem("x_mixed"), li * 1 + 1)
                ch.then(f(sqX, xT, ACT.Square), "moe_sq")
                n = 2 if li == 0 else 4
                ch.then(rms(6, L, n, "norm_mm"), "rms_ready")
                act.wait_ge(sem("logits"), li * 1 + 1)
                ch.then(f(at(rtb + 2 * 64, 2 * NE), ps[:, 7, 0:2 * NE], ACT.Exp, scale=-1.0), "rexp")

                def silu(n):
                    return f(sg[:, n % 2], ps[:, 4 + 2 * (n % 2), :], ACT.Silu)
                for n in range(5):
                    act.wait_ge(sem("gu"), li * (NE + 1) + n + 1)
                    if n >= 2:
                        act.wait_ge(sem("h_done"), li * (NE + 1) + n - 1)
                    silu(n).then_inc(sem("sg"), 1)
                with act.Fori(0, (NE - RING) // RING) as i:
                    for q in range(RING):
                        n = 5 + q
                        act.wait_ge(sem("gu"), li * (NE + 1) + i * RING + n + 1)
                        act.wait_ge(sem("h_done"), li * (NE + 1) + i * RING + n - 1)
                        silu(n).then_inc(sem("sg"), 1)

            moe_act(0)
            for i in range(2):
                act.wait_ge(sem("hid_arg"), i + 1)
                ch.then(f(hid[:, i], at(hsc, L, FH), ACT.Sin), "hid_ready")
            act.wait_ge(sem("hf_ready"), 8)
            ch.then(f(tiles(ff0, 4, HYW), hf, ACT.Square), "hf_sq")
            act.wait_ge(sem("hn_mm"), 1)
            ch.then(f(hns, ps[:, 0, 0:8], ACT.Sqrt, bias=at(r_eps, 1)), "hn_read")
            for n in range(8):
                act.wait_ge(sem("H_mm"), n + 1)
                dst = (HR if n < 4 else HS)[:, n // 2 % 2, (n % 2) * 512:(n % 2 + 1) * 512]
                ch.then(f(dst, ps[:, n, :], ACT.Copy), "H_evicted")
            ch.then(f(sqX, xT, ACT.Square), "hy_sq")
            ch.then(rms(6, L, 3, "norm_mm"), "rms_ready")
            for i in range(6):
                act.wait_ge(sem("hy_proj"), i + 1)
                if i >= 2:
                    act.wait_ge(sem("conv_done"), i - 1)
                for hb in range(2):
                    ins = f(pp[:, i % 2, 2 * hb:2 * hb + 2].rearrange("p i t -> p (i t)"), ps[:, 2 * (i % 2) + hb, :], ACT.Copy)
                    if hb == 0:
                        ch(ins)
                    else:
                        ch.then(ins, "hyp_evicted")
            for n in range(4):
                act.wait_ge(sem("zs_mm"), n + 1)
                ch.then(f(zs[:, n // 2, (n % 2) * 512:(n % 2 + 1) * 512], ps[:, 4 + n, :], ACT.Copy), "zs_ready")
            moe_act(1)

        @block.vector
        def _(dve):
            ch = Chain(dve, sem("dve_chain"), sem)
            tt, ts, stt = dve.tensor_tensor, dve.tensor_scalar, dve.scalar_tensor_tensor
            M, AD, SU = ALU.mult, ALU.add, ALU.subtract
            ch.then(dve.memset(at(r_eps, 1), EPS), "eps_ready")
            ch(dve.memset(bdr.rearrange("p t m -> p (t m)"), 0.0))
            ch(dve.memset(bdi.rearrange("p t m -> p (t m)"), 0.0))
            dve.wait_ge(sem("s5_step"), 1)

            def cmul(o, a, b, t):
                ch(tt(t, a[1], b[1], M))
                ch(tt(o[0], a[0], b[0], M))
                ch(tt(o[0], o[0], t, SU))
                ch(tt(t, a[1], b[0], M))
                ch(tt(o[1], a[0], b[1], M))
                ch(tt(o[1], o[1], t, AD))

            def reduced(out, x, t, quarter):
                ch(ts(t, x, 1.0 / TWO_PI, 0.25 * quarter, M, AD))
                ch(ts(t, t, ROUND, None, AD))
                ch(ts(t, t, ROUND, None, SU))
                ch(stt(out, t, -PI_HI, x, M, AD))
                ch(stt(out, t, -PI_LO, out, M, AD))
                if quarter:
                    ch(ts(out, out, quarter * math.pi / 2, None, AD))
                ch(ts(out, out, PI_SAFE, -PI_SAFE, ALU.min, ALU.max))

            ch(ts(sm(7), s5("lre"), -1e-4, None, ALU.min))
            ch(tt(sm(1), sm(7), sm(0), M))
            ch(tt(sm(8), s5("lim"), sm(0), M))
            reduced(sm(2), sm(8), sm(9), 0)
            ch(ts(sm(10), sm(8), 0.0, None, AD))
            reduced(sm(3), sm(10), sm(9), 1)
            ch.then(ts(sm(9), sm(9), 0.0, None, M), "s5_arg")
            dve.wait_ge(sem("s5_trig"), 1)
            ch(dve.memset(pw[:, 0, 0], 1.0))
            ch(dve.memset(pw[:, 1, 0], 0.0))
            ch(tt(pw[:, 0, 1], sm(4), sm(6), M))
            ch(tt(pw[:, 1, 1], sm(4), sm(5), M))

            def p_(a, b):
                return pw[:, 0, a:b], pw[:, 1, a:b]

            def pb(a, n):
                return tuple(pw[:, r, a:a + 1].broadcast_to([P, n, NT5]) for r in range(2))
            tq = at(r10 + NT5 * 11, 4 * NT5).rearrange("p (j t) -> p j t", j=4)
            cmul(p_(2, 3), p_(1, 2), p_(1, 2), tq[:, 0:1])
            cmul(p_(3, 5), p_(1, 3), pb(2, 2), tq[:, 0:2])
            cmul(p_(5, 9), p_(1, 5), pb(4, 4), tq)
            A8, B8 = tiles(tmp5, 2, NT5), tiles(tmp5 + 64, 2, NT5)
            ch(dve.tensor_copy(A8[:, 0], pw[:, 0, 8]))
            ch(dve.tensor_copy(A8[:, 1], pw[:, 0, 8]))
            ch(ts(B8[:, 0], pw[:, 1, 8], -1.0, None, M))
            ch.then(dve.tensor_copy(B8[:, 1], pw[:, 1, 8]), "lam8_ready")
            ch(tt(sm(15), sm(7), sm(7), M))
            ch(tt(sm(16), s5("lim"), s5("lim"), M))
            ch(tt(sm(15), sm(15), sm(16), AD))
            ch(dve.reciprocal(sm(16), sm(15)))
            ch(ts(sm(17), pw[:, 0, 1], -1.0, None, AD))
            ch(tt(sm(18), sm(7), sm(16), M))
            ch(tt(sm(19), s5("lim"), sm(16), M))
            ch(ts(sm(19), sm(19), -1.0, None, M))
            cmul((sm(20), sm(21)), (sm(17), pw[:, 1, 1]), (sm(18), sm(19)), sm(22))

            def over(v):
                return v.rearrange("p (t c) -> p t c", c=1).broadcast_to([P, NT5, C5])
            tb = big[:, 0:512].rearrange("p (t c) -> p t c", c=C5)
            cmul((fb[:, 0], fb[:, 1]), (s5("br"), s5("bi")), (over(sm(20)), over(sm(21))), tb)
            for g2 in range(2):
                rows = slice(g2 * N5, (g2 + 1) * N5)
                ch(dve.tensor_copy(bdr[rows, :, g2 * C5:(g2 + 1) * C5], fb[rows, 0]))
                ch(dve.tensor_copy(bdi[rows, :, g2 * C5:(g2 + 1) * C5], fb[rows, 1]))
            cr_, ci_ = (s5(n).rearrange("p (g d) c -> p g d c", d=2) for n in ("cr", "ci"))
            for d in range(2):
                def lam(r):
                    v = pw[:, r, :].rearrange("p j (g d) -> p g d j", d=2)[:, :, d]
                    v = v if d == 0 else v[:, :, ::-1]
                    return v

                for g0 in range(0, GP, 8):
                    gs = slice(g0, g0 + 8)

                    def C(v):
                        return v[:, gs, d].unsqueeze(2).broadcast_to([P, 8, 9, C5])

                    def W(r):
                        return lam(r)[:, gs].unsqueeze(3).broadcast_to([P, 8, 9, C5])
                    t = big[:, 0:8 * 144].rearrange("p (g j c) -> p g j c", g=8, j=9)
                    o, q = ctr[:, gs, d], ctn[:, gs, d]
                    ch(tt(t, C(ci_), W(1), M))
                    ch(tt(o, C(cr_), W(0), M))
                    ch(tt(o, o, t, SU))
                    ch(tt(t, C(cr_), W(1), M))
                    ch(tt(q, C(ci_), W(0), M))
                    ch(stt(q.rearrange("p g j c -> p g (j c)"), q.rearrange("p g j c -> p g (j c)"), -1.0,
                           t.rearrange("p g j c -> p g (j c)"), M, SU))
            ch.then(ts(sm(23), sm(22), 0.0, None, M), "ctab_ready")
            ch.then(ts(sm(23), sm(22), 0.0, None, M), "s5_params_used")
            for half in range(2):
                dve.wait_ge(sem("kk_mm"), half + 1)
                for b in range(4):
                    src = ps[0:2 * C5, 3 + b, :].rearrange("p (g d j c) -> p g d j c", d=2, j=T5, c=C5)
                    gs = slice(8 * half + 2 * b, 8 * half + 2 * b + 2)
                    ch(dve.tensor_copy(kk[:, gs, 0:7], src[:, :, 1, 0:7]))
                    ch(dve.tensor_copy(kk[:, gs, 7], src[:, :, 1, 7]))
                    ch(tt(kk[:, gs, 7], kk[:, gs, 7], src[:, :, 0, 0], AD))
                    ins = dve.tensor_copy(kk[:, gs, 8:15], src[:, :, 0, 1:8])
                    if half == 0 and b == 3:
                        ch.then(ins, "kk_half")
                    else:
                        ch(ins)
            ch.then(dve.memset(sm(23), 0.0), "bd_used")
            td = big[0:32, 0:GP * C5].rearrange("p (g c) -> p g c", c=C5)
            ch(tt(td, col("s5d", 0, GP, 32).unsqueeze(2).broadcast_to([32, GP, C5]),
                  cst("eye16", 32).unsqueeze(1).broadcast_to([32, GP, C5]), M))
            ch.then(tt(kk[:, :, 7], kk[:, :, 7], td, AD), "kk_ready")
            for q in range(4):
                if q >= 2:
                    dve.wait_ge(sem("bt_turned"), 4 * (q - 1))
                for d in range(2):
                    gs = slice(4 * q, 4 * q + 4)

                    def B(r):
                        return fb[:, r].rearrange("p (g d) c -> p g d c", d=2)[:, gs, d].unsqueeze(2).broadcast_to([P, 4, T5, C5])

                    def W(r):
                        v = pw[:, r, 0:8].rearrange("p j (g d) -> p g d j", d=2)[:, gs, d]
                        v = v[:, :, ::-1] if d == 0 else v
                        return v.unsqueeze(3).broadcast_to([P, 4, T5, C5])
                    o = [bt[:, q % 2, r].rearrange("p (g d) (j c) -> p g d j c", d=2, c=C5)[:, :, d] for r in range(2)]
                    t = at(r11, 4 * TW).rearrange("p (g j c) -> p g j c", g=4, c=C5)
                    ch(tt(t, B(1), W(1), M))
                    ch(tt(o[0], B(0), W(0), M))
                    ch(tt(o[0], o[0], t, SU))
                    ch(tt(t, B(1), W(0), M))
                    ch(tt(o[1], B(0), W(1), M))
                    ins = tt(o[1], o[1], t, AD)
                    if d == 1:
                        if q == 0:
                            ch(ins)
                            ins = ts(sm(23), sm(22), 0.0, None, M)
                        ch.then(ins, "bt_ready")
                    else:
                        ch(ins)
            dve.wait_ge(sem("modc_ready"), NADC)
            ch(tt(modc, modc, col("ada_b", 0, 192).rearrange("p (c m) -> p c m", m=2), AD))
            for j in (1, 4):
                ch(ts(mod[:, :, j], mod[:, :, j], 1.0, None, AD))

            rms_n = [0]

            def inv_rms(n):
                rms_n[0] += 1
                dve.wait_ge(sem("rms_ready"), rms_n[0])
                ch(dve.reciprocal(rsx[:, 0:n], stx[:, 0:n]))

            def scaled(dst, src, r, li, m, jsh):
                ch(tt(dst, src, r.unsqueeze(1).broadcast_to([P, KD, L]), M))
                for k in range(KD):
                    ch(ts(dst[:, k], dst[:, k], scol(li, jsh + 1, k, m), scol(li, jsh, k, m), M, AD))
            inv_rms(512)
            scaled(hT[:, :, 0:L], cx, rsx[:, 0:L], 0, 1, 0)
            scaled(hT[:, :, L:2 * L], xT, rsx[:, L:2 * L], 0, 0, 0)
            ch.then(ts(sm(23), sm(22), 0.0, None, M), "h_ready")
            dve.wait_ge(sem("proj_mm"), 7)
            ch.then(dve.tensor_copy(kvl, ps[:, 0, :]), "kvl_evicted")
            ch.then(dve.tensor_copy(krl, ps[0:QKH, 1, :]), "kvl_evicted")
            ch.then(dve.tensor_copy(ql.rearrange("p k t -> p (k t)"), ps[:, 2, :]), "kvl_evicted")
            dve.wait_ge(sem("lrms_ready"), 1)
            ch(dve.reciprocal(rsx, stx))
            ch.then(stt(kvl, kvl, col("kvn"), rsx, M, M), "kvl_normed")
            dve.wait_ge(sem("lrms_ready"), 2)
            ch(dve.reciprocal(rsx[:, 0:L], stx[:, 0:L]))
            ch(stt(ql[:, 0], ql[:, 0], col("qn", 0), rsx[:, 0:L], M, M))
            ch.then(stt(ql[:, 1], ql[:, 1], col("qn", 1), rsx[:, 0:L], M, M), "ql_normed")
            kbank = (0, 1, 2, 7)
            for h in range(HEADS):
                dve.wait_ge(sem("kh_mm"), h + 1)
                ch.then(dve.tensor_copy(kh[0:NOPE, h], ps[0:NOPE, kbank[h % 4], :]), "kh_evicted")
            ch.then(dve.tensor_copy(kh[NOPE:QKH], krl[NOPE:QKH].unsqueeze(1).broadcast_to([ROPE, HEADS, 2 * L])), "kr_copied")
            dve.wait_ge(sem("qrms"), 4)
            ch(dve.reciprocal(sqq, sqq))
            ch.then(stt(qh.rearrange("p h t -> p (h t)"), qh.rearrange("p h t -> p (h t)"), col("qqk", rows=QKH), sqq.rearrange("p h t -> p (h t)"), M, M), "qh_normed")
            dve.wait_ge(sem("krms"), 8)
            ch(dve.reciprocal(sqk, sqk))
            ch.then(stt(kh.rearrange("p h t -> p (h t)"), kh.rearrange("p h t -> p (h t)"), col("kqk", rows=QKH), sqk.rearrange("p h t -> p (h t)"), M, M), "kh_normed")
            for name, b0, v in (("qswap_mm", 0, qh), ("kswap_mm", 4, kh[:, :, L:2 * L])):
                dve.wait_ge(sem(name), 4)
                tmp = sqk[:, 0:4].rearrange("p h t -> p (h t)").rearrange("p (h t) -> p h t", t=L)
                ch(tt(tmp, ps[0:QKH, b0:b0 + 4, :].rearrange("p b (h t) -> p (b h) t", h=2),
                      cst("sin", QKH).unsqueeze(1).broadcast_to([QKH, HEADS, L]), M))
                ch(tt(v, v, cst("cos", QKH).unsqueeze(1).broadcast_to([QKH, HEADS, L]), M))
                ch.then(tt(v, v, tmp, AD), "rope_done")
            for n in range(2 * HEADS + 1):
                if n < 2 * HEADS:
                    dve.wait_ge(sem("scores_done"), n + 1)
                    ch(dve.tensor_reduce(at(r_st + 32, 1), ps[:, n % 2, :], AX.X, ALU.max))
                    ch.then(ts(at(r_st + n, 1), at(r_st + 32, 1), -QKH ** -0.5, None, M), "max_done")
                if n >= 1:
                    k = n - 1
                    dve.wait_ge(sem("exp_done"), k + 1)
                    ch(dve.reciprocal(at(r_st + 33, 1), at(r_st + 16 + k, 1)))
                    ch.then(ts(prob[:, k % 2], prob[:, k % 2], at(r_st + 33, 1), None, M), "prob_ready")
                if n >= 3 and n % 2 == 1:
                    attend_out(dve, ch, (n - 3) // 2)
            attend_out(dve, ch, HEADS - 1)
            dve.wait_ge(sem("y_mm"), 1)
            for b in range(2):
                ch.then(dve.tensor_copy(ysb.rearrange("p (g b) c -> p g b c", b=2)[:, :, b], ps[:, 5 + b, :].rearrange("p (g c) -> p g c", c=XCH)), "y_evicted")
            for j in range(4):
                dve.wait_ge(sem("glu_sig"), j + 1)
                if j == 0:
                    dve.wait_ge(sem("glu_mm"), 4)
                ch.then(tt(zT[:, j], zT[:, j], yT.rearrange("p i t c -> p i (t c)")[:, j], M), "s5_out")
            for j in range(KD):
                dve.wait_ge(sem("mix_mm0"), j // 2 * 2 + 2)
                ins = stt(xT[:, j], ps[:, j // 2, (j % 2) * L:(j % 2 + 1) * L], scol(0, 2, j), xT[:, j], M, AD)
                ch(ins) if j < KD - 1 else ch.then(ins, "x_mixed")

            def moe_dve(li):
                inv_rms(L)
                scaled(hX, xT, rsx[:, 0:L], li, 0, 3)
                ch.then(ts(at(rtb + 23 * 64, 1), at(r_eps, 1), 0.0, None, M), "moe_h")
                dve.wait_ge(sem("rexp"), li * 1 + 1)
                dve.wait_ge(sem("rw_in"), li * 32 + 32)

                def S(i, n=1):
                    return at(rtb + 64 * i, 64 * n)
                ch(ts(S(2, 2), S(2, 2), 1.0, None, AD))
                ch(dve.reciprocal(S(2, 2), S(2, 2)))
                for t in range(2):
                    s_, b_, top, gt, eq, cum = S(2 + t), S(4), at(rtb + 64 * 5, 8), S(6), S(7), S(8)
                    need = at(rtb + 64 * 9, 1)
                    ch(tt(b_, s_, S(0), AD))
                    ch(dve.max(top, b_))
                    ch(ts(gt, b_, top[:, TOPK - 1:TOPK], None, ALU.is_gt))
                    ch(ts(eq, b_, top[:, TOPK - 1:TOPK], None, ALU.is_equal))
                    ch(dve.tensor_reduce(need, gt, AX.X, AD))
                    ch(ts(need, need, -1.0, float(TOPK), M, AD))
                    ch(dve.tensor_tensor_scan(cum, eq, eq, 0.0, AD, ALU.bypass))
                    ch(ts(cum, cum, need, None, ALU.is_le))
                    ch(tt(eq, eq, cum, M))
                    ch(tt(gt, gt, eq, AD))
                    ch(tt(gt, gt, s_, M))
                    ch(dve.tensor_reduce(need, gt, AX.X, AD))
                    ch(dve.reciprocal(need, need))
                    ch.then(ts(S(14 + t), gt, need, ROUTE_SCALE, M, M), "route")
                dve.wait_ge(sem("wT_mm"), li * 1 + 1)
                ch.then(dve.tensor_copy(at(rtb + 16 * 64, L, NE), ps[0:NE, 6, 0:L]), "wT_ready")
                def product(n):
                    return tt(hh[:, n % 2], sg[:, n % 2], ps[:, 5 + 2 * (n % 2), :], M)

                def weighted(n):
                    v = hh[:, n % 2].rearrange("p (f t) -> p f t", f=2)
                    return tt(v, v, wbc[:, n % 2].unsqueeze(1).broadcast_to([P, 2, L]), M)
                dve.wait_ge(sem("sg"), li * (NE + 1) + 1)
                product(0).then_inc(sem("h_done"), 1)
                for n in range(1, 5):
                    dve.wait_ge(sem("sg"), li * (NE + 1) + n + 1)
                    if n >= 2:
                        dve.wait_ge(sem("down"), li * (NE + 1) + n - 1)
                    product(n).then_inc(sem("prod"), 1)
                    dve.wait_ge(sem("prod"), li * NE + n)
                    dve.wait_ge(sem(f"wbc_in{n % 2}"), 16 * li * (NE // 2) + 16 * ((n + 1) // 2))
                    weighted(n).then_inc(sem("h_done"), 1)
                with dve.Fori(0, (NE - RING) // RING) as i:
                    for q in range(RING):
                        n = 5 + q
                        dve.wait_ge(sem("sg"), li * (NE + 1) + i * RING + n + 1)
                        dve.wait_ge(sem("down"), li * (NE + 1) + i * RING + n - 1)
                        product(n).then_inc(sem("prod"), 1)
                        dve.wait_ge(sem("prod"), li * NE + i * RING + n)
                        dve.wait_ge(sem(f"wbc_in{n % 2}"), 16 * li * (NE // 2) + i * (16 * RING // 2) + 16 * ((n + 1) // 2))
                        weighted(n).then_inc(sem("h_done"), 1)
                dve.wait_ge(sem("down"), li * (NE + 1) + NE + 1)
                for j in range(KD):
                    ins = stt(xT[:, j], ps[:, j // 2, (j % 2) * L:(j % 2 + 1) * L], scol(li, 5, j), xT[:, j], M, AD)
                    ch(ins) if j < KD - 1 else ch.then(ins, "moe_x")

            moe_dve(0)
            for i in range(2):
                dve.wait_ge(sem("hid_mm"), i + 1)
                if i == 1:
                    dve.wait_ge(sem("hid_ready"), 1)
                a, t = at(hsc + L, L, FH), at(hsc + 2 * L, L, FH)
                ch(ts(a, ps[0:FH, 4 + i, 0:L], col("fb1" if i == 0 else "fb2", rows=FH), col("freq", rows=FH), AD, M))
                reduced(at(hsc, L, FH), a, t, 0)
                ch.then(ts(t, t, 0.0, None, M), "hid_arg")
            for n in range(8):
                t, j = n // 4, n % 4
                dve.wait_ge(sem("hf_mm"), n + 1)
                ch.then(tt(hf[:, 2 * (j // 2) + t, (j % 2) * 512:(j % 2 + 1) * 512], ps[:, n, :],
                             hcst("decay")[:, t, (j % 2) * 512:(j % 2 + 1) * 512], M), "hf_ready")
            dve.wait_ge(sem("hf_sq"), 1)
            dve.wait_ge(sem("hn_mm"), 1)
            hd = tiles(ff0, 2, HYW)
            ch(tt(hd, hf[:, 0:2], hf[:, 2:4], SU))
            ch(tt(hf[:, 0:2], hf[:, 0:2], hf[:, 2:4], AD))
            ch.then(dve.tensor_copy(hf[:, 2:4], hd), "hf_comb")
            dve.wait_ge(sem("hn_read"), 1)
            ch(dve.reciprocal(hns, hns))
            inv_rms(L)
            scaled(hX, xT, rsx[:, 0:L], 1, 0, 0)
            ch.then(ts(at(hsc, 1), at(r_eps, 1), 0.0, None, M), "hy_h")
            for i in range(6):
                dve.wait_ge(sem("hyp_evicted"), i + 1)
                for j in range(4):
                    c = 4 * i + j
                    p_in, o = pp[:, i % 2, j], xc[:, c]
                    ch(ts(o, p_in, col("convw", 24 + c), col("convb", c), M, AD))
                    ch(stt(o[:, 1:L], p_in[:, 0:L - 1], col("convw", c), o[:, 1:L], M, AD))
                    ins = stt(o[:, 0:L - 1], p_in[:, 1:L], col("convw", 48 + c), o[:, 0:L - 1], M, AD)
                    ch(ins) if j < 3 else ch.then(ins, "conv_done")
            ch.then(tt(zt, xc[:, 8:16], xc[:, 16:24], M), "z_conv")
            dve.wait_ge(sem("Z_mm"), 8)
            ZR = ps[:, 0:4, :].rearrange("p (m c) n -> p m (c n)", m=2)
            ZS = ps[:, 4:8, :].rearrange("p (m c) n -> p m (c n)", m=2)
            ch(tt(YR, ZR, HR, M))
            ch(tt(ytmp, ZS, HS, M))
            ch(tt(YR, YR, ytmp, SU))
            ch(tt(YS, ZR, HS, M))
            ch(tt(ytmp, ZS, HR, M))
            ch.then(tt(YS, YS, ytmp, AD), "Y_ready")
            for j in range(KD):
                dve.wait_ge(sem("conv_mm"), j // 2 * 2 + 2)
                ch(ts(zt[:, j], zt[:, j], col("hybias", j), None, M))
                ch(stt(zt[:, j], ps[:, j // 2, (j % 2) * L:(j % 2 + 1) * L], hns[:, j:j + 1], zt[:, j], M, AD))
                ch.then(tt(zt[:, j], zt[:, j], xc[:, j], M), "yh_ready")
            for j in range(KD):
                dve.wait_ge(sem("mix_mm1"), j // 2 * 2 + 2)
                ins = stt(xT[:, j], ps[:, 4 + j // 2, (j % 2) * L:(j % 2 + 1) * L], scol(1, 2, j), xT[:, j], M, AD)
                ch(ins) if j < KD - 1 else ch.then(ins, "x_mixed")
            moe_dve(1)


def tiles_of(w):
    k, n = w.shape
    return np.ascontiguousarray(w.reshape(k // P, P, n).transpose(1, 0, 2))


def columns(v):
    return v.reshape(-1, P).T


def constants():
    c = np.zeros((P, NCST), np.float32)

    def put(name, v):
        a, w = CST[name]
        c[:v.shape[0], a:a + w] = v
    put("ident", np.eye(P, dtype=np.float32))
    t = np.arange(L)
    nf = ROPE // 4
    inv = (10000.0 ** (-np.arange(nf, dtype=np.float32) / nf)).astype(np.float32)
    ang = np.concatenate([(t // 64).astype(np.float32)[:, None] * inv, (t % 64).astype(np.float32)[:, None] * inv], -1).T
    cos, sin = np.ones((QKH, L), np.float32), np.zeros((QKH, L), np.float32)
    cos[NOPE:] = np.repeat(np.cos(ang), 2, 0)
    sin[NOPE:] = np.repeat(np.sin(ang), 2, 0)
    swap = np.zeros((QKH, QKH), np.float32)
    for i in range(NOPE, QKH, 2):
        swap[i + 1, i] = -1.0
        swap[i, i + 1] = 1.0
    put("cos", cos)
    put("sin", sin)
    put("swap", swap)
    put("eye16", np.tile(np.eye(C5, dtype=np.float32), (2, 1)))
    return c


def hyena_constants():
    c = np.zeros((P, NHCST), np.float32)

    def put(name, v):
        a, w = HCST[name]
        c[:v.shape[0], a:a + w] = v.reshape(v.shape[0], -1)
    n, k = np.arange(L, dtype=np.float64), np.arange(L) + 0.5
    w = 2 * np.pi / (2 * L) * np.outer(n, k)
    C, S = np.cos(w).astype(np.float32), np.sin(w).astype(np.float32)
    put("fc", tiles_of(C))
    put("fs", tiles_of(S))
    put("ic", tiles_of(np.ascontiguousarray(C.T) / np.float32(L)))
    put("is", tiles_of(np.ascontiguousarray(S.T) / np.float32(L)))
    t = np.linspace(0.0, 1.0, L, dtype=np.float32)[:, None]
    deltas = np.linspace(-math.log(1e-2) / 1.5, -math.log(1e-2) / 0.3, HYW, dtype=np.float32)
    put("decay", tiles_of(np.exp(-t * deltas).astype(np.float32)))
    ang = (2.0 * math.pi * np.arange(L, dtype=np.float32)[:, None] / L).astype(np.float32)
    bands = np.linspace(1e-4, (FE - 1) // 2 - 1, (FE - 1) // 2, dtype=np.float32)
    z = np.concatenate([t, np.cos(bands * ang), -np.sin(bands * ang)], -1).astype(np.float32)
    put("zemb", np.ascontiguousarray(z.T))
    return c


def laid_out(i):
    i = {k: np.asarray(v) for k, v in i.items()}
    cols = np.zeros((P, NCOLS), np.float32)

    def put(name, v, rows=P):
        a, w = COLS[name]
        cols[:rows, a:a + w] = v
    put("ada_b", np.repeat(i["ada_b"].reshape(96, P).T[:, :, None], 2, 2).reshape(P, 192))
    put("c", np.stack([columns(i["c"][0]), columns(i["c_ctx"])], 2).reshape(P, 16))
    put("qn", columns(i["mla_q_norm"][0]))
    put("kvn", columns(i["mla_kv_norm"][0]))
    put("qqk", i["mla_q_qknorm"][0][:, None], QKH)
    put("kqk", i["mla_k_qknorm"][0][:, None], QKH)
    put("glub", columns(i["s5_glu_b"][0]))
    put("convw", i["hy_conv_w"][0].reshape(3 * 24, P).T)
    put("convb", columns(i["hy_conv_b"][0]))
    put("hybias", columns(i["hy_bias"][0]))
    put("fb1", i["hy_f_b1"][0][:, None], FH)
    put("fb2", i["hy_f_b2"][0][:, None], FH)
    put("freq", i["hy_f_freq"][0][:, None], FH)
    put("s5d", i["s5_d"][0].reshape(GP, 2 * C5).T, 2 * C5)
    s5p = np.zeros((P, NS5P), np.float32)

    def put5(name, v):
        a, w = S5P[name]
        v = v.reshape((2, GP, 2, N5) + v.shape[3:])
        v = np.moveaxis(v, (2, 3, 1, 0), (0, 1, 2, 3))
        s5p[:, a:a + w] = v.reshape(P, w)
    put5("lre", i["s5_lam_re"][0])
    put5("lim", i["s5_lam_im"][0])
    put5("lst", np.broadcast_to(i["s5_log_step"][0][:, :, None], (2, G5, N5)))
    put5("br", i["s5_b_re"][0])
    put5("bi", i["s5_b_im"][0])
    put5("cr", i["s5_c_re"][0].transpose(0, 1, 3, 2))
    put5("ci", i["s5_c_im"][0].transpose(0, 1, 3, 2))

    def weights(gate, up, down):
        lead = gate.shape[:-2]
        g, u = (w.reshape(lead + (KD, P, FF)) for w in (gate, up))
        d = down.reshape(lead + (FF // P, P, D))
        out = np.empty(lead + (P, WEXP), np.float32)
        n = len(lead)
        for a, w in ((0, g), (KD * FF, u), (2 * KD * FF, d)):
            out[..., a:a + w.shape[-3] * w.shape[-1]] = np.moveaxis(w, n, n + 1).reshape(lead + (P, -1))
        return out
    return {
        "cols": cols, "s5p": s5p, "cst": constants(), "hcst": hyena_constants(),
        "ada_w": np.ascontiguousarray(i["ada_w"].reshape(2, KD, P, 12, ADC).transpose(0, 3, 2, 1, 4)).reshape(NADC, P, KD, ADC),
        "xT": tiles_of(np.ascontiguousarray(i["x"][0].T)), "ctxT": tiles_of(np.ascontiguousarray(i["ctx"][0].T)),
        "w_in": tiles_of(i["ev_w_in"][0]), "w_uq": tiles_of(i["mla_w_uq"][0]), "w_ukv": i["mla_w_ukv"][0],
        "glu_w": tiles_of(i["s5_glu_w"][0]), "ev_w_out": tiles_of(i["ev_w_out"][0]),
        "hy_w_in": np.ascontiguousarray(i["hy_w_in"][0].reshape(KD, P, 6, 512).transpose(2, 1, 0, 3)),
        "hy_w_out": tiles_of(i["hy_w_out"][0]), "f_w1": i["hy_f_w1"][0], "f_w2": i["hy_f_w2"][0], "f_w3": i["hy_f_w3"][0],
        "router_w": np.ascontiguousarray(i["moe_router_w"].reshape(2, KD, P, NE).transpose(0, 2, 1, 3)),
        "router_b": i["moe_router_b"],
        "w_experts": weights(i["moe_w_gate"], i["moe_w_up"], i["moe_w_down"]),
        "w_shared": weights(i["moe_sh_gate"], i["moe_sh_up"], i["moe_sh_down"]),
    }


def kernel(**inputs):
    import concourse.bacc as bacc
    from concourse.bass_utils import run_bass_kernel_spmd

    nc = bacc.Bacc("TRN2", target_bir_lowering=False, num_devices=1)
    arrays = {f"in_{k}": np.ascontiguousarray(v) for k, v in laid_out(inputs).items()}
    A = {k[3:]: nc.dram_tensor(k, v.shape, mybir.dt.from_np(v.dtype), kind="ExternalInput").ap() for k, v in arrays.items()}
    A["out"] = nc.dram_tensor("out_x", (P, KD, L), F32, kind="ExternalOutput").ap()
    program(nc, A)
    r = run_bass_kernel_spmd(nc, [arrays], core_ids=[0])
    y = r.results[0]["out_x"]
    return np.ascontiguousarray(y.transpose(2, 1, 0).reshape(1, L, D))
```

```python
import math
from contextlib import ExitStack

import numpy as np
import concourse.bass as bass
from concourse import mybir

F32 = mybir.dt.float32
U32 = mybir.dt.uint32
ALU = mybir.AluOpType
ACT = mybir.ActivationFunctionType
AX = mybir.AxisListType

P = 128
D = 1024
KD = D // P
L = 256
EPS = 1e-6
HEADS, NOPE, ROPE, VH = 8, 64, 32, 64
QKH = NOPE + ROPE
QL, KVL = 256, 128
G5, C5, N5 = 32, 16, 64
T5 = 8
NCH = 2 * L // T5
XCH = L // T5
NT5 = G5
GP = G5 // 2
TW = T5 * C5
UOFF = QL + KVL + ROPE
EVIN = UOFF + G5 * C5
NE, TOPK, FF = 64, 6, 256
ROUTE_SCALE = 2.5
HYW = 1024
FH, FE = 64, 33
RING = 4
S = 64
NB = 2 + NE
GD = 4
OV_SEL, OV_INDEX, OV_TURNED, OV_HIDDEN, OV_HIDDEN_TURNED, OV_ROWS, OVD = 2, 9, 11, 12, 13, 14, 15
RPT = TOPK
WEXP = KD * FF * 2 + (FF // P) * D
ADC = 512
NADC = 2 * 6 * D // ADC
TWO_PI = 2.0 * math.pi
PI_HI = 6.28125
PI_LO = TWO_PI - PI_HI
ROUND = 12582912.0
PI_SAFE = 3.1415925


def offsets(widths):
    out, at = {}, 0
    for name, width in widths:
        out[name] = (at, width)
        at += width
    return out, at


COLS, NCOLS = offsets((("ada_b", 2 * 48 * 2), ("c", KD * 2), ("qn", 2), ("kvn", 1), ("qqk", 1), ("kqk", 1),
                       ("glub", 4), ("convw", 3 * 24), ("convb", 24), ("hybias", 8), ("fb1", 1), ("fb2", 1),
                       ("freq", 1), ("s5d", GP)))
S5P, NS5P = offsets((("lre", NT5), ("lim", NT5), ("lst", NT5), ("br", NT5 * C5), ("bi", NT5 * C5),
                     ("cr", NT5 * C5), ("ci", NT5 * C5)))
CST, NCST = offsets((("ident", P), ("cos", L), ("sin", L), ("swap", QKH), ("eye16", C5)))
MCST, NMCST = offsets((("tri", P), ("iota", S), ("iota_more", L - S), ("tok", 2), ("row", 2), ("beyond", 1)))
HCST, NHCST = offsets((("fc", 2 * L), ("fs", 2 * L), ("ic", 2 * L), ("is", 2 * L), ("decay", 2 * HYW), ("zemb", L)))


class Chain:

    def __init__(self, eng, semaphore, sem):
        self.eng, self.own, self.sem, self.n, self.counts = eng, semaphore, sem, 0, {}

    def __call__(self, ins):
        self.n += 1
        ins.then_inc(self.own, 1)
        self.eng.wait_ge(self.own, self.n)

    def then(self, ins, name):
        self.counts[name] = self.counts.get(name, 0) + 1
        ins.then_inc(self.sem(name), 1)
        self.eng.wait_ge(self.sem(name), self.counts[name])


def program(nc, A):
    with ExitStack() as ctx:
        sems = {}

        def sem(name):
            if name not in sems:
                sems[name] = ctx.enter_context(nc.semaphore(name))
            return sems[name]

        NAR = 53105
        ar = ctx.enter_context(nc.sbuf_tensor("arena", [P, NAR], F32))
        ps = ctx.enter_context(nc.psum_tensor("ps", [P, 8, 512], F32))
        scr = {n: nc.dram_tensor(n, sh, F32, kind="Internal").ap()
               for n, sh in (("u_scr", [G5 * C5, T5, NCH]), ("k_scr", [2 * C5, GP, 15 * C5]),
                             ("y_scr", [TW, G5, XCH]), ("h_scr", [L, D]), ("r_scr", [L * RPT, D]))}
        top = [0]

        def region(width):
            a = top[0]
            top[0] += width
            assert top[0] <= NAR, top
            return a

        def at(a, width, rows=P):
            return ar[0:rows, a:a + width]

        r_cst, r_cols, r_x, r_h = region(NCST), region(NCOLS), region(KD * L), region(2 * KD * L)
        r_mod, r_ones, r_row, r_sc = region(192), region(P), region(1024), region(16)
        r_eps, r_st, r_flag, r_pad = region(1), region(34), region(2), region(3)
        r_free = top[0]
        ident = at(r_cst, P)
        ones = at(r_ones, P)

        def cst(name, rows=P):
            a, w = CST[name]
            return at(r_cst + a, w, rows)

        def col(name, i=0, n=1, rows=P):
            return at(r_cols + COLS[name][0] + i, n, rows)

        def tiles(a, k, n, rows=P):
            return at(a, k * n, rows).rearrange("p (k t) -> p k t", k=k)

        xT = tiles(r_x, KD, L)
        hT = tiles(r_h, KD, 2 * L)
        hX = tiles(r_h, KD, L)
        sqX = tiles(r_h + KD * L, KD, L)
        mod = at(r_mod, 192).rearrange("p (l j k m) -> p l j k m", l=2, j=6, k=KD)
        modc = at(r_mod, 192).rearrange("p (c m) -> p c m", m=2)
        sc = at(r_sc, 16).rearrange("p (k m) -> p k m", m=2)
        adrow = at(r_row, 1024, 2).rearrange("p (b n) -> p b n", b=2)
        rsx = at(r_row, 512)
        stx = at(r_row + 512, 512)

        r1 = region(8192)
        r2 = region(2 * NT5 * 144)
        r3 = region(8192)
        r4 = region(4096)
        r6 = region(35 * 64)
        r7 = region(4096)
        r8 = region(2560)
        r9 = region(NS5P)
        r10 = region(3000)

        adw = at(r1, 8192).rearrange("p (b k n) -> p b k n", b=2, k=KD)
        w_in = tiles(r1, KD, EVIN)
        kh = tiles(r1, HEADS, 2 * L, QKH)
        qh = tiles(r1 + 4096, HEADS, L, QKH)
        vt = tiles(r1 + 6144, 4, 512)
        glu_w = tiles(r1, 4, 512)
        ctr = at(r2, NT5 * 144).rearrange("p (g d j c) -> p g d j c", d=2, j=9, c=C5)
        ctn = at(r2 + NT5 * 144, NT5 * 144).rearrange("p (g d j c) -> p g d j c", d=2, j=9, c=C5)
        bm = at(r3, 8192).rearrange("p (t r m) -> p t r m", t=NT5, r=2)
        sqk = tiles(r3, HEADS, 2 * L, QKH)
        sqq = tiles(r3 + 4096, HEADS, L, QKH)
        w_out = tiles(r3, KD, D)
        toep = tiles(r4, G5, TW)
        st = at(r6, 35 * 64).rearrange("p (s r t) -> p s r t", r=2, t=NT5)
        bt = at(r7, 4096).rearrange("p (b r t m) -> p b r t m", b=2, r=2, t=8)
        U = tiles(r7, G5, NCH)
        u_sb = at(r7 + 2048, 2048).rearrange("p (i t c) -> p i t c", i=4, t=T5)
        prob = tiles(r7 + 2048, 2, 512)
        att = tiles(r7 + 3072, 4, L)
        ysb = tiles(r3, G5, XCH)
        w_uq = tiles(r8, 2, 768)
        w_ukv = at(r8 + 1536, 1024)
        cx = tiles(r9, KD, L)
        pT = at(r9, 2048).rearrange("p (b k t) -> p b k t", b=2, k=4)
        kvl, krl, ql = at(r9, 512), at(r9 + 512, 512, QKH), tiles(r9 + 1024, 2, L)
        kk = at(r_h, GP * 240, 2 * C5).rearrange("p (g j c) -> p g j c", j=15, c=C5)
        est = at(r_h, 4096).rearrange("p (s r t) -> p s r t", r=2, t=NT5)
        sql = tiles(r_h, 3, 512)
        yT = at(r10 + 0, 1024).rearrange("p (i t c) -> p i t c", i=4, t=T5)
        zT = tiles(r10 + 1024, 4, L)

        def s5(name):
            a, w = S5P[name]
            v = at(r9 + a, w)
            return v if w == NT5 else v.rearrange("p (t c) -> p t c", c=C5)

        def sm(i, n=1):
            return at(r10 + NT5 * i, NT5 * n)
        pw = at(r10 + NT5 * 30, 18 * NT5).rearrange("p (r j t) -> p r j t", r=2, j=9)
        fb = at(r10 + NT5 * 48, 2 * NT5 * C5).rearrange("p (r t c) -> p r t c", r=2, c=C5)
        tmp5 = r10 + NT5 * 81
        bdr = at(r4, NT5 * 32).rearrange("p (t m) -> p t m", m=32)
        bdi = at(r4 + NT5 * 32, NT5 * 32).rearrange("p (t m) -> p t m", m=32)
        big = at(r3, 4096)
        r11 = region(4 * TW)

        m1 = r_free
        m2 = m1 + RING * WEXP
        wring = at(m1, RING * WEXP).rearrange("p (b n) -> p b n", b=RING)
        xg = tiles(m2, GD, D)
        xgT = at(m2 + GD * D, 2 * KD * S).rearrange("p (b k t) -> p b k t", b=2, k=KD)
        m3 = m2 + GD * D + 2 * KD * S
        yb = tiles(m3, GD, D)
        ysh = tiles(m3 + GD * D, 2, D)
        m4 = m3 + (GD + 2) * D
        sg, hh = tiles(m4, 2, FF), tiles(m4 + 512, 2, FF)
        hT2 = at(m4 + 1024, 2 * FF).rearrange("p (b f t) -> p b f t", b=2, f=2)
        rw = tiles(m4 + 1536, KD, NE)
        r_mc = m4 + 2048
        r_sel = r_mc + NMCST
        sel = at(r_sel, 4 * S).rearrange("p (b t s) -> p b t s", b=2, t=2)
        r_tab = r_sel + 4 * S
        pos = tiles(r_tab, 2, NE)
        rt = at(r_tab + 2 * NE, 6 * NE).rearrange("p (t e c) -> p t e c", t=2, c=3)
        wtab = at(r_tab + 8 * NE, NE, S)
        idx = at(r_tab + 9 * NE, 2 * NE, S).bitcast(U32).rearrange("p (c e) -> p c e", c=2)
        ib = at(r_tab + 11 * NE, 2 * GD, S).bitcast(U32)
        flags = at(r_flag, 2, 1).bitcast(U32)
        ov = at(r_tab + 11 * NE + 2 * GD + 8, 16, S)
        rtb = r_tab + 12 * NE
        assert rtb + 24 * NE <= NAR

        def mcst(name, i=0, n=None):
            a, w = MCST[name]
            return at(r_mc + a + i, w if n is None else n)

        def gate_up(slot, k):
            return wring[:, slot, k * 2 * FF:(k + 1) * 2 * FF]

        def w_down(slot, f, c):
            a = 2 * KD * FF + f * D + c * 512
            return wring[:, slot, a:a + 512]

        def slot_of(n):
            return 0 if n < 2 else (n - 1) % RING

        def rows_of(n):
            return P if n < 2 else S

        def steady(step, eng, rounds=(NB - 6) // 4):
            for n in range(3):
                step(n, 0)
            with eng.Fori(0, rounds) as i:
                for n in range(3, 7):
                    step(n, i)
            for n in range(3 + 4 * rounds, NB + 1):
                step(n, 0)

        def overflow(li, eng, body, last=None):
            r = eng.value_load(flags[:, li:li + 1], min_val=0, max_val=L)
            for s in range(1, L // S):
                with eng.If(r > s * S):
                    with eng.Fori(0, NE) as i:
                        body(s, i)
                    if last:
                        last(s)
                eng.nop()

        hyw = at(m1, 3 * 4096).rearrange("p (b k n) -> p b k n", b=3, k=KD)
        hyo = tiles(m1, KD, D)
        hc0 = m1 + 3 * 4096
        xc = tiles(hc0 + NHCST, 24, L)
        ff0 = hc0 + NHCST + 24 * L
        pp = at(ff0, 2 * 4 * L).rearrange("p (b i t) -> p b i t", b=2, i=4)
        zt = tiles(ff0 + 2048, KD, L)
        zs = tiles(ff0 + 4096, 2, HYW)
        hf = tiles(ff0 + 6144, 4, HYW)
        HR, HS = tiles(ff0 + 10240, 2, HYW), tiles(ff0 + 12288, 2, HYW)
        f_w3 = at(ff0 + 14336, 2048, FH)
        f_w1 = at(ff0 + 16384, FH, FE)
        f_w2 = at(ff0 + 16384 + FH, FH, FH)
        hid = tiles(ff0 + 16512, 2, L, FH)
        hsc = ff0 + 17024
        hns = at(hsc + 1024, 8)
        YR, YS = tiles(ff0 + 6144, 2, HYW), tiles(ff0 + 8192, 2, HYW)
        ytmp = tiles(ff0 + 4096, 2, HYW)
        assert hsc + 1040 <= NAR, hsc

        def hcst(name, k=2, rows=P):
            a, w = HCST[name]
            v = at(hc0 + a, w, rows)
            return v if k == 1 else v.rearrange("p (k t) -> p k t", k=k)

        def scol(li, j, k, m=0):
            return mod[:, li, j, k, m:m + 1]

        def ada_turn(pe, i):
            pe.wait_ge(sem("adrow_ready"), i + 1)
            if i >= 1:
                pe.wait_ge(sem("modc_ready"), i)
            for j in range(4):
                last = pe.matmul(ps[:, 2, 2 * j:2 * j + 2], adrow[:, i % 2, j * P:(j + 1) * P], ident[0:2, 0:2], start=True, stop=True)
            last.then_inc(sem("ada_turned"), 1)

        def turned(act, f, ch, n):
            h, t = n // 2, n % 2
            act.wait_ge(sem("pT_mm"), n + 1)
            if h >= 2:
                act.wait_ge(sem("pv_mm"), h - 1)
            ch.then(f(pT[:, h % 2, :, t * P:(t + 1) * P], ps[:, 2 + n % 2, :].rearrange("p (k q) -> p k q", k=4), ACT.Copy), "pT_ready")

        def attend_out(dve, ch, h):
            dve.wait_ge(sem("pv_mm"), h + 1)
            rows = slice((h % 2) * VH, (h % 2 + 1) * VH)
            ch.then(dve.tensor_copy(att[rows, h // 2], ps[rows, 4 if h % 2 == 0 else 7, 0:L]), "att_ready")

        block = ctx.enter_context(nc.Block())

        @block.sync
        def _(sp):
            def load(dst, src, name, n=16):
                sp.dma_start(dst, src).then_inc(sem(name), 16)

            load(at(r_cols, NCOLS), A["cols"], "small_in")
            load(at(r9, NS5P), A["s5p"], "s5p_in")
            load(at(r_cst, NCST), A["cst"], "small_in")
            load(w_uq, A["w_uq"], "uw_in")
            load(w_ukv, A["w_ukv"], "uw_in")
            for i in range(NADC):
                if i >= 2:
                    sp.wait_ge(sem("ada_mm"), i - 1)
                load(adw[:, i % 2], A["ada_w"][i], f"ada_in{i % 2}")
            load(xT, A["xT"], "x_in")
            sp.wait_ge(sem("s5_params_used"), 1)
            load(cx, A["ctxT"], "ctx_in")
            sp.wait_ge(sem("ada_mm"), NADC)
            load(w_in, A["w_in"], "win_in")
            sp.wait_ge(sem("kk_ready"), 1)
            load(scr["k_scr"], kk.rearrange("p g j c -> p g (j c)"), "kscr_out")
            sp.wait_ge(sem("kscr_out"), 16)
            sp.wait_ge(sem("bd_used"), 1)
            for t in range(T5):
                for g2 in range(2):
                    load(toep[t * C5:(t + 1) * C5].rearrange("p (g b) m -> p g b m", b=2)[:, :, g2],
                         scr["k_scr"][g2 * C5:(g2 + 1) * C5, :, (T5 - 1 - t) * C5:(2 * T5 - 1 - t) * C5], "toep_in")
            sp.wait_ge(sem("u_evicted"), 4)
            load(scr["u_scr"].rearrange("(i p) t c -> p i (t c)", p=P), u_sb.rearrange("p i t c -> p i (t c)"), "uscr_out")
            sp.wait_ge(sem("uscr_out"), 16)
            for t in range(T5):
                load(U[t * C5:(t + 1) * C5], scr["u_scr"][:, t].rearrange("(g p) c -> p g c", p=C5), "U_in")
            sp.wait_ge(sem("scores_done"), 2 * HEADS)
            load(glu_w, A["glu_w"], "glu_in")
            sp.wait_ge(sem("y_evicted"), 2)
            load(scr["y_scr"], ysb, "yscr_out")
            sp.wait_ge(sem("yscr_out"), 16)
            for g8 in range(8):
                for i in range(4):
                    load(yT[g8 * C5:(g8 + 1) * C5, i],
                         scr["y_scr"].rearrange("(t p) g c -> p t g c", p=C5)[:, :, i * 8 + g8], "yT_in")
            load(w_out, A["ev_w_out"], "wout_in")

            def moe_loads(li):
                sp.wait_ge(sem("x_mixed"), li + 1)
                load(rw, A["router_w"][li], "rw_in")
                load(at(rtb, NE), A["router_b"][li:li + 1].broadcast_to([P, NE]), "rw_in")
                load(at(r_mc, NMCST), A["mcst"], "rw_in")
                load(wring[:, 0], A["w_shared"][li], "w_slot0")
                for e in range(RING - 1):
                    load(wring[:, e + 1], A["w_experts"][li, e], f"w_slot{e + 1}")
                sp.wait_ge(sem("hrow_ready"), 4 * (li + 1))
                load(scr["h_scr"].rearrange("(t p) n -> p t n", p=P), xg[:, 0:2], "hscr_out")

                def step(n, i):
                    if 5 <= n < NB:
                        sp.wait_ge(sem("dn_mm"), li * NB + (n - 3) + 4 * i)
                        sp.dma_start(wring[:, slot_of(n)], A["w_experts"][li, (n - 2) + 4 * i]).then_inc(sem(f"w_slot{slot_of(n)}"), 16)
                with sp.Fori(0, (NE - RING) // RING) as i:
                    for n in range(5, 9):
                        step(n, i)
                step(NB - 1, 0)
                for b in range(GD):
                    sp.wait_ge(sem(f"scat{b}"), 16 * (NE // GD) * (li + 1))

                def more(s, i):
                    sp.wait_ge(sem(f"ov_q{li}"), i * 32 + 32 * NE * (s - 1))
                    sp.dma_start(wring[:, 0], A["w_experts"][li, i]).then_inc(sem(f"ov_w{li}"), 16)
                overflow(li, sp, more, lambda s: sp.wait_ge(sem(f"ov_q{li}"), 32 * NE * s))
                for t in range(2):
                    load(wring[:, t], scr["r_scr"].rearrange("(t p k) n -> t p (k n)", t=2, p=P)[t], "rows_in")

            moe_loads(0)
            sp.wait_ge(sem("moe_x"), 1)
            load(at(hc0, NHCST), A["hcst"], "fw_in")
            load(f_w1, A["f_w1"], "fw_in")
            load(f_w2, A["f_w2"], "fw_in")
            load(f_w3, A["f_w3"], "fw_in")
            for i in range(6):
                if i >= 3:
                    sp.wait_ge(sem("hy_proj"), i - 2)
                load(hyw[:, i % 3], A["hy_w_in"][i], f"hyw_in{i % 3}")
            sp.wait_ge(sem("hy_proj"), 6)
            load(hyo, A["hy_w_out"], "hyo_in")
            moe_loads(1)
            sp.wait_ge(sem("moe_x"), 2)
            load(A["out"], xT, "out_done")
            sp.wait_ge(sem("out_done"), 16)

        @block.gpsimd
        def _(pool):
            ch = Chain(pool, sem("pool_chain"), sem)
            ch.then(pool.memset(ones, 1.0), "ones_ready")
            ch(pool.memset(st[:, 0], 0.0))
            lam8 = pw[:, :, 8]
            A8, B8 = tiles(tmp5, 2, NT5), tiles(tmp5 + 64, 2, NT5)
            t1, t2 = tiles(tmp5 + 128, 2, NT5), tiles(tmp5 + 192, 2, NT5)
            pool.wait_ge(sem("lam8_ready"), 1)
            pool.wait_ge(sem("est_ready"), 8)
            for k in range(NCH):
                a = k % 2 if k < NCH // 2 else 2 + k - NCH // 2
                b = (k + 1) % 2 if k + 1 < NCH // 2 else 2 + k + 1 - NCH // 2
                ins = pool.tensor_tensor(t1, A8, st[:, a], ALU.mult)
                ch(ins)
                ch(pool.tensor_tensor(t2, B8, st[:, a, ::-1], ALU.mult))
                ch(pool.tensor_tensor(t1, t1, est[:, k], ALU.add))
                ch(pool.tensor_tensor(st[:, b], t1, t2, ALU.add))
            ch.then(pool.memset(t1, 0.0), "scan_done")

            def moe_pool(li):
                def gather(out, index, name):
                    pool.indirect_dma_start(out, None, scr["h_scr"], bass.IndirectOffsetOnAxis(index, 0), bounds_check=L - 1,
                                            oob_is_err=False).then_inc(sem(name), 16)

                def scatter(index, in_, name):
                    pool.indirect_dma_start(scr["r_scr"], bass.IndirectOffsetOnAxis(index, 0), in_, None, bounds_check=L * RPT - 1,
                                            oob_is_err=False).then_inc(sem(name), 16)

                def stand(name, count):
                    pool.wait_ge(sem(name), count)
                    pool.tensor_tensor(pads[name[:4]], ones[:, 0:1], ones[:, 0:1], ALU.add).then_inc(sem(name), 1)

                def gather_block(n, i):
                    b = n % GD
                    pool.tensor_copy(ib[:, b:b + 1], idx[:, 0, bass.ds(n - 2 + 4 * i, 1)]).then_inc(sem("ib_g"), 1)
                    stand("ib_g", 2 * (li * NE + n - 2) + 1 + 8 * i)
                    gather(xg[0:S, b], ib[:, b:b + 1], f"gath{b}")

                def step(n, i):
                    if n + GD < NB:
                        if n >= 2:
                            pool.wait_ge(sem("tx_mm"), li * NE + n - 1 + 4 * i)
                        gather_block(n + GD, i)
                    if n >= 3:
                        b = (n - 1) % GD
                        pool.wait_ge(sem("y_act"), li * NB + n + 4 * i)
                        pool.wait_ge(sem("y_dve"), li * NB + n + 4 * i)
                        pool.tensor_copy(ib[:, GD + b:GD + b + 1], idx[:, 1, bass.ds(n - 3 + 4 * i, 1)]).then_inc(sem("ib_s"), 1)
                        stand("ib_s", 2 * (li * NE + n - 3) + 1 + 8 * i)
                        scatter(ib[:, GD + b:GD + b + 1], yb[0:S, b], f"scat{b}")
                pool.wait_ge(sem("idx_ready"), li + 1)
                pool.wait_ge(sem("hscr_out"), 16 * (li + 1))
                ch(pool.memset(xg.rearrange("p b n -> p (b n)"), 0.0))
                gather_block(2, 0)
                gather_block(3, 0)
                steady(step, pool, (NB - 6) // 4 - 1)

                def more(s, i):
                    pool.wait_ge(sem(f"ov_d{li}"), i * OVD + OVD * NE * (s - 1) + OV_INDEX)
                    stand(f"ov_t{li}", i * 2 + 2 * NE * (s - 1))
                    gather(xg[0:S, 0], ib[:, 0:1], f"ov_q{li}")
                    pool.wait_ge(sem(f"ov_d{li}"), i * OVD + OVD * NE * (s - 1) + OV_ROWS)
                    stand(f"ov_t{li}", i * 2 + 2 * NE * (s - 1) + 1)
                    scatter(ib[:, GD:GD + 1], yb[0:S, 0], f"ov_q{li}")
                overflow(li, pool, more)
                pool.wait_ge(sem("rows_in"), 32 * (li + 1))
                for k in range(RPT):
                    ins = pool.tensor_tensor(xg[:, 1], ysh[:, 1] if k == 0 else xg[:, 1], wring[:, 1, k * D:(k + 1) * D], ALU.add)
                    ch(ins) if k < RPT - 1 else ch.then(ins, "sum_pool")

            pads = {"ib_g": at(r_pad, 1), "ib_s": at(r_pad + 1, 1), "ov_t": at(r_pad + 2, 1)}
            moe_pool(0)
            moe_pool(1)

        @block.tensor
        def _(pe):
            def mm(out, lhsT, rhs, start, stop, skip=False):
                return pe.matmul(out, lhsT, rhs, start=start, stop=stop, skip_group_check=skip)

            def sum_squares(src, bank, n):
                for k in range(KD):
                    last = mm(ps[:, bank, 0:n], ones, src[:, k], k == 0, k == KD - 1)
                return last

            pe.wait_ge(sem("sc_ready"), 1)
            pe.wait_ge(sem("small_in"), 32)
            for i in range(NADC):
                pe.wait_ge(sem(f"ada_in{i % 2}"), 16 * (i // 2 + 1))
                if i >= 2:
                    pe.wait_ge(sem("adrow_ready"), i - 1)
                for k in range(KD):
                    last = mm(ps[0:2, i % 2, :], sc[:, k], adw[:, i % 2, k], k == 0, k == KD - 1)
                last.then_inc(sem("ada_mm"), 1)
                if i >= 1:
                    ada_turn(pe, i - 1)
            ada_turn(pe, NADC - 1)
            pe.wait_ge(sem("ctab_ready"), 1)
            for t in range(NT5):
                g, d = t // 2, t % 2
                bank, off = 3 + (t % 16) // 4, (t % 4) * TW
                if t == 16:
                    pe.wait_ge(sem("kk_half"), 1)
                o = ps[0:2 * C5, bank, off:off + TW]
                j0 = 0 if d == 0 else 1
                mm(o, bdr[:, t], ctr[:, g, d, j0:j0 + T5].rearrange("p j c -> p (j c)"), True, False)
                last = mm(o, bdi[:, t], ctn[:, g, d, j0:j0 + T5].rearrange("p j c -> p (j c)"), False, True)
                if t == 15:
                    last.then_inc(sem("kk_mm"), 1)
            last.then_inc(sem("kk_mm"), 1)
            for q in range(4):
                pe.wait_ge(sem("bt_ready"), q + 1)
                for r in range(2):
                    for hb in range(2):
                        n = 4 * q + 2 * r + hb
                        if n >= 2:
                            pe.wait_ge(sem("bm_evicted"), n - 1)
                        for t in range(4):
                            last = pe.transpose(ps[:, n % 2, t * P:(t + 1) * P], bt[:, q % 2, r, hb * 4 + t], ident)
                        last.then_inc(sem("bt_turned"), 1)
            pe.wait_ge(sem("squared"), 2)
            pe.wait_ge(sem("ones_ready"), 1)
            sum_squares(hT, 7, 512).then_inc(sem("norm_mm"), 1)
            pe.wait_ge(sem("win_in"), 16)
            pe.wait_ge(sem("h_ready"), 1)
            pe.wait_ge(sem("bm_evicted"), 16)
            for bank, c0, m, tok in ((0, QL, P, 0), (1, QL + KVL - NOPE, QKH, 0)):
                for k in range(KD):
                    last = mm(ps[0:m, bank, :], w_in[:, k, c0:c0 + m], hT[:, k], k == 0, k == KD - 1)
                last.then_inc(sem("proj_mm"), 1)
            for i in range(2):
                for k in range(KD):
                    last = mm(ps[:, 2, i * L:(i + 1) * L], w_in[:, k, i * P:(i + 1) * P], hT[:, k, L:2 * L], k == 0, k == KD - 1)
            last.then_inc(sem("proj_mm"), 1)
            for i in range(4):
                for k in range(KD):
                    last = mm(ps[:, 3 + i, :], w_in[:, k, UOFF + i * P:UOFF + (i + 1) * P], hT[:, k], k == 0, k == KD - 1)
                last.then_inc(sem("proj_mm"), 1)
            pe.wait_ge(sem("squared"), 2 + 2)
            pe.wait_ge(sem("kvl_evicted"), 3)
            mm(ps[:, 7, :], ones, sql[:, 0], True, True).then_inc(sem("lat_mm"), 1)
            for i in range(2):
                last = mm(ps[:, 0, 0:L], ones, sql[:, 1, i * L:(i + 1) * L], i == 0, i == 1)
            last.then_inc(sem("lat_mm"), 1)
            pe.wait_ge(sem("ql_normed"), 1)
            pe.wait_ge(sem("u_evicted"), 4)
            pe.wait_ge(sem("uw_in"), 32)
            pe.wait_ge(sem("uw_in"), 32)
            for h in range(HEADS):
                for k in range(2):
                    last = mm(ps[0:QKH, 3 + h // 2, (h % 2) * L:(h % 2 + 1) * L], w_uq[:, k, h * QKH:(h + 1) * QKH], ql[:, k], k == 0, k == 1)
                if h % 2:
                    last.then_inc(sem("head_mm"), 1)
            kbank = (0, 1, 2, 7)
            for h in range(HEADS):
                if h >= 4:
                    pe.wait_ge(sem("kh_evicted"), h - 3)
                mm(ps[0:NOPE, kbank[h % 4], :], w_ukv[:, h * P:h * P + NOPE], kvl, True, True).then_inc(sem("head_mm"), 1)
            for t in range(4):
                pe.wait_ge(sem("qh_evicted"), t + 1)
                mm(ps[:, 3 + t, :], kvl[:, t * P:(t + 1) * P],
                   w_ukv.rearrange("p (h n) -> p h n", h=HEADS)[:, :, NOPE:P], True, True).then_inc(sem("head_mm"), 1)
            pe.wait_ge(sem("U_in"), 16 * T5)
            pe.wait_ge(sem("kh_evicted"), 8)
            pe.wait_ge(sem("vt_evicted"), 4)
            for b in range(8):
                for t in range(8):
                    tile, r = (b // 2) * 8 + t, b % 2
                    for g2 in range(2):
                        last = mm(ps[g2 * N5:(g2 + 1) * N5, b, t * NCH:(t + 1) * NCH], bm[:, tile, r, g2 * N5:(g2 + 1) * N5],
                                  U[:, 2 * (tile // 2) + g2], True, True)
                last.then_inc(sem("head_mm"), 1)
            pe.wait_ge(sem("squared"), 4 + 1)
            for h in range(HEADS):
                if h % 2 == 0:
                    pe.wait_ge(sem("est_ready"), 8)
                last = mm(ps[0:QKH, h // 2, (h % 2) * L:(h % 2 + 1) * L], ones[0:QKH, 0:QKH], sqq[:, h], True, True)
                if h % 2:
                    last.then_inc(sem("rot_mm"), 1)
            pe.wait_ge(sem("squared"), 5 + 1)
            for h in range(HEADS):
                if h >= 4:
                    pe.wait_ge(sem("krms"), h - 3)
                mm(ps[0:QKH, 4 + h % 4, :], ones[0:QKH, 0:QKH], sqk[:, h], True, True).then_inc(sem("rot_mm"), 1)
            pe.wait_ge(sem("qrms"), 4)
            pe.wait_ge(sem("qh_normed"), 1)
            for b in range(4):
                mm(ps[0:QKH, b, :], cst("swap", QKH), qh[:, 2 * b:2 * b + 2].rearrange("p h t -> p (h t)"), True, True).then_inc(sem("rot_mm"), 1)
            pe.wait_ge(sem("krms"), 8)
            pe.wait_ge(sem("kh_normed"), 1)
            for b in range(4):
                mm(ps[0:QKH, 4 + b, :], cst("swap", QKH), kh[:, 2 * b:2 * b + 2, L:2 * L], True, True).then_inc(sem("rot_mm"), 1)
            pe.wait_ge(sem("rope_done"), 2)

            def scores(n):
                h, t = n // 2, n % 2
                if n >= 2:
                    pe.wait_ge(sem("exp_done"), n - 1)
                mm(ps[:, n % 2, :], qh[:, h, t * P:(t + 1) * P], kh[:, h], True, True).then_inc(sem("scores_done"), 1)
            scores(0)
            for n in range(2 * HEADS):
                h, t = n // 2, n % 2
                if n + 1 < 2 * HEADS:
                    scores(n + 1)
                pe.wait_ge(sem("prob_ready"), n + 1)
                if n >= 2:
                    pe.wait_ge(sem("pT_ready"), n - 1)
                for k in range(4):
                    last = pe.transpose(ps[:, 2 + n % 2, k * P:(k + 1) * P], prob[:, n % 2, k * P:(k + 1) * P], ident)
                last.then_inc(sem("pT_mm"), 1)
                if t == 1:
                    pe.wait_ge(sem("pT_ready"), n + 1)
                    if h >= 2:
                        pe.wait_ge(sem("att_ready"), h - 1)
                    o = ps[(h % 2) * VH:(h % 2 + 1) * VH, 4 if h % 2 == 0 else 7, 0:L]
                    for k in range(4):
                        last = mm(o, vt[:, k, h * VH:(h + 1) * VH], pT[:, h % 2, k], k == 0, k == 3)
                    last.then_inc(sem("pv_mm"), 1)
            pe.wait_ge(sem("scan_done"), 1)
            pe.wait_ge(sem("toep_in"), 16 * 2 * T5)
            for g in range(G5):
                o = ps[:, 5 + g % 2, (g // 2) * XCH:(g // 2 + 1) * XCH]
                rows = slice((g % 2) * N5, (g % 2 + 1) * N5)
                mm(o, toep[:, g], U[:, g, XCH:2 * XCH], True, False)
                for d in range(2):
                    sl = st[rows, 2:2 + XCH] if d == 0 else st[rows, 1 + XCH:1:-1]
                    j0 = 1 - d
                    for r, tab in ((0, ctr), (1, ctn)):
                        last = mm(o, tab[rows, g // 2, d, j0:j0 + T5].rearrange("p j c -> p (j c)"),
                                  sl[:, :, r, (g // 2) * 2 + d], False, d == 1 and r == 1)
            last.then_inc(sem("y_mm"), 1)
            pe.wait_ge(sem("z_ready"), 1)
            pe.wait_ge(sem("glu_in"), 16)
            for j in range(4):
                for k in range(4):
                    last = mm(ps[:, 5 + j // 2, (j % 2) * L:(j % 2 + 1) * L], glu_w[:, k, j * P:(j + 1) * P], zT[:, k], k == 0, k == 3)
                last.then_inc(sem("glu_mm"), 1)
            pe.wait_ge(sem("att_ready"), HEADS)
            pe.wait_ge(sem("s5_out"), 4)
            pe.wait_ge(sem("wout_in"), 16)
            for j in range(KD):
                for k in range(KD):
                    rhs = att[:, k] if k < 4 else zT[:, k - 4]
                    last = mm(ps[:, j // 2, (j % 2) * L:(j % 2 + 1) * L], w_out[:, k, j * P:(j + 1) * P], rhs, k == 0, k == KD - 1)
                last.then_inc(sem("mix_mm"), 1)

            def moe_pe(li):
                pe.wait_ge(sem("squared"), 7 + 3 * li)
                sum_squares(sqX, 6, L).then_inc(sem("norm_mm"), 1)
                pe.wait_ge(sem("moe_h"), li + 1)
                pe.wait_ge(sem("rw_in"), 48 * (li + 1))
                for t in range(2):
                    for k in range(KD):
                        last = mm(ps[:, 7, t * NE:(t + 1) * NE], hX[:, k, t * P:(t + 1) * P], rw[:, k], k == 0, k == KD - 1)
                last.then_inc(sem("logits"), 1)
                for t in range(2):
                    for c in range(2):
                        for k in range(4):
                            last = pe.transpose(ps[:, 3 + 2 * t + c, k * P:(k + 1) * P], hX[:, 4 * c + k, t * P:(t + 1) * P], ident)
                        last.then_inc(sem("hrow_mm"), 1)
                pe.wait_ge(sem("route"), 2 * (li + 1))
                m0, m1_ = at(rtb + 10 * NE, NE), at(rtb + 11 * NE, NE)
                mm(ps[:, 7, 0:NE], mcst("tri"), m0, True, True)
                mm(ps[:, 7, NE:2 * NE], ones, m0, True, False)
                mm(ps[:, 7, NE:2 * NE], mcst("tri"), m1_, False, True)
                mm(ps[:, 7, 2 * NE:3 * NE], ones, m0, True, False)
                mm(ps[:, 7, 2 * NE:3 * NE], ones, m1_, False, True).then_inc(sem("pos_mm"), 1)

                def turn(out, in_, one, first):
                    return mm(out, in_, one, True, True) if first else pe.transpose(out, in_, one)

                def half_gate_up(n, k0):
                    for k in range(k0, k0 + 4):
                        lhsT = hX[:, k, n * P:(n + 1) * P] if n < 2 else xgT[:, n % 2, k]
                        last = mm(ps[0:rows_of(n), 2 + n % 2, :], lhsT, gate_up(slot_of(n), k), k == 0, k == KD - 1)
                    return last

                def step(n, i):
                    def at_least(name, count, per=NB):
                        pe.wait_ge(sem(name), li * per + count + 4 * i)
                    m = n + 1
                    if 2 <= m < NB:
                        pe.wait_ge(sem(f"gath{m % GD}"), 16 * (li * (NE // GD) + (m - 2) // GD + 1) + 16 * i)
                        if m >= 3:
                            at_least("xt_act", m - 2, NE)
                            at_least("xt_dve", m - 2, NE)
                        for k in range(KD):
                            last = turn(ps[:, k // 4, (k % 4) * S:(k % 4 + 1) * S], xg[0:S, m % GD, k * P:(k + 1) * P], ident[0:S, 0:S], k == 0)
                        last.then_inc(sem("tx_mm"), 1)
                    if n < NB:
                        if n < 2:
                            pe.wait_ge(sem("w_slot0"), 16 * (17 * li + 1))
                        else:
                            s_ = slot_of(n)
                            pe.wait_ge(sem(f"w_slot{s_}"), 16 * (li * (17 if s_ == 0 else 16) + (n - 1) // RING + 1) + 16 * i)
                            at_least("xt_act", n - 1, NE)
                            at_least("xt_dve", n - 1, NE)
                            at_least("h_done", n - 1)
                        half_gate_up(n, 0)
                    if n >= 1:
                        at_least("h_done", n)
                        if n >= 2:
                            at_least("hT_ready", n - 1)
                        for f in range(2):
                            q = rows_of(n - 1)
                            last = turn(ps[:, 4, f * q:(f + 1) * q], hh[0:q, (n - 1) % 2, f * P:(f + 1) * P], ident[0:q, 0:q], f == 0)
                        last.then_inc(sem("ht_mm"), 1)
                    if n < NB:
                        half_gate_up(n, 4).then_inc(sem("gu_mm"), 1)
                    if n >= 1:
                        at_least("hT_ready", n)
                        if n >= 2:
                            at_least("y_act", n - 1)
                            at_least("y_dve", n - 1)
                        for c in range(2):
                            for f in range(2):
                                q = rows_of(n - 1)
                                last = mm(ps[0:q, 5 + c, :], hT2[:, (n - 1) % 2, f, 0:q], w_down(slot_of(n - 1), f, c), f == 0, f == 1)
                        last.then_inc(sem("dn_mm"), 1)
                pe.wait_ge(sem("hrow_ready"), 4 * (li + 1))
                step(0, 0)
                with pe.Fori(0, NE // 2) as i:
                    for b in range(2):
                        pe.wait_ge(sem("sel_ready"), i * 2 + (li * NE + b + 1))
                        for t in range(2):
                            last = mm(ps[0:S, 7, bass.ds(i * 6 + 3 * b, 3)], sel[:, b, t], rt[:, t, bass.ds(i * 2 + b, 1)].rearrange("p e c -> p (e c)"), t == 0, t == 1, skip=True)
                        last.then_inc(sem("tab_mm"), 1)
                for n in range(1, 3):
                    step(n, 0)
                with pe.Fori(0, (NB - 6) // 4) as i:
                    for n in range(3, 7):
                        step(n, i)
                for n in range(NB - 3, NB + 1):
                    step(n, 0)
                def more(s, i):
                    ovd, ovp = sem(f"ov_d{li}"), sem(f"ov_p{li}")
                    base = NE * (s - 1)
                    pe.wait_ge(ovd, i * OVD + OVD * base + OV_SEL)
                    for t in range(2):
                        last = mm(ps[0:S, 7, 0:3], sel[:, 0, t], sel[:, 1, t, 0:3], t == 0, t == 1)
                    last.then_inc(ovp, 1)
                    pe.wait_ge(sem(f"ov_q{li}"), i * 32 + 32 * base + 16)
                    for k in range(KD):
                        last = turn(ps[:, k // 4, (k % 4) * S:(k % 4 + 1) * S], xg[0:S, 0, k * P:(k + 1) * P], ident[0:S, 0:S], k == 0)
                    last.then_inc(ovp, 1)
                    pe.wait_ge(sem(f"ov_w{li}"), i * 16 + 16 * (base + 1))
                    pe.wait_ge(ovd, i * OVD + OVD * base + OV_TURNED)
                    for k in range(KD):
                        last = mm(ps[0:S, 2, :], xgT[:, 0, k], gate_up(0, k), k == 0, k == KD - 1)
                    last.then_inc(ovp, 1)
                    pe.wait_ge(ovd, i * OVD + OVD * base + OV_HIDDEN)
                    for f in range(2):
                        last = turn(ps[:, 4, f * S:(f + 1) * S], hh[0:S, 0, f * P:(f + 1) * P], ident[0:S, 0:S], f == 0)
                    last.then_inc(ovp, 1)
                    pe.wait_ge(ovd, i * OVD + OVD * base + OV_HIDDEN_TURNED)
                    for c in range(2):
                        for f in range(2):
                            last = mm(ps[0:S, 5 + c, :], hT2[:, 0, f, 0:S], w_down(0, f, c), f == 0, f == 1)
                    last.then_inc(ovp, 1)
                overflow(li, pe, more)
                for t in range(2):
                    pe.wait_ge(sem("sum_dve" if t == 0 else "sum_pool"), li + 1)
                    for k in range(KD):
                        last = pe.transpose(ps[:, k // 2, (k % 2) * L + t * P:(k % 2) * L + (t + 1) * P], xg[:, t, k * P:(k + 1) * P], ident)
                    last.then_inc(sem("out_mm"), 1)

            moe_pe(0)
            pe.wait_ge(sem("fw_in"), 64)
            mm(ps[0:FH, 4, 0:L], f_w1, hcst("zemb", 1, FE), True, True).then_inc(sem("filter_mm"), 1)
            pe.wait_ge(sem("hid_ready"), 1)
            mm(ps[0:FH, 5, 0:L], f_w2, hid[:, 0], True, True).then_inc(sem("filter_mm"), 1)
            pe.wait_ge(sem("hid_ready"), 2)
            for t in range(2):
                for j in range(4):
                    mm(ps[:, (t * 4 + j) % 8, :], hid[:, 1, t * P:(t + 1) * P], f_w3[:, j * 512:(j + 1) * 512], True, True).then_inc(sem("filter_mm"), 1)
            pe.wait_ge(sem("squared"), 7 + 1)
            for j in range(8):
                for k in range(4):
                    last = mm(ps[:, 0, j:j + 1], tiles(ff0, 4, HYW)[:, k, j * P:(j + 1) * P], ones[:, 0:1], k == 0, k == 3)
            last.then_inc(sem("filter_mm"), 1)
            pe.wait_ge(sem("hf_comb"), 1)
            for w, (mat, src) in enumerate((("fc", 0), ("fs", 2))):
                for m in range(2):
                    for c in range(2):
                        n = w * 4 + m * 2 + c
                        if n == 0:
                            pe.wait_ge(sem("hn_read"), 1)
                        for k in range(2):
                            last = mm(ps[:, n, :], hcst(mat)[:, k, m * P:(m + 1) * P], hf[:, src + k, c * 512:(c + 1) * 512], k == 0, k == 1)
                        last.then_inc(sem("filter_mm"), 1)
            pe.wait_ge(sem("squared"), 8 + 1)
            pe.wait_ge(sem("H_evicted"), 8)
            sum_squares(sqX, 6, L).then_inc(sem("norm_mm"), 1)
            pe.wait_ge(sem("hy_h"), 1)
            for i in range(6):
                pe.wait_ge(sem(f"hyw_in{i % 3}"), 16 * (i // 3 + 1))
                if i >= 2:
                    pe.wait_ge(sem("hyp_evicted"), i - 1)
                for j in range(4):
                    for k in range(KD):
                        last = mm(ps[:, 2 * (i % 2) + j // 2, (j % 2) * L:(j % 2 + 1) * L], hyw[:, i % 3, k, j * P:(j + 1) * P], hX[:, k], k == 0, k == KD - 1)
                last.then_inc(sem("hy_proj"), 1)
            pe.wait_ge(sem("z_conv"), 1)
            for t in range(2):
                for hb in range(2):
                    for j in range(4):
                        last = pe.transpose(ps[:, 4 + 2 * t + hb, j * P:(j + 1) * P], zt[:, hb * 4 + j, t * P:(t + 1) * P], ident)
                    last.then_inc(sem("zs_mm"), 1)
            pe.wait_ge(sem("zs_ready"), 4)
            for w, mat in enumerate(("fc", "fs")):
                for m in range(2):
                    for c in range(2):
                        n = w * 4 + m * 2 + c
                        for k in range(2):
                            last = mm(ps[:, n, :], hcst(mat)[:, k, m * P:(m + 1) * P], zs[:, k, c * 512:(c + 1) * 512], k == 0, k == 1)
                        last.then_inc(sem("Z_mm"), 1)
            pe.wait_ge(sem("Y_ready"), 1)
            for j in range(KD):
                for w, (mat, src) in enumerate((("ic", YR), ("is", YS))):
                    for k in range(2):
                        last = mm(ps[:, j // 2, (j % 2) * L:(j % 2 + 1) * L], src[:, k, j * P:(j + 1) * P], hcst(mat)[:, k], w == 0 and k == 0, w == 1 and k == 1)
                last.then_inc(sem("conv_mm"), 1)
            pe.wait_ge(sem("yh_ready"), 8)
            pe.wait_ge(sem("hyo_in"), 16)
            for j in range(KD):
                for k in range(KD):
                    last = mm(ps[:, 4 + j // 2, (j % 2) * L:(j % 2 + 1) * L], hyo[:, k, j * P:(j + 1) * P], zt[:, k], k == 0, k == KD - 1)
                last.then_inc(sem("mix_mm"), 1)
            moe_pe(1)

        @block.scalar
        def _(act):
            ch = Chain(act, sem("act_chain"), sem)

            def f(out, in_, func, **kw):
                return act.activation(out, in_, func, **kw)

            act.wait_ge(sem("small_in"), 32)
            ch.then(f(sc, col("c", 0, 16).rearrange("p (k m) -> p k m", m=2), ACT.Silu), "sc_ready")
            act.wait_ge(sem("s5p_in"), 16)
            ch.then(f(sm(0), s5("lst"), ACT.Exp), "s5_step")
            act.wait_ge(sem("s5_arg"), 1)
            ch(f(sm(4), sm(1), ACT.Exp))
            ch(f(sm(5), sm(2), ACT.Sin))
            ch.then(f(sm(6), sm(3), ACT.Sin), "s5_trig")
            for i in range(NADC):
                act.wait_ge(sem("ada_mm"), i + 1)
                if i >= 2:
                    act.wait_ge(sem("ada_turned"), i - 1)
                ch.then(f(adrow[:, i % 2], ps[0:2, i % 2, :], ACT.Copy), "adrow_ready")
                if i >= 1:
                    act.wait_ge(sem("ada_turned"), i)
                    ch.then(f(modc[:, 4 * (i - 1):4 * i].rearrange("p c m -> p (c m)"), ps[:, 2, 0:8], ACT.Copy), "modc_ready")
            act.wait_ge(sem("ada_turned"), NADC)
            ch.then(f(modc[:, 4 * (NADC - 1):4 * NADC].rearrange("p c m -> p (c m)"), ps[:, 2, 0:8], ACT.Copy), "modc_ready")
            for n in range(16):
                act.wait_ge(sem("bt_turned"), n + 1)
                q, r, hb = n // 4, n // 2 % 2, n % 2
                if n == 0:
                    act.wait_ge(sem("kk_ready"), 1)
                ch.then(f(bm[:, 8 * q + 4 * hb:8 * q + 4 * hb + 4, r], ps[:, n % 2, :].rearrange("p (t m) -> p t m", t=4), ACT.Copy), "bm_evicted")
            act.wait_ge(sem("x_in"), 16)
            act.wait_ge(sem("kscr_out"), 16)
            act.wait_ge(sem("ctx_in"), 16)
            ch.then(f(hT[:, :, 0:L], cx, ACT.Square), "squared")
            ch.then(f(hT[:, :, L:2 * L], xT, ACT.Square), "squared")

            def rms(bank, n, count, name, rows=P, width=D, out=None):
                act.wait_ge(sem(name), count)
                return f(out if out is not None else stx[:, 0:n], ps[0:rows, bank, 0:n], ACT.Sqrt, scale=1.0 / width, bias=at(r_eps, 1, rows))

            act.wait_ge(sem("eps_ready"), 1)
            ch.then(rms(7, 512, 1, "norm_mm"), "rms_ready")
            for i in range(4):
                act.wait_ge(sem("proj_mm"), 4 + i)
                ch.then(f(u_sb[:, i], ps[:, 3 + i, :].rearrange("p (c t) -> p t c", t=T5), ACT.Copy), "u_evicted")
            act.wait_ge(sem("kvl_evicted"), 3)
            ch.then(f(sql[:, 0], kvl, ACT.Square), "squared")
            ch.then(f(sql[:, 1], ql.rearrange("p k t -> p (k t)"), ACT.Square), "squared")
            act.wait_ge(sem("h_ready"), 1)
            ch.then(rms(7, 512, 1, "lat_mm", width=KVL), "lrms_ready")
            act.wait_ge(sem("kvl_normed"), 1)
            ch.then(rms(0, L, 2, "lat_mm", width=QL), "lrms_ready")
            for b in range(4):
                act.wait_ge(sem("head_mm"), b + 1)
                if b == 0:
                    act.wait_ge(sem("kvl_evicted"), 3)
                ch.then(f(qh[:, 2 * b:2 * b + 2].rearrange("p h t -> p (h t)"), ps[0:QKH, 3 + b, :], ACT.Copy), "qh_evicted")
            for t in range(4):
                act.wait_ge(sem("head_mm"), 12 + t + 1)
                ch.then(f(vt[:, t], ps[:, 3 + t, :], ACT.Copy), "vt_evicted")
            for b in range(8):
                act.wait_ge(sem("head_mm"), 16 + b + 1)
                r, g0 = b % 2, (b // 2) * 8
                src = ps[:, b, :].rearrange("p (g d c) -> p g d c", d=2, c=NCH)
                dst = est[:, :, r, g0:g0 + 8].rearrange("p s (g d) -> p g d s", d=2)
                ch(f(dst[:, :, 0], src[:, :, 0], ACT.Copy))
                ch(f(dst[:, :, 1, 0:XCH], src[:, :, 1, XCH - 1::-1], ACT.Copy))
                ch.then(f(dst[:, :, 1, XCH:NCH], src[:, :, 1, NCH - 1:XCH - 1:-1], ACT.Copy), "est_ready")
            act.wait_ge(sem("head_mm"), 16 + 8)
            ch.then(f(sqq, qh, ACT.Square), "squared")
            act.wait_ge(sem("kh_evicted"), 8)
            act.wait_ge(sem("kr_copied"), 1)
            ch.then(f(sqk, kh, ACT.Square), "squared")
            for b in range(4):
                act.wait_ge(sem("rot_mm"), b + 1)
                ch.then(f(sqq[:, 2 * b:2 * b + 2].rearrange("p h t -> p (h t)"), ps[0:QKH, b, :], ACT.Sqrt, scale=1.0 / QKH, bias=at(r_eps, 1, QKH)), "qrms")
            for h in range(HEADS):
                act.wait_ge(sem("rot_mm"), 4 + h + 1)
                ch.then(f(sqk[:, h], ps[0:QKH, 4 + h % 4, :], ACT.Sqrt, scale=1.0 / QKH, bias=at(r_eps, 1, QKH)), "krms")
            for n in range(2 * HEADS):
                act.wait_ge(sem("max_done"), n + 1)
                if n >= 2:
                    act.wait_ge(sem("pT_mm"), n - 1)
                ch.then(f(prob[:, n % 2], ps[:, n % 2, :], ACT.Exp, scale=QKH ** -0.5, bias=at(r_st + n, 1), accum_out=at(r_st + 16 + n, 1)), "exp_done")
                if n >= 1:
                    turned(act, f, ch, n - 1)
            turned(act, f, ch, 2 * HEADS - 1)
            act.wait_ge(sem("pv_mm"), HEADS)
            act.wait_ge(sem("yT_in"), 16 * 32)
            ch.then(f(zT.rearrange("p i (c t) -> p i t c", t=T5), yT, ACT.Gelu_apprx_tanh), "z_ready")
            for j in range(4):
                act.wait_ge(sem("glu_mm"), j // 2 * 2 + 2)
                ch.then(f(yT.rearrange("p i t c -> p i (t c)")[:, j], ps[:, 5 + j // 2, (j % 2) * L:(j % 2 + 1) * L], ACT.Sigmoid, bias=col("glub", j)), "glu_sig")

            def moe_act(li):
                act.wait_ge(sem("x_mixed"), li + 1)
                ch.then(f(sqX, xT, ACT.Square), "squared")
                ch.then(rms(6, L, 2 if li == 0 else 4, "norm_mm"), "rms_ready")
                act.wait_ge(sem("logits"), li + 1)
                ch.then(f(at(rtb + 2 * NE, 2 * NE), ps[:, 7, 0:2 * NE], ACT.Exp, scale=-1.0), "rexp")
                for n in range(4):
                    act.wait_ge(sem("hrow_mm"), 4 * li + n + 1)
                    ch.then(f(xg[:, n // 2, (n % 2) * 512:(n % 2 + 1) * 512], ps[:, 3 + n, :], ACT.Copy), "hrow_ready")

                def step(n, i):
                    def at_least(name, count, per=NB):
                        act.wait_ge(sem(name), li * per + count + 4 * i)
                    m = n + 1
                    if 2 <= m < NB:
                        at_least("tx_mm", m - 1, NE)
                        if n - 1 >= 2:
                            at_least("gu_mm", n)
                        f(xgT[:, m % 2, 0:4].rearrange("p k t -> p (k t)"), ps[:, 0, 0:4 * S], ACT.Copy).then_inc(sem("xt_act"), 1)
                    if n >= 1:
                        at_least("ht_mm", n)
                        if n >= 3:
                            at_least("dn_mm", n - 2)
                        q = rows_of(n - 1)
                        f(hT2[:, (n - 1) % 2, :, 0:q], ps[:, 4, 0:2 * q].rearrange("p (f t) -> p f t", f=2), ACT.Copy).then_inc(sem("hT_ready"), 1)
                    if n < NB:
                        at_least("gu_mm", n + 1)
                        if n >= 2:
                            at_least("h_done", n - 1)
                        q = rows_of(n)
                        f(sg[0:q, n % 2], ps[0:q, 2 + n % 2, 0:FF], ACT.Silu).then_inc(sem("sg_ready"), 1)
                    if n >= 1:
                        at_least("dn_mm", n)
                        if n >= 3:
                            act.wait_ge(sem(f"scat{(n - 1) % GD}"), 16 * (li * (NE // GD) + (n - 7) // GD + 1) + 16 * i)
                        dst = ysh[:, n - 1, 512:] if n <= 2 else yb[0:S, (n - 1) % GD, 512:]
                        f(dst, ps[0:rows_of(n - 1), 6, :], ACT.Copy).then_inc(sem("y_act"), 1)
                steady(step, act)

                def more(s, i):
                    act.wait_ge(sem(f"ov_p{li}"), i * 5 + 5 * NE * (s - 1) + 3)
                    f(sg[0:S, 0], ps[0:S, 2, 0:FF], ACT.Silu).then_inc(sem(f"ov_a{li}"), 1)
                overflow(li, act, more)

            moe_act(0)
            for i in range(2):
                act.wait_ge(sem("hid_arg"), i + 1)
                ch.then(f(hid[:, i], at(hsc, L, FH), ACT.Sin), "hid_ready")
            act.wait_ge(sem("hf_ready"), 8)
            ch.then(f(tiles(ff0, 4, HYW), hf, ACT.Square), "squared")
            act.wait_ge(sem("filter_mm"), 10 + 1)
            ch.then(f(hns, ps[:, 0, 0:8], ACT.Sqrt, bias=at(r_eps, 1)), "hn_read")
            for n in range(8):
                act.wait_ge(sem("filter_mm"), 11 + n + 1)
                dst = (HR if n < 4 else HS)[:, n // 2 % 2, (n % 2) * 512:(n % 2 + 1) * 512]
                ch.then(f(dst, ps[:, n, :], ACT.Copy), "H_evicted")
            ch.then(f(sqX, xT, ACT.Square), "squared")
            ch.then(rms(6, L, 3, "norm_mm"), "rms_ready")
            for i in range(6):
                act.wait_ge(sem("hy_proj"), i + 1)
                if i >= 2:
                    act.wait_ge(sem("conv_done"), i - 1)
                for hb in range(2):
                    ins = f(pp[:, i % 2, 2 * hb:2 * hb + 2].rearrange("p i t -> p (i t)"), ps[:, 2 * (i % 2) + hb, :], ACT.Copy)
                    if hb == 0:
                        ch(ins)
                    else:
                        ch.then(ins, "hyp_evicted")
            for n in range(4):
                act.wait_ge(sem("zs_mm"), n + 1)
                ch.then(f(zs[:, n // 2, (n % 2) * 512:(n % 2 + 1) * 512], ps[:, 4 + n, :], ACT.Copy), "zs_ready")
            moe_act(1)

        @block.vector
        def _(dve):
            ch = Chain(dve, sem("dve_chain"), sem)
            tt, ts, stt = dve.tensor_tensor, dve.tensor_scalar, dve.scalar_tensor_tensor
            M, AD, SU = ALU.mult, ALU.add, ALU.subtract
            ch.then(dve.memset(at(r_eps, 1), EPS), "eps_ready")
            ch(dve.memset(bdr.rearrange("p t m -> p (t m)"), 0.0))
            ch(dve.memset(bdi.rearrange("p t m -> p (t m)"), 0.0))
            dve.wait_ge(sem("s5_step"), 1)

            def cmul(o, a, b, t):
                ch(tt(t, a[1], b[1], M))
                ch(tt(o[0], a[0], b[0], M))
                ch(tt(o[0], o[0], t, SU))
                ch(tt(t, a[1], b[0], M))
                ch(tt(o[1], a[0], b[1], M))
                ch(tt(o[1], o[1], t, AD))

            def reduced(out, x, t, quarter):
                ch(ts(t, x, 1.0 / TWO_PI, 0.25 * quarter, M, AD))
                ch(ts(t, t, ROUND, None, AD))
                ch(ts(t, t, ROUND, None, SU))
                ch(stt(out, t, -PI_HI, x, M, AD))
                ch(stt(out, t, -PI_LO, out, M, AD))
                if quarter:
                    ch(ts(out, out, quarter * math.pi / 2, None, AD))
                ch(ts(out, out, PI_SAFE, -PI_SAFE, ALU.min, ALU.max))

            ch(ts(sm(7), s5("lre"), -1e-4, None, ALU.min))
            ch(tt(sm(1), sm(7), sm(0), M))
            ch(tt(sm(8), s5("lim"), sm(0), M))
            reduced(sm(2), sm(8), sm(9), 0)
            ch(ts(sm(10), sm(8), 0.0, None, AD))
            reduced(sm(3), sm(10), sm(9), 1)
            ch.then(ts(sm(9), sm(9), 0.0, None, M), "s5_arg")
            dve.wait_ge(sem("s5_trig"), 1)
            ch(dve.memset(pw[:, 0, 0], 1.0))
            ch(dve.memset(pw[:, 1, 0], 0.0))
            ch(tt(pw[:, 0, 1], sm(4), sm(6), M))
            ch(tt(pw[:, 1, 1], sm(4), sm(5), M))

            def p_(a, b):
                return pw[:, 0, a:b], pw[:, 1, a:b]

            def pb(a, n):
                return tuple(pw[:, r, a:a + 1].broadcast_to([P, n, NT5]) for r in range(2))
            tq = at(r10 + NT5 * 11, 4 * NT5).rearrange("p (j t) -> p j t", j=4)
            cmul(p_(2, 3), p_(1, 2), p_(1, 2), tq[:, 0:1])
            cmul(p_(3, 5), p_(1, 3), pb(2, 2), tq[:, 0:2])
            cmul(p_(5, 9), p_(1, 5), pb(4, 4), tq)
            A8, B8 = tiles(tmp5, 2, NT5), tiles(tmp5 + 64, 2, NT5)
            ch(dve.tensor_copy(A8[:, 0], pw[:, 0, 8]))
            ch(dve.tensor_copy(A8[:, 1], pw[:, 0, 8]))
            ch(ts(B8[:, 0], pw[:, 1, 8], -1.0, None, M))
            ch.then(dve.tensor_copy(B8[:, 1], pw[:, 1, 8]), "lam8_ready")
            ch(tt(sm(15), sm(7), sm(7), M))
            ch(tt(sm(16), s5("lim"), s5("lim"), M))
            ch(tt(sm(15), sm(15), sm(16), AD))
            ch(dve.reciprocal(sm(16), sm(15)))
            ch(ts(sm(17), pw[:, 0, 1], -1.0, None, AD))
            ch(tt(sm(18), sm(7), sm(16), M))
            ch(tt(sm(19), s5("lim"), sm(16), M))
            ch(ts(sm(19), sm(19), -1.0, None, M))
            cmul((sm(20), sm(21)), (sm(17), pw[:, 1, 1]), (sm(18), sm(19)), sm(22))

            def over(v):
                return v.rearrange("p (t c) -> p t c", c=1).broadcast_to([P, NT5, C5])
            tb = big[:, 0:512].rearrange("p (t c) -> p t c", c=C5)
            cmul((fb[:, 0], fb[:, 1]), (s5("br"), s5("bi")), (over(sm(20)), over(sm(21))), tb)
            for g2 in range(2):
                rows = slice(g2 * N5, (g2 + 1) * N5)
                ch(dve.tensor_copy(bdr[rows, :, g2 * C5:(g2 + 1) * C5], fb[rows, 0]))
                ch(dve.tensor_copy(bdi[rows, :, g2 * C5:(g2 + 1) * C5], fb[rows, 1]))
            cr_, ci_ = (s5(n).rearrange("p (g d) c -> p g d c", d=2) for n in ("cr", "ci"))
            for d in range(2):
                def lam(r):
                    v = pw[:, r, :].rearrange("p j (g d) -> p g d j", d=2)[:, :, d]
                    v = v if d == 0 else v[:, :, ::-1]
                    return v

                for g0 in range(0, GP, 8):
                    gs = slice(g0, g0 + 8)

                    def C(v):
                        return v[:, gs, d].unsqueeze(2).broadcast_to([P, 8, 9, C5])

                    def W(r):
                        return lam(r)[:, gs].unsqueeze(3).broadcast_to([P, 8, 9, C5])
                    t = big[:, 0:8 * 144].rearrange("p (g j c) -> p g j c", g=8, j=9)
                    o, q = ctr[:, gs, d], ctn[:, gs, d]
                    ch(tt(t, C(ci_), W(1), M))
                    ch(tt(o, C(cr_), W(0), M))
                    ch(tt(o, o, t, SU))
                    ch(tt(t, C(cr_), W(1), M))
                    ch(tt(q, C(ci_), W(0), M))
                    ch(stt(q.rearrange("p g j c -> p g (j c)"), q.rearrange("p g j c -> p g (j c)"), -1.0,
                           t.rearrange("p g j c -> p g (j c)"), M, SU))
            ch.then(ts(sm(23), sm(22), 0.0, None, M), "ctab_ready")
            ch.then(ts(sm(23), sm(22), 0.0, None, M), "s5_params_used")
            for half in range(2):
                dve.wait_ge(sem("kk_mm"), half + 1)
                for b in range(4):
                    src = ps[0:2 * C5, 3 + b, :].rearrange("p (g d j c) -> p g d j c", d=2, j=T5, c=C5)
                    gs = slice(8 * half + 2 * b, 8 * half + 2 * b + 2)
                    ch(dve.tensor_copy(kk[:, gs, 0:7], src[:, :, 1, 0:7]))
                    ch(dve.tensor_copy(kk[:, gs, 7], src[:, :, 1, 7]))
                    ch(tt(kk[:, gs, 7], kk[:, gs, 7], src[:, :, 0, 0], AD))
                    ins = dve.tensor_copy(kk[:, gs, 8:15], src[:, :, 0, 1:8])
                    if half == 0 and b == 3:
                        ch.then(ins, "kk_half")
                    else:
                        ch(ins)
            ch.then(dve.memset(sm(23), 0.0), "bd_used")
            td = big[0:32, 0:GP * C5].rearrange("p (g c) -> p g c", c=C5)
            ch(tt(td, col("s5d", 0, GP, 32).unsqueeze(2).broadcast_to([32, GP, C5]),
                  cst("eye16", 32).unsqueeze(1).broadcast_to([32, GP, C5]), M))
            ch.then(tt(kk[:, :, 7], kk[:, :, 7], td, AD), "kk_ready")
            for q in range(4):
                if q >= 2:
                    dve.wait_ge(sem("bt_turned"), 4 * (q - 1))
                for d in range(2):
                    gs = slice(4 * q, 4 * q + 4)

                    def B(r):
                        return fb[:, r].rearrange("p (g d) c -> p g d c", d=2)[:, gs, d].unsqueeze(2).broadcast_to([P, 4, T5, C5])

                    def W(r):
                        v = pw[:, r, 0:8].rearrange("p j (g d) -> p g d j", d=2)[:, gs, d]
                        v = v[:, :, ::-1] if d == 0 else v
                        return v.unsqueeze(3).broadcast_to([P, 4, T5, C5])
                    o = [bt[:, q % 2, r].rearrange("p (g d) (j c) -> p g d j c", d=2, c=C5)[:, :, d] for r in range(2)]
                    t = at(r11, 4 * TW).rearrange("p (g j c) -> p g j c", g=4, c=C5)
                    ch(tt(t, B(1), W(1), M))
                    ch(tt(o[0], B(0), W(0), M))
                    ch(tt(o[0], o[0], t, SU))
                    ch(tt(t, B(1), W(0), M))
                    ch(tt(o[1], B(0), W(1), M))
                    ins = tt(o[1], o[1], t, AD)
                    if d == 1:
                        if q == 0:
                            ch(ins)
                            ins = ts(sm(23), sm(22), 0.0, None, M)
                        ch.then(ins, "bt_ready")
                    else:
                        ch(ins)
            dve.wait_ge(sem("modc_ready"), NADC)
            ch(tt(modc, modc, col("ada_b", 0, 192).rearrange("p (c m) -> p c m", m=2), AD))
            for j in (1, 4):
                ch(ts(mod[:, :, j], mod[:, :, j], 1.0, None, AD))

            rms_n = [0]

            def inv_rms(n):
                rms_n[0] += 1
                dve.wait_ge(sem("rms_ready"), rms_n[0])
                ch(dve.reciprocal(rsx[:, 0:n], stx[:, 0:n]))

            def scaled(dst, src, r, li, m, jsh):
                ch(tt(dst, src, r.unsqueeze(1).broadcast_to([P, KD, L]), M))
                for k in range(KD):
                    ch(ts(dst[:, k], dst[:, k], scol(li, jsh + 1, k, m), scol(li, jsh, k, m), M, AD))
            inv_rms(512)
            scaled(hT[:, :, 0:L], cx, rsx[:, 0:L], 0, 1, 0)
            scaled(hT[:, :, L:2 * L], xT, rsx[:, L:2 * L], 0, 0, 0)
            ch.then(ts(sm(23), sm(22), 0.0, None, M), "h_ready")
            dve.wait_ge(sem("proj_mm"), 7)
            ch.then(dve.tensor_copy(kvl, ps[:, 0, :]), "kvl_evicted")
            ch.then(dve.tensor_copy(krl, ps[0:QKH, 1, :]), "kvl_evicted")
            ch.then(dve.tensor_copy(ql.rearrange("p k t -> p (k t)"), ps[:, 2, :]), "kvl_evicted")
            dve.wait_ge(sem("lrms_ready"), 1)
            ch(dve.reciprocal(rsx, stx))
            ch.then(stt(kvl, kvl, col("kvn"), rsx, M, M), "kvl_normed")
            dve.wait_ge(sem("lrms_ready"), 2)
            ch(dve.reciprocal(rsx[:, 0:L], stx[:, 0:L]))
            ch(stt(ql[:, 0], ql[:, 0], col("qn", 0), rsx[:, 0:L], M, M))
            ch.then(stt(ql[:, 1], ql[:, 1], col("qn", 1), rsx[:, 0:L], M, M), "ql_normed")
            kbank = (0, 1, 2, 7)
            for h in range(HEADS):
                dve.wait_ge(sem("head_mm"), 4 + h + 1)
                ch.then(dve.tensor_copy(kh[0:NOPE, h], ps[0:NOPE, kbank[h % 4], :]), "kh_evicted")
            ch.then(dve.tensor_copy(kh[NOPE:QKH], krl[NOPE:QKH].unsqueeze(1).broadcast_to([ROPE, HEADS, 2 * L])), "kr_copied")
            dve.wait_ge(sem("qrms"), 4)
            ch(dve.reciprocal(sqq, sqq))
            ch.then(stt(qh.rearrange("p h t -> p (h t)"), qh.rearrange("p h t -> p (h t)"), col("qqk", rows=QKH), sqq.rearrange("p h t -> p (h t)"), M, M), "qh_normed")
            dve.wait_ge(sem("krms"), 8)
            ch(dve.reciprocal(sqk, sqk))
            ch.then(stt(kh.rearrange("p h t -> p (h t)"), kh.rearrange("p h t -> p (h t)"), col("kqk", rows=QKH), sqk.rearrange("p h t -> p (h t)"), M, M), "kh_normed")
            for count, b0, v in ((16, 0, qh), (20, 4, kh[:, :, L:2 * L])):
                dve.wait_ge(sem("rot_mm"), count)
                tmp = sqk[:, 0:4].rearrange("p h t -> p (h t)").rearrange("p (h t) -> p h t", t=L)
                ch(tt(tmp, ps[0:QKH, b0:b0 + 4, :].rearrange("p b (h t) -> p (b h) t", h=2),
                      cst("sin", QKH).unsqueeze(1).broadcast_to([QKH, HEADS, L]), M))
                ch(tt(v, v, cst("cos", QKH).unsqueeze(1).broadcast_to([QKH, HEADS, L]), M))
                ch.then(tt(v, v, tmp, AD), "rope_done")
            for n in range(2 * HEADS + 1):
                if n < 2 * HEADS:
                    dve.wait_ge(sem("scores_done"), n + 1)
                    ch(dve.tensor_reduce(at(r_st + 32, 1), ps[:, n % 2, :], AX.X, ALU.max))
                    ch.then(ts(at(r_st + n, 1), at(r_st + 32, 1), -QKH ** -0.5, None, M), "max_done")
                if n >= 1:
                    k = n - 1
                    dve.wait_ge(sem("exp_done"), k + 1)
                    ch(dve.reciprocal(at(r_st + 33, 1), at(r_st + 16 + k, 1)))
                    ch.then(ts(prob[:, k % 2], prob[:, k % 2], at(r_st + 33, 1), None, M), "prob_ready")
                if n >= 3 and n % 2 == 1:
                    attend_out(dve, ch, (n - 3) // 2)
            attend_out(dve, ch, HEADS - 1)
            dve.wait_ge(sem("y_mm"), 1)
            for b in range(2):
                ch.then(dve.tensor_copy(ysb.rearrange("p (g b) c -> p g b c", b=2)[:, :, b], ps[:, 5 + b, :].rearrange("p (g c) -> p g c", c=XCH)), "y_evicted")
            for j in range(4):
                dve.wait_ge(sem("glu_sig"), j + 1)
                if j == 0:
                    dve.wait_ge(sem("glu_mm"), 4)
                ch.then(tt(zT[:, j], zT[:, j], yT.rearrange("p i t c -> p i (t c)")[:, j], M), "s5_out")
            for j in range(KD):
                dve.wait_ge(sem("mix_mm"), j // 2 * 2 + 2)
                ins = stt(xT[:, j], ps[:, j // 2, (j % 2) * L:(j % 2 + 1) * L], scol(0, 2, j), xT[:, j], M, AD)
                ch(ins) if j < KD - 1 else ch.then(ins, "x_mixed")

            def moe_dve(li):
                inv_rms(L)
                scaled(hX, xT, rsx[:, 0:L], li, 0, 3)
                ch.then(ts(at(rtb + 23 * 64, 1), at(r_eps, 1), 0.0, None, M), "moe_h")
                dve.wait_ge(sem("rexp"), li + 1)
                dve.wait_ge(sem("rw_in"), 48 * (li + 1))

                def T(i, n=1):
                    return at(rtb + NE * i, NE * n)
                ch(ts(T(2, 2), T(2, 2), 1.0, None, AD))
                ch(dve.reciprocal(T(2, 2), T(2, 2)))
                for t in range(2):
                    s_, b_, top, eq, cum = T(2 + t), T(4), at(rtb + NE * 5, 8), T(7), T(8)
                    gt, w_ = T(10 + t), T(12 + t)
                    need = at(rtb + NE * 9, 1)
                    ch(tt(b_, s_, T(0), AD))
                    ch(dve.max(top, b_))
                    ch(ts(gt, b_, top[:, TOPK - 1:TOPK], None, ALU.is_gt))
                    ch(ts(eq, b_, top[:, TOPK - 1:TOPK], None, ALU.is_equal))
                    ch(dve.tensor_reduce(need, gt, AX.X, AD))
                    ch(ts(need, need, -1.0, float(TOPK), M, AD))
                    ch(dve.tensor_tensor_scan(cum, eq, eq, 0.0, AD, ALU.bypass))
                    ch(ts(cum, cum, need, None, ALU.is_le))
                    ch(tt(eq, eq, cum, M))
                    ch.then(tt(gt, gt, eq, AD), "route")
                    ch(tt(w_, gt, s_, M))
                    ch(dve.tensor_reduce(need, w_, AX.X, AD))
                    ch(dve.reciprocal(need, need))
                    ch(ts(rt[:, t, :, 1], w_, need, ROUTE_SCALE, M, M))
                    ch(ts(rt[:, t, :, 0], gt, 0.0, mcst("tok", t, 1), M, AD))
                    ch(dve.tensor_tensor_scan(cum, gt, gt, 0.0, AD, ALU.bypass))
                    ch(tt(cum, cum, gt, SU))
                    ch(ts(rt[:, t, :, 2], cum, mcst("row", t, 1), None, AD))
                dve.wait_ge(sem("pos_mm"), li + 1)
                for t in range(2):
                    ch(stt(pos[:, t], ps[:, 7, t * NE:(t + 1) * NE], 1.0, T(10 + t), AD, M))
                    ch(ts(pos[:, t], pos[:, t], -1.0, None, AD))
                ch(dve.tensor_reduce(at(rtb + NE * 9, 1), ps[:, 7, 2 * NE:3 * NE], AX.X, ALU.max))
                ch(dve.tensor_copy(flags[:, li:li + 1], at(rtb + NE * 9, 1, 1)))

                def one_hot(out, slots, e):
                    return tt(out, slots.unsqueeze(1).broadcast_to([P, 2, S]), pos[:, :, bass.ds(e, 1)].broadcast_to([P, 2, S]), ALU.is_equal)

                for b in range(2):
                    one_hot(sel[:, b], mcst("iota"), b).then_inc(sem("sel_ready"), 1)
                with dve.Fori(1, NE // 2) as i:
                    for b in range(2):
                        dve.wait_ge(sem("tab_mm"), i * 2 + (li * NE + b - 1))
                        one_hot(sel[:, b], mcst("iota"), i * 2 + b).then_inc(sem("sel_ready"), 1)
                dve.wait_ge(sem("tab_mm"), NE * (li + 1))

                def indices(gidx, sidx, weight, src, empty, step_):
                    step_(ts(empty, src[:, :, 0], 0.0, mcst("beyond")[0:S], ALU.is_equal, M))
                    step_(tt(empty, empty, src[:, :, 0], AD))
                    step_(ts(gidx, empty, -1.0, None, AD))
                    step_(ts(empty, src[:, :, 2], 0.0, mcst("beyond")[0:S], ALU.is_equal, M))
                    step_(tt(empty, empty, src[:, :, 2], AD))
                    step_(ts(sidx, empty, -1.0, None, AD))
                    step_(dve.tensor_copy(weight, src[:, :, 1]))
                indices(idx[:, 0], idx[:, 1], wtab, ps[0:S, 7, 0:3 * NE].rearrange("p (e c) -> p e c", c=3), T(14)[0:S], ch)
                ch.then(dve.memset(T(15), 0.0), "idx_ready")

                def step(n, i):
                    def at_least(name, count, per=NB):
                        dve.wait_ge(sem(name), li * per + count + 4 * i)
                    m = n + 1
                    if 2 <= m < NB:
                        at_least("tx_mm", m - 1, NE)
                        if n - 1 >= 2:
                            at_least("gu_mm", n)
                        dve.tensor_copy(xgT[:, m % 2, 4:8].rearrange("p k t -> p (k t)"), ps[:, 1, 0:4 * S]).then_inc(sem("xt_dve"), 1)
                    if n < NB:
                        at_least("sg_ready", n + 1)
                        if n >= 2:
                            at_least("ht_mm", n - 1)
                        if n < 2:
                            ins = tt(hh[:, n % 2], sg[:, n % 2], ps[:, 2 + n % 2, FF:2 * FF], M)
                        else:
                            ins = stt(hh[0:S, n % 2], sg[0:S, n % 2], wtab[:, bass.ds(n - 2 + 4 * i, 1)], ps[0:S, 2 + n % 2, FF:2 * FF], M, M)
                        ins.then_inc(sem("h_done"), 1)
                    if n >= 1:
                        at_least("dn_mm", n)
                        if n >= 3:
                            dve.wait_ge(sem(f"scat{(n - 1) % GD}"), 16 * (li * (NE // GD) + (n - 7) // GD + 1) + 16 * i)
                        dst = ysh[:, n - 1, 0:512] if n <= 2 else yb[0:S, (n - 1) % GD, 0:512]
                        dve.tensor_copy(dst, ps[0:rows_of(n - 1), 5, :]).then_inc(sem("y_dve"), 1)
                steady(step, dve)
                for b in range(GD):
                    dve.wait_ge(sem(f"scat{b}"), 16 * (NE // GD) * (li + 1))
                def more(s, i):
                    ovd, ovp = sem(f"ov_d{li}"), sem(f"ov_p{li}")
                    base, own = NE * (s - 1), [0]

                    def oc(ins):
                        own[0] += 1
                        ins.then_inc(ovd, 1)
                        dve.wait_ge(ovd, i * OVD + OVD * base + own[0])
                    oc(one_hot(sel[:, 0], mcst("iota_more", (s - 1) * S, S), i))
                    oc(dve.tensor_copy(sel[:, 1, :, 0:3], rt[:, :, bass.ds(i, 1)].rearrange("p t e c -> p t (e c)")))
                    dve.wait_ge(ovp, i * 5 + 5 * base + 1)
                    indices(ib[:, 0:1], ib[:, GD:GD + 1], ov[:, 0:1], ps[0:S, 7, 0:3].rearrange("p (e c) -> p e c", c=3), ov[:, 1:2], oc)
                    oc(dve.memset(ov[:, 2:3], 0.0))
                    dve.wait_ge(ovp, i * 5 + 5 * base + 2)
                    oc(dve.tensor_copy(xgT[:, 0].rearrange("p (h k) t -> p h (k t)", h=2), ps[:, 0:2, 0:4 * S]))
                    dve.wait_ge(sem(f"ov_a{li}"), i + base + 1)
                    oc(stt(hh[0:S, 0], sg[0:S, 0], ov[:, 0:1], ps[0:S, 2, FF:2 * FF], M, M))
                    dve.wait_ge(ovp, i * 5 + 5 * base + 4)
                    oc(dve.tensor_copy(hT2[:, 0, :, 0:S], ps[:, 4, 0:2 * S].rearrange("p (f t) -> p f t", f=2)))
                    dve.wait_ge(ovp, i * 5 + 5 * base + 5)
                    oc(dve.tensor_copy(yb[0:S, 0], ps[0:S, 5:7, :].rearrange("p b n -> p (b n)")))
                    oc(dve.memset(ov[:, 2:3], 0.0))
                    dve.wait_ge(sem(f"ov_q{li}"), i * 32 + 32 * (base + 1))
                overflow(li, dve, more)
                dve.wait_ge(sem("rows_in"), 32 * (li + 1))
                for k in range(RPT):
                    ins = tt(xg[:, 0], ysh[:, 0] if k == 0 else xg[:, 0], wring[:, 0, k * D:(k + 1) * D], AD)
                    ch(ins) if k < RPT - 1 else ch.then(ins, "sum_dve")
                dve.wait_ge(sem("out_mm"), 2 * (li + 1))
                for j in range(KD):
                    ins = stt(xT[:, j], ps[:, j // 2, (j % 2) * L:(j % 2 + 1) * L], scol(li, 5, j), xT[:, j], M, AD)
                    ch(ins) if j < KD - 1 else ch.then(ins, "moe_x")

            moe_dve(0)
            for i in range(2):
                dve.wait_ge(sem("filter_mm"), i + 1)
                if i == 1:
                    dve.wait_ge(sem("hid_ready"), 1)
                a, t = at(hsc + L, L, FH), at(hsc + 2 * L, L, FH)
                ch(ts(a, ps[0:FH, 4 + i, 0:L], col("fb1" if i == 0 else "fb2", rows=FH), col("freq", rows=FH), AD, M))
                reduced(at(hsc, L, FH), a, t, 0)
                ch.then(ts(t, t, 0.0, None, M), "hid_arg")
            for n in range(8):
                t, j = n // 4, n % 4
                dve.wait_ge(sem("filter_mm"), 2 + n + 1)
                ch.then(tt(hf[:, 2 * (j // 2) + t, (j % 2) * 512:(j % 2 + 1) * 512], ps[:, n, :],
                             hcst("decay")[:, t, (j % 2) * 512:(j % 2 + 1) * 512], M), "hf_ready")
            dve.wait_ge(sem("squared"), 7 + 1)
            dve.wait_ge(sem("filter_mm"), 10 + 1)
            hd = tiles(ff0, 2, HYW)
            ch(tt(hd, hf[:, 0:2], hf[:, 2:4], SU))
            ch(tt(hf[:, 0:2], hf[:, 0:2], hf[:, 2:4], AD))
            ch.then(dve.tensor_copy(hf[:, 2:4], hd), "hf_comb")
            dve.wait_ge(sem("hn_read"), 1)
            ch(dve.reciprocal(hns, hns))
            inv_rms(L)
            scaled(hX, xT, rsx[:, 0:L], 1, 0, 0)
            ch.then(ts(at(hsc, 1), at(r_eps, 1), 0.0, None, M), "hy_h")
            for i in range(6):
                dve.wait_ge(sem("hyp_evicted"), i + 1)
                for j in range(4):
                    c = 4 * i + j
                    p_in, o = pp[:, i % 2, j], xc[:, c]
                    ch(ts(o, p_in, col("convw", 24 + c), col("convb", c), M, AD))
                    ch(stt(o[:, 1:L], p_in[:, 0:L - 1], col("convw", c), o[:, 1:L], M, AD))
                    ins = stt(o[:, 0:L - 1], p_in[:, 1:L], col("convw", 48 + c), o[:, 0:L - 1], M, AD)
                    ch(ins) if j < 3 else ch.then(ins, "conv_done")
            ch.then(tt(zt, xc[:, 8:16], xc[:, 16:24], M), "z_conv")
            dve.wait_ge(sem("Z_mm"), 8)
            ZR = ps[:, 0:4, :].rearrange("p (m c) n -> p m (c n)", m=2)
            ZS = ps[:, 4:8, :].rearrange("p (m c) n -> p m (c n)", m=2)
            ch(tt(YR, ZR, HR, M))
            ch(tt(ytmp, ZS, HS, M))
            ch(tt(YR, YR, ytmp, SU))
            ch(tt(YS, ZR, HS, M))
            ch(tt(ytmp, ZS, HR, M))
            ch.then(tt(YS, YS, ytmp, AD), "Y_ready")
            for j in range(KD):
                dve.wait_ge(sem("conv_mm"), j // 2 * 2 + 2)
                ch(ts(zt[:, j], zt[:, j], col("hybias", j), None, M))
                ch(stt(zt[:, j], ps[:, j // 2, (j % 2) * L:(j % 2 + 1) * L], hns[:, j:j + 1], zt[:, j], M, AD))
                ch.then(tt(zt[:, j], zt[:, j], xc[:, j], M), "yh_ready")
            for j in range(KD):
                dve.wait_ge(sem("mix_mm"), 8 + j // 2 * 2 + 2)
                ins = stt(xT[:, j], ps[:, 4 + j // 2, (j % 2) * L:(j % 2 + 1) * L], scol(1, 2, j), xT[:, j], M, AD)
                ch(ins) if j < KD - 1 else ch.then(ins, "x_mixed")
            moe_dve(1)


def tiles_of(w):
    k, n = w.shape
    return np.ascontiguousarray(w.reshape(k // P, P, n).transpose(1, 0, 2))


def columns(v):
    return v.reshape(-1, P).T


def constants():
    c = np.zeros((P, NCST), np.float32)

    def put(name, v):
        a, w = CST[name]
        c[:v.shape[0], a:a + w] = v
    put("ident", np.eye(P, dtype=np.float32))
    t = np.arange(L)
    nf = ROPE // 4
    inv = (10000.0 ** (-np.arange(nf, dtype=np.float32) / nf)).astype(np.float32)
    ang = np.concatenate([(t // 64).astype(np.float32)[:, None] * inv, (t % 64).astype(np.float32)[:, None] * inv], -1).T
    cos, sin = np.ones((QKH, L), np.float32), np.zeros((QKH, L), np.float32)
    cos[NOPE:] = np.repeat(np.cos(ang), 2, 0)
    sin[NOPE:] = np.repeat(np.sin(ang), 2, 0)
    swap = np.zeros((QKH, QKH), np.float32)
    for i in range(NOPE, QKH, 2):
        swap[i + 1, i] = -1.0
        swap[i, i + 1] = 1.0
    put("cos", cos)
    put("sin", sin)
    put("swap", swap)
    put("eye16", np.tile(np.eye(C5, dtype=np.float32), (2, 1)))
    return c


def hyena_constants():
    c = np.zeros((P, NHCST), np.float32)

    def put(name, v):
        a, w = HCST[name]
        c[:v.shape[0], a:a + w] = v.reshape(v.shape[0], -1)
    n, k = np.arange(L, dtype=np.float64), np.arange(L) + 0.5
    w = 2 * np.pi / (2 * L) * np.outer(n, k)
    C, S = np.cos(w).astype(np.float32), np.sin(w).astype(np.float32)
    put("fc", tiles_of(C))
    put("fs", tiles_of(S))
    put("ic", tiles_of(np.ascontiguousarray(C.T) / np.float32(L)))
    put("is", tiles_of(np.ascontiguousarray(S.T) / np.float32(L)))
    t = np.linspace(0.0, 1.0, L, dtype=np.float32)[:, None]
    deltas = np.linspace(-math.log(1e-2) / 1.5, -math.log(1e-2) / 0.3, HYW, dtype=np.float32)
    put("decay", tiles_of(np.exp(-t * deltas).astype(np.float32)))
    ang = (2.0 * math.pi * np.arange(L, dtype=np.float32)[:, None] / L).astype(np.float32)
    bands = np.linspace(1e-4, (FE - 1) // 2 - 1, (FE - 1) // 2, dtype=np.float32)
    z = np.concatenate([t, np.cos(bands * ang), -np.sin(bands * ang)], -1).astype(np.float32)
    put("zemb", np.ascontiguousarray(z.T))
    return c


def routing_constants():
    c = np.zeros((P, NMCST), np.float32)
    p = np.arange(P, dtype=np.float32)[:, None]
    for name, v in (("tri", np.triu(np.ones((P, P)), 1)), ("iota", p.T[:, :S]), ("iota_more", np.arange(S, L)[None]), ("tok", p + [1, 1 + P]),
                    ("row", p * RPT + [1, 1 + P * RPT]), ("beyond", p + 1e6)):
        a, w = MCST[name]
        c[:, a:a + w] = v
    return c


def laid_out(i):
    i = {k: np.asarray(v) for k, v in i.items()}
    cols = np.zeros((P, NCOLS), np.float32)

    def put(name, v, rows=P):
        a, w = COLS[name]
        cols[:rows, a:a + w] = v
    put("ada_b", np.repeat(i["ada_b"].reshape(96, P).T[:, :, None], 2, 2).reshape(P, 192))
    put("c", np.stack([columns(i["c"][0]), columns(i["c_ctx"])], 2).reshape(P, 16))
    put("qn", columns(i["mla_q_norm"][0]))
    put("kvn", columns(i["mla_kv_norm"][0]))
    put("qqk", i["mla_q_qknorm"][0][:, None], QKH)
    put("kqk", i["mla_k_qknorm"][0][:, None], QKH)
    put("glub", columns(i["s5_glu_b"][0]))
    put("convw", i["hy_conv_w"][0].reshape(3 * 24, P).T)
    put("convb", columns(i["hy_conv_b"][0]))
    put("hybias", columns(i["hy_bias"][0]))
    put("fb1", i["hy_f_b1"][0][:, None], FH)
    put("fb2", i["hy_f_b2"][0][:, None], FH)
    put("freq", i["hy_f_freq"][0][:, None], FH)
    put("s5d", i["s5_d"][0].reshape(GP, 2 * C5).T, 2 * C5)
    s5p = np.zeros((P, NS5P), np.float32)

    def put5(name, v):
        a, w = S5P[name]
        v = v.reshape((2, GP, 2, N5) + v.shape[3:])
        v = np.moveaxis(v, (2, 3, 1, 0), (0, 1, 2, 3))
        s5p[:, a:a + w] = v.reshape(P, w)
    put5("lre", i["s5_lam_re"][0])
    put5("lim", i["s5_lam_im"][0])
    put5("lst", np.broadcast_to(i["s5_log_step"][0][:, :, None], (2, G5, N5)))
    put5("br", i["s5_b_re"][0])
    put5("bi", i["s5_b_im"][0])
    put5("cr", i["s5_c_re"][0].transpose(0, 1, 3, 2))
    put5("ci", i["s5_c_im"][0].transpose(0, 1, 3, 2))

    def weights(gate, up, down):
        lead = gate.shape[:-2]
        g, u = (w.reshape(lead + (KD, P, FF)) for w in (gate, up))
        d = down.reshape(lead + (FF // P, P, D))
        n = len(lead)
        gu = np.concatenate([g, u], -1)
        return np.concatenate([np.moveaxis(w, n, n + 1).reshape(lead + (P, -1)) for w in (gu, d)], -1)
    return {
        "cols": cols, "s5p": s5p, "cst": constants(), "hcst": hyena_constants(), "mcst": routing_constants(),
        "ada_w": np.ascontiguousarray(i["ada_w"].reshape(2, KD, P, 12, ADC).transpose(0, 3, 2, 1, 4)).reshape(NADC, P, KD, ADC),
        "xT": tiles_of(np.ascontiguousarray(i["x"][0].T)), "ctxT": tiles_of(np.ascontiguousarray(i["ctx"][0].T)),
        "w_in": tiles_of(i["ev_w_in"][0]), "w_uq": tiles_of(i["mla_w_uq"][0]), "w_ukv": i["mla_w_ukv"][0],
        "glu_w": tiles_of(i["s5_glu_w"][0]), "ev_w_out": tiles_of(i["ev_w_out"][0]),
        "hy_w_in": np.ascontiguousarray(i["hy_w_in"][0].reshape(KD, P, 6, 512).transpose(2, 1, 0, 3)),
        "hy_w_out": tiles_of(i["hy_w_out"][0]), "f_w1": i["hy_f_w1"][0], "f_w2": i["hy_f_w2"][0], "f_w3": i["hy_f_w3"][0],
        "router_w": np.ascontiguousarray(i["moe_router_w"].reshape(2, KD, P, NE).transpose(0, 2, 1, 3)),
        "router_b": i["moe_router_b"],
        "w_experts": weights(i["moe_w_gate"], i["moe_w_up"], i["moe_w_down"]),
        "w_shared": weights(i["moe_sh_gate"], i["moe_sh_up"], i["moe_sh_down"]),
    }


def kernel(**inputs):
    import concourse.bacc as bacc
    from concourse.bass_utils import run_bass_kernel_spmd

    nc = bacc.Bacc("TRN2", target_bir_lowering=False, num_devices=1)
    arrays = {f"in_{k}": np.ascontiguousarray(v) for k, v in laid_out(inputs).items()}
    A = {k[3:]: nc.dram_tensor(k, v.shape, mybir.dt.from_np(v.dtype), kind="ExternalInput").ap() for k, v in arrays.items()}
    A["out"] = nc.dram_tensor("out_x", (P, KD, L), F32, kind="ExternalOutput").ap()
    program(nc, A)
    r = run_bass_kernel_spmd(nc, [arrays], core_ids=[0])
    y = r.results[0]["out_x"]
    return np.ascontiguousarray(y.transpose(2, 1, 0).reshape(1, L, D))
```

```python
import math
from contextlib import ExitStack

import numpy as np
import concourse.bass as bass
from concourse import mybir

F32 = mybir.dt.float32
U32 = mybir.dt.uint32
BF16 = mybir.dt.bfloat16
ALU = mybir.AluOpType
ACT = mybir.ActivationFunctionType
AX = mybir.AxisListType

P = 128
D = 1024
KD = D // P
L = 256
EPS = 1e-6
HEADS, NOPE, ROPE, VH = 8, 64, 32, 64
QKH = NOPE + ROPE
QL, KVL = 256, 128
G5, C5, N5 = 32, 16, 64
T5 = 8
NCH = 2 * L // T5
XCH = L // T5
NT5 = G5
GP = G5 // 2
TW = T5 * C5
UOFF = QL + KVL + ROPE
EVIN = UOFF + G5 * C5
NE, TOPK, FF = 64, 6, 256
ROUTE_SCALE = 2.5
HYW = 1024
FH, FE = 64, 33
RING = 4
S = 64
NB = 2 + NE
S5_AT = 10
KK_AT, BT_AT, SQUARES_AT, NORM_AT = (10, 12), (14, 16, 18, 20), 21, 22
SG = 8
GD = 4
OV_SEL, OV_INDEX, OV_TURNED, OV_HIDDEN, OV_HIDDEN_TURNED, OV_ROWS, OVD = 2, 9, 11, 12, 13, 14, 15
ROW_PARTS = (0, 4), (4, TOPK)
RPT = TOPK
WEXP = KD * FF * 2 + (FF // P) * D
ADC = 512
NADC = 2 * 6 * D // ADC
TWO_PI = 2.0 * math.pi
PI_HI = 6.28125
PI_LO = TWO_PI - PI_HI
ROUND = 12582912.0
PI_SAFE = 3.1415925


def offsets(widths):
    out, at = {}, 0
    for name, width in widths:
        out[name] = (at, width)
        at += width
    return out, at


COLS, NCOLS = offsets((("ada_b", 2 * 48 * 2), ("c", KD * 2), ("qn", 2), ("kvn", 1), ("qqk", 1), ("kqk", 1),
                       ("glub", 4), ("convw", 3 * 24), ("convb", 24), ("hybias", 8), ("fb1", 1), ("fb2", 1),
                       ("freq", 1), ("s5d", GP)))
S5P, NS5P = offsets((("lre", NT5), ("lim", NT5), ("lst", NT5), ("br", NT5 * C5), ("bi", NT5 * C5),
                     ("cr", NT5 * C5), ("ci", NT5 * C5)))
CST, NCST = offsets((("ident", P), ("cos", L), ("sin", L), ("swap", QKH), ("eye16", C5), ("pick", 2 * HEADS - 1)))
MCST, NMCST = offsets((("tri", P), ("iota", S), ("iota_more", L - S), ("tok", 2), ("row", 2), ("beyond", 1)))
HCST, NHCST = offsets((("fc", 2 * L), ("fs", 2 * L), ("ic", 2 * L), ("is", 2 * L), ("decay", 2 * HYW), ("zemb", L)))


class Chain:

    def __init__(self, eng, semaphore, sem):
        self.eng, self.own, self.sem, self.n, self.counts = eng, semaphore, sem, 0, {}

    def __call__(self, ins):
        self.n += 1
        ins.then_inc(self.own, 1)
        self.eng.wait_ge(self.own, self.n)

    def then(self, ins, name):
        self.counts[name] = self.counts.get(name, 0) + 1
        ins.then_inc(self.sem(name), 1)
        self.eng.wait_ge(self.sem(name), self.counts[name])


def program(nc, A):
    with ExitStack() as ctx:
        sems = {}

        def sem(name):
            if name not in sems:
                sems[name] = ctx.enter_context(nc.semaphore(name))
            return sems[name]

        NAR = 53120
        ar = ctx.enter_context(nc.sbuf_tensor("arena", [P, NAR], F32))
        ps = ctx.enter_context(nc.psum_tensor("ps", [P, 8, 512], F32))
        scr = {n: nc.dram_tensor(n, sh, F32, kind="Internal").ap()
               for n, sh in (("u_scr", [G5 * C5, T5, NCH]), ("k_scr", [2 * C5, GP, 15 * C5]),
                             ("h_scr", [L, D]), ("r_scr", [L * RPT, D]))}
        top = [0]

        def region(width):
            a = top[0]
            top[0] += width
            assert top[0] <= NAR, top
            return a

        def at(a, width, rows=P):
            return ar[0:rows, a:a + width]

        r_cst, r_cols, r_x, r_h = region(NCST), region(NCOLS), region(KD * L), region(2 * KD * L)
        r_mod, r_ones, r_row, r_sc = region(192), region(P), region(1024), region(16)
        r_eps, r_st, r_flag, r_pad = region(1), region(34), region(2), region(3)
        r_free = top[0]
        ident = at(r_cst, P)
        ones = at(r_ones, P)

        def cst(name, rows=P):
            a, w = CST[name]
            return at(r_cst + a, w, rows)

        def col(name, i=0, n=1, rows=P):
            return at(r_cols + COLS[name][0] + i, n, rows)

        def tiles(a, k, n, rows=P):
            return at(a, k * n, rows).rearrange("p (k t) -> p k t", k=k)

        xT = tiles(r_x, KD, L)
        hT = tiles(r_h, KD, 2 * L)
        hX = tiles(r_h, KD, L)
        sqX = tiles(r_h + KD * L, KD, L)
        mod = at(r_mod, 192).rearrange("p (l j k m) -> p l j k m", l=2, j=6, k=KD)
        modc = at(r_mod, 192).rearrange("p (c m) -> p c m", m=2)
        sc = at(r_sc, 16).rearrange("p (k m) -> p k m", m=2)
        adrow = at(r_row, 1024, 2).rearrange("p (b n) -> p b n", b=2)
        rkq = at(r_row, 3 * L, HEADS)
        rsx = at(r_row, 512)
        stx = at(r_row + 512, 512)

        r1 = region(8192)
        r2 = region(2 * NT5 * 144)
        r3 = region(8192)
        r4 = region(4096)
        r6 = region(35 * 64)
        r7 = region(4096)
        r8 = region(2560)
        r9 = region(NS5P)
        r10 = region(3000)

        adw = at(r1, 8192).rearrange("p (b k n) -> p b k n", b=2, k=KD)
        w_in = tiles(r1, KD, EVIN)
        kh = tiles(r1, HEADS, 2 * L, QKH)
        qh = tiles(r1 + 4096, HEADS, L, QKH)
        vt = tiles(r1 + 6144, 4, 512)
        glu_w = tiles(r1, 4, 512)
        ctr = at(r2, NT5 * 144).rearrange("p (g d j c) -> p g d j c", d=2, j=9, c=C5)
        ctn = at(r2 + NT5 * 144, NT5 * 144).rearrange("p (g d j c) -> p g d j c", d=2, j=9, c=C5)
        bm = at(r3, 8192).rearrange("p (t r m) -> p t r m", t=NT5, r=2)
        sqk = tiles(r3, HEADS, 2 * L, QKH)
        sqq = tiles(r3 + 4096, HEADS, L, QKH)
        w_out = tiles(r3, KD, D)
        toep = tiles(r4, G5, TW)
        st = at(r6, 35 * 64).rearrange("p (s r t) -> p s r t", r=2, t=NT5)
        bt = at(r7, 4096).rearrange("p (b r t m) -> p b r t m", b=2, r=2, t=8)
        U = tiles(r7, G5, NCH)
        u_sb = at(r7 + 2048, 2048).rearrange("p (i t c) -> p i t c", i=4, t=T5)
        prob = tiles(r7 + 2048, 2, 512)
        att = tiles(r7 + 3072, 4, L)
        ys = at(r_h, G5 * TW, XCH).rearrange("p (i t g c) -> p i t g c", i=4, t=T5, c=C5)
        w_uq = tiles(r8, 2, 768)
        w_ukv = at(r8 + 1536, 1024)
        cx = tiles(r9, KD, L)
        pT = at(r9, 2048).rearrange("p (b k t) -> p b k t", b=2, k=4)
        kvl, krl, ql = at(r9, 512), at(r9 + 512, 512, QKH), tiles(r9 + 1024, 2, L)
        kk = at(r_h, GP * 240, 2 * C5).rearrange("p (g j c) -> p g j c", j=15, c=C5)
        est = at(r_h, 4096).rearrange("p (s r t) -> p s r t", r=2, t=NT5)
        sql = tiles(r_h, 3, 512)
        stb = at(r10, XCH * NT5).rearrange("p (s r g) -> p s r g", r=2, g=GP)
        yT = at(r10 + 0, 1024).rearrange("p (i t c) -> p i t c", i=4, t=T5)
        zT = tiles(r10 + 1024, 4, L)

        def s5(name):
            a, w = S5P[name]
            v = at(r9 + a, w)
            return v if w == NT5 else v.rearrange("p (t c) -> p t c", c=C5)

        def sm(i, n=1):
            return at(r10 + NT5 * i, NT5 * n)
        pw = at(r10 + NT5 * 30, 18 * NT5).rearrange("p (r j t) -> p r j t", r=2, j=9)
        fb = at(r10 + NT5 * 48, 2 * NT5 * C5).rearrange("p (r t c) -> p r t c", r=2, c=C5)
        tmp5 = r10 + NT5 * 81
        bdr = at(r4, NT5 * 32).rearrange("p (t m) -> p t m", m=32)
        bdi = at(r4 + NT5 * 32, NT5 * 32).rearrange("p (t m) -> p t m", m=32)
        big = at(r3, 4096)
        r11 = region(4 * TW)
        rs0 = at(r11, 512)

        m1 = r_free
        m2 = m1 + RING * WEXP
        wring = at(m1, RING * WEXP).rearrange("p (b n) -> p b n", b=RING)
        xg = tiles(m2, GD, D)
        xgT = at(m2 + GD * D, 2 * KD * S).rearrange("p (b k t) -> p b k t", b=2, k=KD)
        m3 = m2 + GD * D + 2 * KD * S
        yb = tiles(m3, GD, D)
        ysh = tiles(m3 + GD * D, 2, D)
        m4 = m3 + (GD + 2) * D
        sg, hh = tiles(m4, 2, FF), tiles(m4 + 512, 2, FF)
        hT2 = at(m4 + 1024, 2 * FF).rearrange("p (b f t) -> p b f t", b=2, f=2)
        rw = tiles(m4 + 1536, KD, NE)
        r_mc = m4 + 2048
        r_sel = r_mc + NMCST
        selg = at(m3, 2 * SG * S).bitcast(BF16).rearrange("p (b t e s) -> p b t e s", b=2, t=2, e=SG)
        sel = at(r_sel, 4 * S).rearrange("p (b t s) -> p b t s", b=2, t=2)
        r_tab = r_sel + 4 * S
        pos = tiles(r_tab, 2, NE)
        rt = at(r_tab + 2 * NE, 6 * NE).rearrange("p (t e c) -> p t e c", t=2, c=3)
        wtab = at(r_tab + 8 * NE, NE, S)
        idx = at(r_tab + 9 * NE, 2 * NE, S).bitcast(U32).rearrange("p (c e) -> p c e", c=2)
        ib = at(r_tab + 11 * NE, 2 * GD, S).bitcast(U32)
        flags = at(r_flag, 2, 1).bitcast(U32)
        ov = at(r_tab + 11 * NE + 2 * GD + 8, 16, S)
        rtb = r_tab + 12 * NE
        assert rtb + 24 * NE <= NAR
        NR = 5
        rparts = at(rtb + 16 * NE, NE * NR).bitcast(BF16).rearrange("p (t e c) -> p t e c", t=2, c=NR)

        def mcst(name, i=0, n=None):
            a, w = MCST[name]
            return at(r_mc + a + i, w if n is None else n)

        def gate_up(slot, k):
            return wring[:, slot, k * 2 * FF:(k + 1) * 2 * FF]

        def w_down(slot, f, c):
            a = 2 * KD * FF + f * D + c * 512
            return wring[:, slot, a:a + 512]

        def slot_of(n):
            return 0 if n < 2 else (n - 1) % RING

        def rows_of(n):
            return P if n < 2 else S

        def steady(step, eng, rounds=(NB - 10) // 4):
            for n in range(7):
                step(n, 0)
            with eng.Fori(0, rounds) as i:
                for n in range(7, 11):
                    step(n, i)
            for n in range(7 + 4 * rounds, NB + 1):
                step(n, 0)

        def overflow(li, eng, body, last=None):
            r = eng.value_load(flags[:, li:li + 1], min_val=0, max_val=L)
            for s in range(1, L // S):
                with eng.If(r > s * S):
                    with eng.Fori(0, NE) as i:
                        body(s, i)
                    if last:
                        last(s)
                eng.nop()

        hyw = at(m1, 3 * 4096).rearrange("p (b k n) -> p b k n", b=3, k=KD)
        hyo = tiles(m1, KD, D)
        hc0 = m1 + 3 * 4096
        xc = tiles(hc0 + NHCST, 24, L)
        ff0 = hc0 + NHCST + 24 * L
        pp = at(ff0, 2 * 4 * L).rearrange("p (b i t) -> p b i t", b=2, i=4)
        zt = tiles(ff0 + 2048, KD, L)
        zs = tiles(ff0 + 4096, 2, HYW)
        hf = tiles(ff0 + 6144, 4, HYW)
        HR, HS = tiles(ff0 + 10240, 2, HYW), tiles(ff0 + 12288, 2, HYW)
        hsq = tiles(ff0 + 10240, 4, HYW)
        f_w3 = at(ff0 + 14336, 2048, FH)
        f_w1 = at(ff0 + 16384, FH, FE)
        f_w2 = at(ff0 + 16384 + FH, FH, FH)
        hid = tiles(ff0 + 16512, 2, L, FH)
        hsc = ff0 + 17024
        hns = at(hsc + 1024, 8)
        YR, YS = tiles(ff0 + 6144, 2, HYW), tiles(ff0 + 8192, 2, HYW)
        ytmp = tiles(ff0 + 4096, 2, HYW)
        assert hsc + 1040 <= NAR, hsc

        def hcst(name, k=2, rows=P):
            a, w = HCST[name]
            v = at(hc0 + a, w, rows)
            return v if k == 1 else v.rearrange("p (k t) -> p k t", k=k)

        def scol(li, j, k, m=0):
            return mod[:, li, j, k, m:m + 1]

        def ada_turn(pe, i):
            pe.wait_ge(sem("adrow_ready"), i + 1)
            if i >= 1:
                pe.wait_ge(sem("modc_ready"), i)
            for j in range(4):
                last = pe.matmul(ps[:, 2, 2 * j:2 * j + 2], adrow[:, i % 2, j * P:(j + 1) * P], ident[0:2, 0:2], start=True, stop=True)
            last.then_inc(sem("ada_turned"), 1)

        def turned(act, f, ch, n):
            h, t = n // 2, n % 2
            act.wait_ge(sem("pT_mm"), n + 1)
            if h >= 2:
                act.wait_ge(sem("pv_mm"), h - 1)
            ch.then(f(pT[:, h % 2, :, t * P:(t + 1) * P], ps[:, 2 + n % 2, :].rearrange("p (k q) -> p k q", k=4), ACT.Copy), "pT_ready")

        def attend_out(dve, ch, h):
            dve.wait_ge(sem("pv_mm"), h + 1)
            rows = slice((h % 2) * VH, (h % 2 + 1) * VH)
            ch.then(dve.tensor_copy(att[rows, h // 2], ps[rows, 4 if h % 2 == 0 else 7, 0:L]), "att_ready")

        block = ctx.enter_context(nc.Block())

        @block.sync
        def _(sp):
            def load(dst, src, name, n=16):
                sp.dma_start(dst, src).then_inc(sem(name), 16)

            load(at(r_cols, NCOLS), A["cols"], "small_in")
            load(at(r9, NS5P), A["s5p"], "s5p_in")
            load(at(r_cst, NCST), A["cst"], "small_in")
            load(w_uq, A["w_uq"], "uw_in")
            load(w_ukv, A["w_ukv"], "uw_in")
            for i in range(NADC):
                if i >= 2:
                    sp.wait_ge(sem("ada_mm"), i - 1)
                load(adw[:, i % 2], A["ada_w"][i], f"ada_in{i % 2}")
                if i == 13:
                    load(xT, A["xT"], "x_in")
                if i == 15:
                    sp.wait_ge(sem("s5_params_used"), 1)
                    load(cx, A["ctxT"], "ctx_in")
                if i == 17:
                    sp.wait_ge(sem("kk_ready"), 1)
                    load(scr["k_scr"], kk.rearrange("p g j c -> p g (j c)"), "kscr_out")
                if i == 18:
                    sp.wait_ge(sem("kscr_out"), 16)
                    sp.wait_ge(sem("bd_used"), 1)
                if 18 <= i < 22:
                    for t in range(2 * (i - 18), 2 * (i - 18) + 2):
                        for g2 in range(2):
                            load(toep[t * C5:(t + 1) * C5].rearrange("p (g b) m -> p g b m", b=2)[:, :, g2],
                                 scr["k_scr"][g2 * C5:(g2 + 1) * C5, :, (T5 - 1 - t) * C5:(2 * T5 - 1 - t) * C5], "toep_in")
            sp.wait_ge(sem("ada_mm"), NADC)
            load(w_in, A["w_in"], "win_in")
            sp.wait_ge(sem("u_evicted"), 4)
            load(scr["u_scr"].rearrange("(i p) t c -> p i (t c)", p=P), u_sb.rearrange("p i t c -> p i (t c)"), "uscr_out")
            sp.wait_ge(sem("uscr_out"), 16)
            for t in range(T5):
                load(U[t * C5:(t + 1) * C5], scr["u_scr"][:, t].rearrange("(g p) c -> p g c", p=C5), "U_in")
            sp.wait_ge(sem("rope_done"), 2)
            load(w_out, A["ev_w_out"], "wout_in")
            sp.wait_ge(sem("scores_done"), 2 * HEADS)
            load(glu_w, A["glu_w"], "glu_in")

            def moe_loads(li):
                sp.wait_ge(sem("x_mixed"), li + 1)
                load(rw, A["router_w"][li], "rw_in")
                load(at(rtb, NE), A["router_b"][li:li + 1].broadcast_to([P, NE]), "rw_in")
                load(at(r_mc, NMCST), A["mcst"], "rw_in")
                load(wring[:, 0], A["w_shared"][li], "w_slot0")
                for e in range(RING - 1):
                    load(wring[:, e + 1], A["w_experts"][li, e], f"w_slot{e + 1}")
                sp.wait_ge(sem("hrow_ready"), 4 * (li + 1))
                load(scr["h_scr"].rearrange("(t p) n -> p t n", p=P), xg[:, 0:2], "hscr_out")

                def step(n, i):
                    if 5 <= n < NB:
                        sp.wait_ge(sem("dn_mm"), li * NB + (n - 3) + 4 * i)
                        sp.dma_start(wring[:, slot_of(n)], A["w_experts"][li, (n - 2) + 4 * i]).then_inc(sem(f"w_slot{slot_of(n)}"), 16)
                with sp.Fori(0, (NE - RING) // RING) as i:
                    for n in range(5, 9):
                        step(n, i)
                step(NB - 1, 0)
                for b in range(GD):
                    sp.wait_ge(sem(f"scat{b}"), 16 * (NE // GD) * (li + 1))

                def more(s, i):
                    sp.wait_ge(sem(f"ov_d{li}"), i * OVD + OVD * NE * (s - 1) + 1)
                    sp.dma_start(wring[:, 0], A["w_experts"][li, i]).then_inc(sem(f"ov_w{li}"), 16)
                overflow(li, sp, more, lambda s: sp.wait_ge(sem(f"ov_q{li}"), 32 * NE * s))
                for part, (k0, k1) in enumerate(ROW_PARTS):
                    for t in range(2):
                        load(wring[:, t, k0 * D:k1 * D], scr["r_scr"].rearrange("(t p k) n -> t p (k n)", t=2, p=P)[t][:, k0 * D:k1 * D], f"rows_in{part}")

            moe_loads(0)
            sp.wait_ge(sem("moe_x"), 1)
            for i in range(6):
                if i >= 3:
                    sp.wait_ge(sem("hy_proj"), i - 2)
                load(hyw[:, i % 3], A["hy_w_in"][i], f"hyw_in{i % 3}")
                if i == 0:
                    load(at(hc0, NHCST), A["hcst"], "fw_in")
                    load(f_w1, A["f_w1"], "fw_in")
                    load(f_w2, A["f_w2"], "fw_in")
                    load(f_w3, A["f_w3"], "fw_in")
            sp.wait_ge(sem("hy_proj"), 6)
            load(hyo, A["hy_w_out"], "hyo_in")
            moe_loads(1)
            sp.wait_ge(sem("moe_x"), 2)
            load(A["out"], xT, "out_done")
            sp.wait_ge(sem("out_done"), 16)

        @block.gpsimd
        def _(pool):
            ch = Chain(pool, sem("pool_chain"), sem)
            ch.then(pool.memset(ones, 1.0), "ones_ready")
            ch(pool.memset(st[:, 0], 0.0))
            lam8 = pw[:, :, 8]
            A8, B8 = tiles(tmp5, 2, NT5), tiles(tmp5 + 64, 2, NT5)
            t1, t2 = tiles(tmp5 + 128, 2, NT5), tiles(tmp5 + 192, 2, NT5)
            pool.wait_ge(sem("lam8_ready"), 1)
            pool.wait_ge(sem("est_ready"), 8)
            for k in range(NCH):
                a = k % 2 if k < NCH // 2 else 2 + k - NCH // 2
                b = (k + 1) % 2 if k + 1 < NCH // 2 else 2 + k + 1 - NCH // 2
                ins = pool.tensor_tensor(t1, A8, st[:, a], ALU.mult)
                ch(ins)
                ch(pool.tensor_tensor(t2, B8, st[:, a, ::-1], ALU.mult))
                ch(pool.tensor_tensor(t1, t1, est[:, k], ALU.add))
                ch(pool.tensor_tensor(st[:, b], t1, t2, ALU.add))
            ch.then(pool.tensor_copy(stb, st[:, 1 + XCH:1:-1].rearrange("p s r (g d) -> p s r g d", d=2)[:, :, :, :, 1]), "scan_done")

            def moe_pool(li):
                def gather(out, index, name):
                    pool.indirect_dma_start(out, None, scr["h_scr"], bass.IndirectOffsetOnAxis(index, 0), bounds_check=L - 1,
                                            oob_is_err=False).then_inc(sem(name), 16)

                def scatter(index, in_, name):
                    pool.indirect_dma_start(scr["r_scr"], bass.IndirectOffsetOnAxis(index, 0), in_, None, bounds_check=L * RPT - 1,
                                            oob_is_err=False).then_inc(sem(name), 16)

                def stand(name, count):
                    pool.wait_ge(sem(name), count)
                    pool.tensor_tensor(pads[name[:4]], ones[:, 0:1], ones[:, 0:1], ALU.add).then_inc(sem(name), 1)

                def gather_block(n, i):
                    b = n % GD
                    pool.tensor_copy(ib[:, b:b + 1], idx[:, 0, bass.ds(n - 2 + 4 * i, 1)]).then_inc(sem("ib_g"), 1)
                    stand("ib_g", 2 * (li * NE + n - 2) + 1 + 8 * i)
                    gather(xg[0:S, b], ib[:, b:b + 1], f"gath{b}")

                def step(n, i):
                    if n + GD < NB:
                        if n >= 2:
                            pool.wait_ge(sem("tx_mm"), li * NE + n - 1 + 4 * i)
                        gather_block(n + GD, i)
                    if n >= 3:
                        b = (n - 1) % GD
                        pool.wait_ge(sem("y_act"), li * NB + n + 4 * i)
                        pool.wait_ge(sem("y_dve"), li * NB + n + 4 * i)
                        pool.tensor_copy(ib[:, GD + b:GD + b + 1], idx[:, 1, bass.ds(n - 3 + 4 * i, 1)]).then_inc(sem("ib_s"), 1)
                        stand("ib_s", 2 * (li * NE + n - 3) + 1 + 8 * i)
                        scatter(ib[:, GD + b:GD + b + 1], yb[0:S, b], f"scat{b}")
                pool.wait_ge(sem("hscr_out"), 16 * (li + 1))
                ch(pool.memset(xg.rearrange("p b n -> p (b n)"), 0.0))
                pool.wait_ge(sem("idx_ready"), li + 1)
                gather_block(2, 0)
                gather_block(3, 0)
                steady(step, pool, (NB - 10) // 4 - 1)

                def more(s, i):
                    pool.wait_ge(sem(f"ov_d{li}"), i * OVD + OVD * NE * (s - 1) + OV_INDEX)
                    stand(f"ov_t{li}", i * 2 + 2 * NE * (s - 1) + 1)
                    gather(xg[0:S, 0], ib[:, 0:1], f"ov_q{li}")
                    pool.wait_ge(sem(f"ov_d{li}"), i * OVD + OVD * NE * (s - 1) + OV_ROWS)
                    stand(f"ov_t{li}", i * 2 + 2 * NE * (s - 1) + 2)
                    scatter(ib[:, GD:GD + 1], yb[0:S, 0], f"ov_q{li}")
                pool.memset(pads["ov_t"], 0.0).then_inc(sem(f"ov_t{li}"), 1)
                overflow(li, pool, more)
                for k in range(RPT):
                    for part, (k0, k1) in enumerate(ROW_PARTS):
                        if k == k0:
                            pool.wait_ge(sem(f"rows_in{part}"), 32 * (li + 1))
                    ins = pool.tensor_tensor(xg[:, 1], ysh[:, 1] if k == 0 else xg[:, 1], wring[:, 1, k * D:(k + 1) * D], ALU.add)
                    ch(ins) if k < RPT - 1 else ch.then(ins, "sum_pool")

            pads = {"ib_g": at(r_pad, 1), "ib_s": at(r_pad + 1, 1), "ov_t": at(r_pad + 2, 1)}
            moe_pool(0)
            moe_pool(1)

        @block.tensor
        def _(pe):
            def mm(out, lhsT, rhs, start, stop, skip=False):
                return pe.matmul(out, lhsT, rhs, start=start, stop=stop, skip_group_check=skip)

            def sum_squares(src, bank, n):
                for k in range(KD):
                    last = mm(ps[:, bank, 0:n], ones, src[:, k], k == 0, k == KD - 1)
                return last

            def chunk_kernels(half):
                if half == 0:
                    pe.wait_ge(sem("ctab_ready"), 1)
                else:
                    pe.wait_ge(sem("kk_half"), 1)
                for t in range(16 * half, 16 * half + 16):
                    g, d = t // 2, t % 2
                    bank, off = 3 + (t % 16) // 4, (t % 4) * TW
                    o = ps[0:2 * C5, bank, off:off + TW]
                    j0 = 0 if d == 0 else 1
                    mm(o, bdr[:, t], ctr[:, g, d, j0:j0 + T5].rearrange("p j c -> p (j c)"), True, False)
                    last = mm(o, bdi[:, t], ctn[:, g, d, j0:j0 + T5].rearrange("p j c -> p (j c)"), False, True)
                last.then_inc(sem("kk_mm"), 1)

            def b_matrices(q):
                pe.wait_ge(sem("bt_ready"), q + 1)
                for r in range(2):
                    for hb in range(2):
                        n = 4 * q + 2 * r + hb
                        if n >= 2:
                            pe.wait_ge(sem("bm_evicted"), n - 1)
                        for t in range(4):
                            last = pe.transpose(ps[:, 3 + n % 2, t * P:(t + 1) * P], bt[:, q % 2, r, hb * 4 + t], ident)
                        last.then_inc(sem("bt_turned"), 1)

            pe.wait_ge(sem("sc_ready"), 1)
            pe.wait_ge(sem("small_in"), 32)
            for i in range(NADC):
                pe.wait_ge(sem(f"ada_in{i % 2}"), 16 * (i // 2 + 1))
                if i >= 2:
                    pe.wait_ge(sem("adrow_ready"), i - 1)
                for k in range(KD):
                    last = mm(ps[0:2, i % 2, :], sc[:, k], adw[:, i % 2, k], k == 0, k == KD - 1)
                last.then_inc(sem("ada_mm"), 1)
                if i >= 1:
                    ada_turn(pe, i - 1)
                if i in KK_AT:
                    chunk_kernels(KK_AT.index(i))
                if i in BT_AT:
                    b_matrices(BT_AT.index(i))
                if i == NORM_AT:
                    pe.wait_ge(sem("squared"), 2)
                    pe.wait_ge(sem("ones_ready"), 1)
                    sum_squares(hT, 7, 512).then_inc(sem("norm_mm"), 1)
            ada_turn(pe, NADC - 1)
            pe.wait_ge(sem("win_in"), 16)
            pe.wait_ge(sem("h_ready"), 1)
            pe.wait_ge(sem("bm_evicted"), 16)
            for bank, c0, m, tok in ((0, QL, P, 0), (1, QL + KVL - NOPE, QKH, 0)):
                for k in range(KD):
                    last = mm(ps[0:m, bank, :], w_in[:, k, c0:c0 + m], hT[:, k], k == 0, k == KD - 1)
                last.then_inc(sem("proj_mm"), 1)
            for i in range(2):
                for k in range(KD):
                    last = mm(ps[:, 2, i * L:(i + 1) * L], w_in[:, k, i * P:(i + 1) * P], hT[:, k, L:2 * L], k == 0, k == KD - 1)
            last.then_inc(sem("proj_mm"), 1)
            for i in range(4):
                for k in range(KD):
                    last = mm(ps[:, 3 + i, :], w_in[:, k, UOFF + i * P:UOFF + (i + 1) * P], hT[:, k], k == 0, k == KD - 1)
                last.then_inc(sem("proj_mm"), 1)
            pe.wait_ge(sem("squared"), 2 + 2)
            pe.wait_ge(sem("kvl_evicted"), 3)
            mm(ps[:, 7, :], ones, sql[:, 0], True, True).then_inc(sem("lat_mm"), 1)
            for i in range(2):
                last = mm(ps[:, 0, 0:L], ones, sql[:, 1, i * L:(i + 1) * L], i == 0, i == 1)
            last.then_inc(sem("lat_mm"), 1)
            pe.wait_ge(sem("ql_normed"), 1)
            pe.wait_ge(sem("u_evicted"), 4)
            pe.wait_ge(sem("uw_in"), 32)
            for h in range(HEADS):
                for k in range(2):
                    last = mm(ps[0:QKH, 3 + h // 2, (h % 2) * L:(h % 2 + 1) * L], w_uq[:, k, h * QKH:(h + 1) * QKH], ql[:, k], k == 0, k == 1)
                if h % 2:
                    last.then_inc(sem("head_mm"), 1)
            kbank = (0, 1, 2, 7)
            for h in range(HEADS):
                if h >= 4:
                    pe.wait_ge(sem("kh_evicted"), h - 3)
                mm(ps[0:NOPE, kbank[h % 4], :], w_ukv[:, h * P:h * P + NOPE], kvl, True, True).then_inc(sem("head_mm"), 1)
            for t in range(4):
                pe.wait_ge(sem("qh_evicted"), t + 1)
                mm(ps[:, 3 + t, :], kvl[:, t * P:(t + 1) * P],
                   w_ukv.rearrange("p (h n) -> p h n", h=HEADS)[:, :, NOPE:P], True, True).then_inc(sem("head_mm"), 1)
            pe.wait_ge(sem("U_in"), 16 * T5)
            pe.wait_ge(sem("kh_evicted"), 8)
            pe.wait_ge(sem("vt_evicted"), 4)
            for b in range(8):
                for t in range(8):
                    tile, r = (b // 2) * 8 + t, b % 2
                    for g2 in range(2):
                        last = mm(ps[g2 * N5:(g2 + 1) * N5, b, t * NCH:(t + 1) * NCH], bm[:, tile, r, g2 * N5:(g2 + 1) * N5],
                                  U[:, 2 * (tile // 2) + g2], True, True)
                last.then_inc(sem("head_mm"), 1)
            def pick(h):
                return at(r_cst + CST["pick"][0] + HEADS - 1 - h, HEADS, QKH)

            def over_features(o, h, a, n):
                return mm(o, ident[0:HEADS, h:h + 1].broadcast_to([HEADS, QKH]), rkq[:, a:a + n], True, True)

            pe.wait_ge(sem("squared"), 4 + 1)
            pe.wait_ge(sem("est_ready"), 8)
            for h in range(HEADS):
                last = mm(ps[0:HEADS, 0, 0:L], pick(h), sqq[:, h], h == 0, h == HEADS - 1)
            last.then_inc(sem("rot_mm"), 1)
            pe.wait_ge(sem("squared"), 5 + 1)
            for h in range(HEADS):
                last = mm(ps[0:HEADS, 1, :], pick(h), sqk[:, h], h == 0, h == HEADS - 1)
            last.then_inc(sem("rot_mm"), 1)
            pe.wait_ge(sem("qh_normed"), 1)
            for b in range(4):
                for h in (2 * b, 2 * b + 1):
                    last = over_features(ps[0:QKH, 2 + b, (h % 2) * L:(h % 2 + 1) * L], h, 2 * L, L)
                last.then_inc(sem("rot_mm"), 1)
            pe.wait_ge(sem("kh_normed"), 1)
            kr_bank = (0, 1, 6, 7)
            for h in range(HEADS):
                if h >= 4:
                    pe.wait_ge(sem("kh_normed"), 1 + h - 3)
                over_features(ps[0:QKH, kr_bank[h % 4], :], h, 0, 2 * L).then_inc(sem("rot_mm"), 1)
            pe.wait_ge(sem("qh_normed"), 5)
            for b in range(4):
                mm(ps[0:QKH, 2 + b, :], cst("swap", QKH), qh[:, 2 * b:2 * b + 2].rearrange("p h t -> p (h t)"), True, True).then_inc(sem("rot_mm"), 1)
            for b in range(4):
                if b == 0:
                    pe.wait_ge(sem("kh_normed"), 1 + HEADS)
                mm(ps[0:QKH, kr_bank[b], :], cst("swap", QKH), kh[:, 2 * b:2 * b + 2, L:2 * L], True, True).then_inc(sem("rot_mm"), 1)
            pe.wait_ge(sem("rope_done"), 2)

            def scores(n):
                h, t = n // 2, n % 2
                if n >= 2:
                    pe.wait_ge(sem("exp_done"), n - 1)
                mm(ps[:, n % 2, :], qh[:, h, t * P:(t + 1) * P], kh[:, h], True, True).then_inc(sem("scores_done"), 1)

            def s5_outputs(j):
                if j == 0:
                    pe.wait_ge(sem("scan_done"), 1)
                    pe.wait_ge(sem("toep_in"), 16 * 2 * T5)
                if j >= 2 and j % 2 == 0:
                    pe.wait_ge(sem("y_evicted"), j)
                for g in range(4 * j, 4 * j + 4):
                    c0 = (g % 8 // 2) * TW
                    o = ps[0:XCH, 5 + g % 2, c0:c0 + TW]
                    rows = slice((g % 2) * N5, (g % 2 + 1) * N5)
                    mm(o, U[:, g, XCH:2 * XCH], toep[:, g], True, False)
                    for d in range(2):
                        j0 = 1 - d
                        for r, tab in ((0, ctr), (1, ctn)):
                            states = st[rows, 2:2 + XCH, r, g // 2 * 2] if d == 0 else stb[rows, :, r, g // 2]
                            last = mm(o, states,
                                      tab[rows, g // 2, d, j0:j0 + T5].rearrange("p j c -> p (j c)"), False, d == 1 and r == 1)
                last.then_inc(sem("y_mm"), 1)
            scores(0)
            for n in range(2 * HEADS):
                h, t = n // 2, n % 2
                if n + 1 < 2 * HEADS:
                    scores(n + 1)
                if n >= S5_AT:
                    s5_outputs(n - S5_AT)
                pe.wait_ge(sem("prob_ready"), n + 1)
                if n >= 2:
                    pe.wait_ge(sem("pT_ready"), n - 1)
                for k in range(4):
                    last = pe.transpose(ps[:, 2 + n % 2, k * P:(k + 1) * P], prob[:, n % 2, k * P:(k + 1) * P], ident)
                last.then_inc(sem("pT_mm"), 1)
                if t == 1:
                    pe.wait_ge(sem("pT_ready"), n + 1)
                    if h >= 2:
                        pe.wait_ge(sem("att_ready"), h - 1)
                    o = ps[(h % 2) * VH:(h % 2 + 1) * VH, 4 if h % 2 == 0 else 7, 0:L]
                    for k in range(4):
                        last = mm(o, vt[:, k, h * VH:(h + 1) * VH], pT[:, h % 2, k], k == 0, k == 3)
                    last.then_inc(sem("pv_mm"), 1)
            for j in range(2 * HEADS - S5_AT, G5 // 4):
                s5_outputs(j)
            pe.wait_ge(sem("y_evicted"), 8)
            for i in range(4):
                for t in range(T5):
                    last = pe.transpose(ps[:, 5 + i // 2, (i % 2) * L + t * XCH:(i % 2) * L + (t + 1) * XCH],
                                        ys[:, i, t].rearrange("p g c -> p (g c)"), ident[0:XCH, 0:XCH])
            last.then_inc(sem("yT_mm"), 1)
            pe.wait_ge(sem("z_ready"), 2)
            pe.wait_ge(sem("glu_in"), 16)
            for j in range(4):
                for k in range(4):
                    last = mm(ps[:, 5 + j // 2, (j % 2) * L:(j % 2 + 1) * L], glu_w[:, k, j * P:(j + 1) * P], zT[:, k], k == 0, k == 3)
                last.then_inc(sem("glu_mm"), 1)
            pe.wait_ge(sem("att_ready"), HEADS)
            pe.wait_ge(sem("s5_out"), 4)
            pe.wait_ge(sem("wout_in"), 16)
            for j in range(KD):
                for k in range(KD):
                    rhs = att[:, k] if k < 4 else zT[:, k - 4]
                    last = mm(ps[:, j // 2, (j % 2) * L:(j % 2 + 1) * L], w_out[:, k, j * P:(j + 1) * P], rhs, k == 0, k == KD - 1)
                last.then_inc(sem("mix_mm"), 1)

            def moe_pe(li):
                def turn(out, in_, one, first):
                    return mm(out, in_, one, True, True) if first else pe.transpose(out, in_, one)

                def half_gate_up(n, k0):
                    for k in range(k0, k0 + 4):
                        lhsT = hX[:, k, n * P:(n + 1) * P] if n < 2 else xgT[:, n % 2, k]
                        last = mm(ps[0:rows_of(n), 2 + n % 2, :], lhsT, gate_up(slot_of(n), k), k == 0, k == KD - 1)
                    return last

                pe.wait_ge(sem("squared"), 7 + 3 * li)
                sum_squares(sqX, 6, L).then_inc(sem("norm_mm"), 1)
                pe.wait_ge(sem("moe_h"), li + 1)
                pe.wait_ge(sem("rw_in"), 48 * (li + 1))
                for t in range(2):
                    for k in range(KD):
                        last = mm(ps[:, 7, t * NE:(t + 1) * NE], hX[:, k, t * P:(t + 1) * P], rw[:, k], k == 0, k == KD - 1)
                last.then_inc(sem("logits"), 1)
                for t in range(2):
                    for c in range(2):
                        for k in range(4):
                            last = pe.transpose(ps[:, 3 + 2 * t + c, k * P:(k + 1) * P], hX[:, 4 * c + k, t * P:(t + 1) * P], ident)
                        last.then_inc(sem("hrow_mm"), 1)
                pe.wait_ge(sem("w_slot0"), 16 * (17 * li + 1))
                half_gate_up(0, 0)
                half_gate_up(0, 4).then_inc(sem("gu_mm"), 1)
                pe.wait_ge(sem("route"), 2 * (li + 1))
                m0, m1_ = at(rtb + 10 * NE, NE), at(rtb + 11 * NE, NE)
                mm(ps[:, 7, 0:NE], mcst("tri"), m0, True, True)
                mm(ps[:, 7, NE:2 * NE], ones, m0, True, False)
                mm(ps[:, 7, NE:2 * NE], mcst("tri"), m1_, False, True)
                mm(ps[:, 7, 2 * NE:3 * NE], ones, m0, True, False)
                mm(ps[:, 7, 2 * NE:3 * NE], ones, m1_, False, True).then_inc(sem("pos_mm"), 1)

                def step(n, i):
                    def at_least(name, count, per=NB):
                        pe.wait_ge(sem(name), li * per + count + 4 * i)

                    def turn_next(m):
                        pe.wait_ge(sem(f"gath{m % GD}"), 16 * (li * (NE // GD) + (m - 2) // GD + 1) + 16 * i)
                        if m >= 3:
                            at_least("xt_act", m - 2, NE)
                            at_least("xt_dve", m - 2, NE)
                        for k in range(KD):
                            last = turn(ps[:, k // 4, (k % 4) * S:(k % 4 + 1) * S], xg[0:S, m % GD, k * P:(k + 1) * P], ident[0:S, 0:S], k == 0)
                        last.then_inc(sem("tx_mm"), 1)
                    if 3 <= n + 1 < NB:
                        turn_next(n + 1)
                    if 2 <= n < NB:
                        s_ = slot_of(n)
                        pe.wait_ge(sem(f"w_slot{s_}"), 16 * (li * (17 if s_ == 0 else 16) + (n - 1) // RING + 1) + 16 * i)
                        at_least("xt_act", n - 1, NE)
                        at_least("xt_dve", n - 1, NE)
                        at_least("h_done", n - 1)
                        half_gate_up(n, 0)
                    if n >= 1:
                        at_least("h_done", n)
                        if n >= 2:
                            at_least("hT_ready", n - 1)
                        for f in range(2):
                            q = rows_of(n - 1)
                            last = turn(ps[:, 4, f * q:(f + 1) * q], hh[0:q, (n - 1) % 2, f * P:(f + 1) * P], ident[0:q, 0:q], f == 0)
                        last.then_inc(sem("ht_mm"), 1)
                    if 2 <= n < NB:
                        half_gate_up(n, 4).then_inc(sem("gu_mm"), 1)
                    if n >= 1:
                        at_least("hT_ready", n)
                        if n >= 2:
                            at_least("y_act", n - 1)
                            at_least("y_dve", n - 1)
                        for c in range(2):
                            for f in range(2):
                                q = rows_of(n - 1)
                                last = mm(ps[0:q, 5 + c, :], hT2[:, (n - 1) % 2, f, 0:q], w_down(slot_of(n - 1), f, c), f == 0, f == 1)
                        last.then_inc(sem("dn_mm"), 1)
                    if n == 1:
                        turn_next(2)
                pe.wait_ge(sem("hrow_ready"), 4 * (li + 1))
                half_gate_up(1, 0)
                half_gate_up(1, 4).then_inc(sem("gu_mm"), 1)
                for q in range(NE // SG):
                    pe.wait_ge(sem("sel_ready"), li * (NE // SG) + q + 1)
                    for e in range(SG * q, SG * q + SG):
                        for t in range(2):
                            last = mm(ps[0:S, 7, NR * e:NR * (e + 1)], selg[:, q % 2, t, e % SG], rparts[:, t, e], t == 0, t == 1, skip=True)
                    last.then_inc(sem("tab_mm"), 1)
                steady(step, pe)
                def more(s, i):
                    ovd, ovp = sem(f"ov_d{li}"), sem(f"ov_p{li}")
                    base = NE * (s - 1)
                    pe.wait_ge(ovd, i * OVD + OVD * base + OV_SEL)
                    for t in range(2):
                        last = mm(ps[0:S, 7, 0:3], sel[:, 0, t], sel[:, 1, t, 0:3], t == 0, t == 1)
                    last.then_inc(ovp, 1)
                    pe.wait_ge(sem(f"ov_q{li}"), i * 32 + 32 * base + 16)
                    for k in range(KD):
                        last = turn(ps[:, k // 4, (k % 4) * S:(k % 4 + 1) * S], xg[0:S, 0, k * P:(k + 1) * P], ident[0:S, 0:S], k == 0)
                    last.then_inc(ovp, 1)
                    pe.wait_ge(sem(f"ov_w{li}"), i * 16 + 16 * (base + 1))
                    pe.wait_ge(ovd, i * OVD + OVD * base + OV_TURNED)
                    for k in range(KD):
                        last = mm(ps[0:S, 2, :], xgT[:, 0, k], gate_up(0, k), k == 0, k == KD - 1)
                    last.then_inc(ovp, 1)
                    pe.wait_ge(ovd, i * OVD + OVD * base + OV_HIDDEN)
                    for f in range(2):
                        last = turn(ps[:, 4, f * S:(f + 1) * S], hh[0:S, 0, f * P:(f + 1) * P], ident[0:S, 0:S], f == 0)
                    last.then_inc(ovp, 1)
                    pe.wait_ge(ovd, i * OVD + OVD * base + OV_HIDDEN_TURNED)
                    for c in range(2):
                        for f in range(2):
                            last = mm(ps[0:S, 5 + c, :], hT2[:, 0, f, 0:S], w_down(0, f, c), f == 0, f == 1)
                    last.then_inc(ovp, 1)
                overflow(li, pe, more)
                for t in range(2):
                    pe.wait_ge(sem("sum_dve" if t == 0 else "sum_pool"), li + 1)
                    for k in range(KD):
                        last = pe.transpose(ps[:, k // 2, (k % 2) * L + t * P:(k % 2) * L + (t + 1) * P], xg[:, t, k * P:(k + 1) * P], ident)
                    last.then_inc(sem("out_mm"), 1)

            moe_pe(0)
            def filter_rows(t):
                for j in range(4):
                    mm(ps[:, 4 + j, :], hid[:, 1, t * P:(t + 1) * P], f_w3[:, j * 512:(j + 1) * 512], True, True).then_inc(sem("filter_mm"), 1)

            pe.wait_ge(sem("squared"), 7 + 1)
            sum_squares(sqX, 6, L).then_inc(sem("norm_mm"), 1)
            pe.wait_ge(sem("hy_h"), 1)
            for i in range(6):
                pe.wait_ge(sem(f"hyw_in{i % 3}"), 16 * (i // 3 + 1))
                if i >= 2:
                    pe.wait_ge(sem("hyp_evicted"), i - 1)
                for j in range(4):
                    for k in range(KD):
                        last = mm(ps[:, 2 * (i % 2) + j // 2, (j % 2) * L:(j % 2 + 1) * L], hyw[:, i % 3, k, j * P:(j + 1) * P], hX[:, k], k == 0, k == KD - 1)
                last.then_inc(sem("hy_proj"), 1)
                if i == 0:
                    pe.wait_ge(sem("fw_in"), 64)
                    mm(ps[0:FH, 4, 0:L], f_w1, hcst("zemb", 1, FE), True, True).then_inc(sem("filter_mm"), 1)
                if i == 1:
                    pe.wait_ge(sem("hid_ready"), 1)
                    mm(ps[0:FH, 5, 0:L], f_w2, hid[:, 0], True, True).then_inc(sem("filter_mm"), 1)
                if i == 2:
                    pe.wait_ge(sem("hid_ready"), 2)
                    filter_rows(0)
                if i == 3:
                    pe.wait_ge(sem("hf_ready"), 4)
                    filter_rows(1)
                if i == 4:
                    pe.wait_ge(sem("squared"), 8 + 1)
                    for j in range(8):
                        for k in range(4):
                            last = mm(ps[:, 4, j:j + 1], hsq[:, k, j * P:(j + 1) * P], ones[:, 0:1], k == 0, k == 3)
                    last.then_inc(sem("filter_mm"), 1)
            pe.wait_ge(sem("hf_comb"), 1)
            pe.wait_ge(sem("hn_read"), 1)
            for w, (mat, src) in enumerate((("fc", 0), ("fs", 2))):
                for m in range(2):
                    for c in range(2):
                        n = w * 4 + m * 2 + c
                        if n >= 4:
                            pe.wait_ge(sem("H_evicted"), n - 3)
                        for k in range(2):
                            last = mm(ps[:, 4 + n % 4, :], hcst(mat)[:, k, m * P:(m + 1) * P], hf[:, src + k, c * 512:(c + 1) * 512], k == 0, k == 1)
                        last.then_inc(sem("filter_mm"), 1)
            pe.wait_ge(sem("H_evicted"), 8)
            pe.wait_ge(sem("z_conv"), 1)
            for t in range(2):
                for hb in range(2):
                    for j in range(4):
                        last = pe.transpose(ps[:, 4 + 2 * t + hb, j * P:(j + 1) * P], zt[:, hb * 4 + j, t * P:(t + 1) * P], ident)
                    last.then_inc(sem("zs_mm"), 1)
            pe.wait_ge(sem("zs_ready"), 4)
            for w, mat in enumerate(("fc", "fs")):
                for m in range(2):
                    for c in range(2):
                        n = w * 4 + m * 2 + c
                        for k in range(2):
                            last = mm(ps[:, n, :], hcst(mat)[:, k, m * P:(m + 1) * P], zs[:, k, c * 512:(c + 1) * 512], k == 0, k == 1)
                        last.then_inc(sem("Z_mm"), 1)
            pe.wait_ge(sem("Y_ready"), 1)
            for j in range(KD):
                for w, (mat, src) in enumerate((("ic", YR), ("is", YS))):
                    for k in range(2):
                        last = mm(ps[:, j // 2, (j % 2) * L:(j % 2 + 1) * L], src[:, k, j * P:(j + 1) * P], hcst(mat)[:, k], w == 0 and k == 0, w == 1 and k == 1)
                last.then_inc(sem("conv_mm"), 1)
            pe.wait_ge(sem("yh_ready"), 8)
            pe.wait_ge(sem("hyo_in"), 16)
            for j in range(KD):
                for k in range(KD):
                    last = mm(ps[:, 4 + j // 2, (j % 2) * L:(j % 2 + 1) * L], hyo[:, k, j * P:(j + 1) * P], zt[:, k], k == 0, k == KD - 1)
                last.then_inc(sem("mix_mm"), 1)
            moe_pe(1)

        @block.scalar
        def _(act):
            ch = Chain(act, sem("act_chain"), sem)

            def f(out, in_, func, **kw):
                return act.activation(out, in_, func, **kw)

            act.wait_ge(sem("small_in"), 32)
            ch.then(f(sc, col("c", 0, 16).rearrange("p (k m) -> p k m", m=2), ACT.Silu), "sc_ready")
            act.wait_ge(sem("s5p_in"), 16)
            ch.then(f(sm(0), s5("lst"), ACT.Exp), "s5_step")
            act.wait_ge(sem("s5_arg"), 1)
            ch(f(sm(4), sm(1), ACT.Exp))
            ch(f(sm(5), sm(2), ACT.Sin))
            ch.then(f(sm(6), sm(3), ACT.Sin), "s5_trig")

            def rms(bank, n, count, name, rows=P, width=D, out=None):
                act.wait_ge(sem(name), count)
                return f(out if out is not None else stx[:, 0:n], ps[0:rows, bank, 0:n], ACT.Sqrt, scale=1.0 / width, bias=at(r_eps, 1, rows))

            for i in range(NADC):
                act.wait_ge(sem("ada_mm"), i + 1)
                if i >= 2:
                    act.wait_ge(sem("ada_turned"), i - 1)
                ch.then(f(adrow[:, i % 2], ps[0:2, i % 2, :], ACT.Copy), "adrow_ready")
                if i >= 1:
                    act.wait_ge(sem("ada_turned"), i)
                    ch.then(f(modc[:, 4 * (i - 1):4 * i].rearrange("p c m -> p (c m)"), ps[:, 2, 0:8], ACT.Copy), "modc_ready")
                if i in BT_AT:
                    q = BT_AT.index(i)
                    for n in range(4 * q, 4 * q + 4):
                        act.wait_ge(sem("bt_turned"), n + 1)
                        r, hb = n // 2 % 2, n % 2
                        if n == 0:
                            act.wait_ge(sem("kk_ready"), 1)
                        ch.then(f(bm[:, 8 * q + 4 * hb:8 * q + 4 * hb + 4, r], ps[:, 3 + n % 2, :].rearrange("p (t m) -> p t m", t=4), ACT.Copy), "bm_evicted")
                if i == SQUARES_AT:
                    act.wait_ge(sem("x_in"), 16)
                    act.wait_ge(sem("kscr_out"), 16)
                    act.wait_ge(sem("ctx_in"), 16)
                    ch.then(f(hT[:, :, 0:L], cx, ACT.Square), "squared")
                    ch.then(f(hT[:, :, L:2 * L], xT, ACT.Square), "squared")
                if i == NORM_AT:
                    act.wait_ge(sem("eps_ready"), 1)
                    ch.then(rms(7, 512, 1, "norm_mm", out=rs0), "rms_ready")
            act.wait_ge(sem("ada_turned"), NADC)
            ch.then(f(modc[:, 4 * (NADC - 1):4 * NADC].rearrange("p c m -> p (c m)"), ps[:, 2, 0:8], ACT.Copy), "modc_ready")
            for i in range(4):
                act.wait_ge(sem("proj_mm"), 4 + i)
                ch.then(f(u_sb[:, i], ps[:, 3 + i, :].rearrange("p (c t) -> p t c", t=T5), ACT.Copy), "u_evicted")
            act.wait_ge(sem("kvl_evicted"), 3)
            ch.then(f(sql[:, 0], kvl, ACT.Square), "squared")
            ch.then(f(sql[:, 1], ql.rearrange("p k t -> p (k t)"), ACT.Square), "squared")
            act.wait_ge(sem("h_ready"), 1)
            ch.then(rms(7, 512, 1, "lat_mm", width=KVL), "lrms_ready")
            act.wait_ge(sem("kvl_normed"), 1)
            ch.then(rms(0, L, 2, "lat_mm", width=QL), "lrms_ready")
            for b in range(4):
                act.wait_ge(sem("head_mm"), b + 1)
                if b == 0:
                    act.wait_ge(sem("kvl_evicted"), 3)
                ch.then(f(qh[:, 2 * b:2 * b + 2].rearrange("p h t -> p (h t)"), ps[0:QKH, 3 + b, :], ACT.Copy), "qh_evicted")
            for t in range(4):
                act.wait_ge(sem("head_mm"), 12 + t + 1)
                ch.then(f(vt[:, t], ps[:, 3 + t, :], ACT.Copy), "vt_evicted")
            for b in range(8):
                act.wait_ge(sem("head_mm"), 16 + b + 1)
                r, g0 = b % 2, (b // 2) * 8
                src = ps[:, b, :].rearrange("p (g d c) -> p g d c", d=2, c=NCH)
                dst = est[:, :, r, g0:g0 + 8].rearrange("p s (g d) -> p g d s", d=2)
                ch(f(dst[:, :, 0], src[:, :, 0], ACT.Copy))
                ch(f(dst[:, :, 1, 0:XCH], src[:, :, 1, XCH - 1::-1], ACT.Copy))
                ch.then(f(dst[:, :, 1, XCH:NCH], src[:, :, 1, NCH - 1:XCH - 1:-1], ACT.Copy), "est_ready")
            act.wait_ge(sem("head_mm"), 16 + 8)
            ch.then(f(sqq, qh, ACT.Square), "squared")
            act.wait_ge(sem("kh_evicted"), 8)
            act.wait_ge(sem("kr_copied"), 1)
            ch.then(f(sqk, kh, ACT.Square), "squared")
            for bank, a, n, name in ((0, 2 * L, L, "qrms"), (1, 0, 2 * L, "qrms")):
                act.wait_ge(sem("rot_mm"), bank + 1)
                ch.then(f(rkq[:, a:a + n], ps[0:HEADS, bank, 0:n], ACT.Sqrt, scale=1.0 / QKH, bias=at(r_eps, 1, HEADS)), name)
            for n in range(2 * HEADS):
                act.wait_ge(sem("max_done"), n + 1)
                if n >= 2:
                    act.wait_ge(sem("pT_mm"), n - 1)
                ch.then(f(prob[:, n % 2], ps[:, n % 2, :], ACT.Exp, scale=QKH ** -0.5, bias=at(r_st + n, 1), accum_out=at(r_st + 16 + n, 1)), "exp_done")
                if n >= 1:
                    turned(act, f, ch, n - 1)
            turned(act, f, ch, 2 * HEADS - 1)
            act.wait_ge(sem("pv_mm"), HEADS)
            act.wait_ge(sem("yT_mm"), 1)
            for b in range(2):
                ins = f(zT[:, 2 * b:2 * b + 2].rearrange("p i (c t) -> p i t c", t=T5),
                        ps[:, 5 + b, :].rearrange("p (i t c) -> p i t c", i=2, t=T5), ACT.Gelu_apprx_tanh)
                ch.then(ins, "z_ready")
            for j in range(4):
                act.wait_ge(sem("glu_mm"), j // 2 * 2 + 2)
                ch.then(f(yT.rearrange("p i t c -> p i (t c)")[:, j], ps[:, 5 + j // 2, (j % 2) * L:(j % 2 + 1) * L], ACT.Sigmoid, bias=col("glub", j)), "glu_sig")

            def moe_act(li):
                act.wait_ge(sem("x_mixed"), li + 1)
                ch.then(f(sqX, xT, ACT.Square), "squared")
                ch.then(rms(6, L, 2 if li == 0 else 4, "norm_mm"), "rms_ready")
                act.wait_ge(sem("logits"), li + 1)
                ch.then(f(at(rtb + 2 * NE, 2 * NE), ps[:, 7, 0:2 * NE], ACT.Exp, scale=-1.0), "rexp")
                for n in range(4):
                    act.wait_ge(sem("hrow_mm"), 4 * li + n + 1)
                    ch.then(f(xg[:, n // 2, (n % 2) * 512:(n % 2 + 1) * 512], ps[:, 3 + n, :], ACT.Copy), "hrow_ready")

                def step(n, i):
                    def at_least(name, count, per=NB):
                        act.wait_ge(sem(name), li * per + count + 4 * i)

                    def turned_next(m):
                        at_least("tx_mm", m - 1, NE)
                        if n - 1 >= 2:
                            at_least("gu_mm", n)
                        f(xgT[:, m % 2, 0:4].rearrange("p k t -> p (k t)"), ps[:, 0, 0:4 * S], ACT.Copy).then_inc(sem("xt_act"), 1)
                    if 3 <= n + 1 < NB:
                        turned_next(n + 1)
                    if n >= 1:
                        at_least("ht_mm", n)
                        if n >= 3:
                            at_least("dn_mm", n - 2)
                        q = rows_of(n - 1)
                        f(hT2[:, (n - 1) % 2, :, 0:q], ps[:, 4, 0:2 * q].rearrange("p (f t) -> p f t", f=2), ACT.Copy).then_inc(sem("hT_ready"), 1)
                    if n < NB:
                        at_least("gu_mm", n + 1)
                        if n >= 2:
                            at_least("h_done", n - 1)
                        q = rows_of(n)
                        f(sg[0:q, n % 2], ps[0:q, 2 + n % 2, 0:FF], ACT.Silu).then_inc(sem("sg_ready"), 1)
                    if n >= 1:
                        at_least("dn_mm", n)
                        if n >= 7:
                            act.wait_ge(sem(f"scat{(n - 1) % GD}"), 16 * (li * (NE // GD) + (n - 7) // GD + 1) + 16 * i)
                        dst = ysh[:, n - 1, 512:] if n <= 2 else yb[0:S, (n - 1) % GD, 512:]
                        f(dst, ps[0:rows_of(n - 1), 6, :], ACT.Copy).then_inc(sem("y_act"), 1)
                    if n == 1:
                        turned_next(2)
                steady(step, act)

                def more(s, i):
                    act.wait_ge(sem(f"ov_p{li}"), i * 5 + 5 * NE * (s - 1) + 3)
                    f(sg[0:S, 0], ps[0:S, 2, 0:FF], ACT.Silu).then_inc(sem(f"ov_a{li}"), 1)
                overflow(li, act, more)

            moe_act(0)
            act.wait_ge(sem("moe_x"), 1)
            ch.then(f(sqX, xT, ACT.Square), "squared")
            ch.then(rms(6, L, 3, "norm_mm"), "rms_ready")
            for i in range(6):
                act.wait_ge(sem("hy_proj"), i + 1)
                if i >= 2:
                    act.wait_ge(sem("conv_done"), i - 1)
                for hb in range(2):
                    ins = f(pp[:, i % 2, 2 * hb:2 * hb + 2].rearrange("p i t -> p (i t)"), ps[:, 2 * (i % 2) + hb, :], ACT.Copy)
                    if hb == 0:
                        ch(ins)
                    else:
                        ch.then(ins, "hyp_evicted")
                if i < 2:
                    act.wait_ge(sem("hid_arg"), i + 1)
                    ch.then(f(hid[:, i], at(hsc, L, FH), ACT.Sin), "hid_ready")
                if i == 3:
                    act.wait_ge(sem("hf_ready"), 8)
                    ch.then(f(hsq, hf, ACT.Square), "squared")
                if i == 4:
                    act.wait_ge(sem("filter_mm"), 10 + 1)
                    ch.then(f(hns, ps[:, 4, 0:8], ACT.Sqrt, bias=at(r_eps, 1)), "hn_read")
            for n in range(8):
                act.wait_ge(sem("filter_mm"), 11 + n + 1)
                dst = (HR if n < 4 else HS)[:, n // 2 % 2, (n % 2) * 512:(n % 2 + 1) * 512]
                ch.then(f(dst, ps[:, 4 + n % 4, :], ACT.Copy), "H_evicted")
            for n in range(4):
                act.wait_ge(sem("zs_mm"), n + 1)
                ch.then(f(zs[:, n // 2, (n % 2) * 512:(n % 2 + 1) * 512], ps[:, 4 + n, :], ACT.Copy), "zs_ready")
            moe_act(1)

        @block.vector
        def _(dve):
            ch = Chain(dve, sem("dve_chain"), sem)
            tt, ts, stt = dve.tensor_tensor, dve.tensor_scalar, dve.scalar_tensor_tensor
            M, AD, SU = ALU.mult, ALU.add, ALU.subtract
            ch.then(dve.memset(at(r_eps, 1), EPS), "eps_ready")
            ch(dve.memset(bdr.rearrange("p t m -> p (t m)"), 0.0))
            ch(dve.memset(bdi.rearrange("p t m -> p (t m)"), 0.0))
            dve.wait_ge(sem("s5_step"), 1)

            def cmul(o, a, b, t):
                ch(tt(t, a[1], b[1], M))
                ch(tt(o[0], a[0], b[0], M))
                ch(tt(o[0], o[0], t, SU))
                ch(tt(t, a[1], b[0], M))
                ch(tt(o[1], a[0], b[1], M))
                ch(tt(o[1], o[1], t, AD))

            def reduced(out, x, t, quarter):
                ch(ts(t, x, 1.0 / TWO_PI, 0.25 * quarter, M, AD))
                ch(ts(t, t, ROUND, None, AD))
                ch(ts(t, t, ROUND, None, SU))
                ch(stt(out, t, -PI_HI, x, M, AD))
                ch(stt(out, t, -PI_LO, out, M, AD))
                if quarter:
                    ch(ts(out, out, quarter * math.pi / 2, None, AD))
                ch(ts(out, out, PI_SAFE, -PI_SAFE, ALU.min, ALU.max))

            ch(ts(sm(7), s5("lre"), -1e-4, None, ALU.min))
            ch(tt(sm(1), sm(7), sm(0), M))
            ch(tt(sm(8), s5("lim"), sm(0), M))
            reduced(sm(2), sm(8), sm(9), 0)
            ch(ts(sm(10), sm(8), 0.0, None, AD))
            reduced(sm(3), sm(10), sm(9), 1)
            ch.then(ts(sm(9), sm(9), 0.0, None, M), "s5_arg")
            dve.wait_ge(sem("s5_trig"), 1)
            ch(dve.memset(pw[:, 0, 0], 1.0))
            ch(dve.memset(pw[:, 1, 0], 0.0))
            ch(tt(pw[:, 0, 1], sm(4), sm(6), M))
            ch(tt(pw[:, 1, 1], sm(4), sm(5), M))

            def p_(a, b):
                return pw[:, 0, a:b], pw[:, 1, a:b]

            def pb(a, n):
                return tuple(pw[:, r, a:a + 1].broadcast_to([P, n, NT5]) for r in range(2))
            tq = at(r10 + NT5 * 11, 4 * NT5).rearrange("p (j t) -> p j t", j=4)
            cmul(p_(2, 3), p_(1, 2), p_(1, 2), tq[:, 0:1])
            cmul(p_(3, 5), p_(1, 3), pb(2, 2), tq[:, 0:2])
            cmul(p_(5, 9), p_(1, 5), pb(4, 4), tq)
            A8, B8 = tiles(tmp5, 2, NT5), tiles(tmp5 + 64, 2, NT5)
            ch(dve.tensor_copy(A8[:, 0], pw[:, 0, 8]))
            ch(dve.tensor_copy(A8[:, 1], pw[:, 0, 8]))
            ch(ts(B8[:, 0], pw[:, 1, 8], -1.0, None, M))
            ch.then(dve.tensor_copy(B8[:, 1], pw[:, 1, 8]), "lam8_ready")
            ch(tt(sm(15), sm(7), sm(7), M))
            ch(tt(sm(16), s5("lim"), s5("lim"), M))
            ch(tt(sm(15), sm(15), sm(16), AD))
            ch(dve.reciprocal(sm(16), sm(15)))
            ch(ts(sm(17), pw[:, 0, 1], -1.0, None, AD))
            ch(tt(sm(18), sm(7), sm(16), M))
            ch(tt(sm(19), s5("lim"), sm(16), M))
            ch(ts(sm(19), sm(19), -1.0, None, M))
            cmul((sm(20), sm(21)), (sm(17), pw[:, 1, 1]), (sm(18), sm(19)), sm(22))

            def over(v):
                return v.rearrange("p (t c) -> p t c", c=1).broadcast_to([P, NT5, C5])
            tb = big[:, 0:512].rearrange("p (t c) -> p t c", c=C5)
            cmul((fb[:, 0], fb[:, 1]), (s5("br"), s5("bi")), (over(sm(20)), over(sm(21))), tb)
            for g2 in range(2):
                rows = slice(g2 * N5, (g2 + 1) * N5)
                ch(dve.tensor_copy(bdr[rows, :, g2 * C5:(g2 + 1) * C5], fb[rows, 0]))
                ch(dve.tensor_copy(bdi[rows, :, g2 * C5:(g2 + 1) * C5], fb[rows, 1]))
            cr_, ci_ = (s5(n).rearrange("p (g d) c -> p g d c", d=2) for n in ("cr", "ci"))
            for d in range(2):
                def lam(r):
                    v = pw[:, r, :].rearrange("p j (g d) -> p g d j", d=2)[:, :, d]
                    v = v if d == 0 else v[:, :, ::-1]
                    return v

                for g0 in range(0, GP, 8):
                    gs = slice(g0, g0 + 8)

                    def C(v):
                        return v[:, gs, d].unsqueeze(2).broadcast_to([P, 8, 9, C5])

                    def W(r):
                        return lam(r)[:, gs].unsqueeze(3).broadcast_to([P, 8, 9, C5])
                    t = big[:, 0:8 * 144].rearrange("p (g j c) -> p g j c", g=8, j=9)
                    o, q = ctr[:, gs, d], ctn[:, gs, d]
                    ch(tt(t, C(ci_), W(1), M))
                    ch(tt(o, C(cr_), W(0), M))
                    ch(tt(o, o, t, SU))
                    ch(tt(t, C(cr_), W(1), M))
                    ch(tt(q, C(ci_), W(0), M))
                    ch(stt(q.rearrange("p g j c -> p g (j c)"), q.rearrange("p g j c -> p g (j c)"), -1.0,
                           t.rearrange("p g j c -> p g (j c)"), M, SU))
            ch.then(ts(sm(23), sm(22), 0.0, None, M), "ctab_ready")
            ch.then(ts(sm(23), sm(22), 0.0, None, M), "s5_params_used")
            for half in range(2):
                dve.wait_ge(sem("kk_mm"), half + 1)
                for b in range(4):
                    src = ps[0:2 * C5, 3 + b, :].rearrange("p (g d j c) -> p g d j c", d=2, j=T5, c=C5)
                    gs = slice(8 * half + 2 * b, 8 * half + 2 * b + 2)
                    ch(dve.tensor_copy(kk[:, gs, 0:7], src[:, :, 1, 0:7]))
                    ch(dve.tensor_copy(kk[:, gs, 7], src[:, :, 1, 7]))
                    ch(tt(kk[:, gs, 7], kk[:, gs, 7], src[:, :, 0, 0], AD))
                    ins = dve.tensor_copy(kk[:, gs, 8:15], src[:, :, 0, 1:8])
                    if half == 0 and b == 3:
                        ch.then(ins, "kk_half")
                    else:
                        ch(ins)
            ch.then(dve.memset(sm(23), 0.0), "bd_used")
            td = big[0:32, 0:GP * C5].rearrange("p (g c) -> p g c", c=C5)
            ch(tt(td, col("s5d", 0, GP, 32).unsqueeze(2).broadcast_to([32, GP, C5]),
                  cst("eye16", 32).unsqueeze(1).broadcast_to([32, GP, C5]), M))
            ch.then(tt(kk[:, :, 7], kk[:, :, 7], td, AD), "kk_ready")
            for q in range(4):
                if q >= 2:
                    dve.wait_ge(sem("bt_turned"), 4 * (q - 1))
                for d in range(2):
                    gs = slice(4 * q, 4 * q + 4)

                    def B(r):
                        return fb[:, r].rearrange("p (g d) c -> p g d c", d=2)[:, gs, d].unsqueeze(2).broadcast_to([P, 4, T5, C5])

                    def W(r):
                        v = pw[:, r, 0:8].rearrange("p j (g d) -> p g d j", d=2)[:, gs, d]
                        v = v[:, :, ::-1] if d == 0 else v
                        return v.unsqueeze(3).broadcast_to([P, 4, T5, C5])
                    o = [bt[:, q % 2, r].rearrange("p (g d) (j c) -> p g d j c", d=2, c=C5)[:, :, d] for r in range(2)]
                    t = at(r11, 4 * TW).rearrange("p (g j c) -> p g j c", g=4, c=C5)
                    ch(tt(t, B(1), W(1), M))
                    ch(tt(o[0], B(0), W(0), M))
                    ch(tt(o[0], o[0], t, SU))
                    ch(tt(t, B(1), W(0), M))
                    ch(tt(o[1], B(0), W(1), M))
                    ins = tt(o[1], o[1], t, AD)
                    if d == 1:
                        if q == 0:
                            ch(ins)
                            ins = ts(sm(23), sm(22), 0.0, None, M)
                        ch.then(ins, "bt_ready")
                    else:
                        ch(ins)
            dve.wait_ge(sem("rms_ready"), 1)
            ch(dve.reciprocal(rs0, rs0))
            dve.wait_ge(sem("x_in"), 16)
            dve.wait_ge(sem("ctx_in"), 16)
            for v, src, r in ((hT[:, :, 0:L], cx, rs0[:, 0:L]), (hT[:, :, L:2 * L], xT, rs0[:, L:2 * L])):
                ch(tt(v, src, r.unsqueeze(1).broadcast_to([P, KD, L]), M))
            dve.wait_ge(sem("modc_ready"), NADC)
            ch(tt(modc, modc, col("ada_b", 0, 192).rearrange("p (c m) -> p c m", m=2), AD))
            for j in (1, 4):
                ch(ts(mod[:, :, j], mod[:, :, j], 1.0, None, AD))

            rms_n = [1]

            def inv_rms(n):
                rms_n[0] += 1
                dve.wait_ge(sem("rms_ready"), rms_n[0])
                ch(dve.reciprocal(rsx[:, 0:n], stx[:, 0:n]))

            def scaled(dst, src, r, li, m, jsh):
                ch(tt(dst, src, r.unsqueeze(1).broadcast_to([P, KD, L]), M))
                modulated(dst, li, m, jsh)

            def modulated(dst, li, m, jsh):
                for k in range(KD):
                    ch(ts(dst[:, k], dst[:, k], scol(li, jsh + 1, k, m), scol(li, jsh, k, m), M, AD))
            modulated(hT[:, :, 0:L], 0, 1, 0)
            modulated(hT[:, :, L:2 * L], 0, 0, 0)
            ch.then(ts(sm(23), sm(22), 0.0, None, M), "h_ready")
            dve.wait_ge(sem("proj_mm"), 7)
            ch.then(dve.tensor_copy(kvl, ps[:, 0, :]), "kvl_evicted")
            ch.then(dve.tensor_copy(krl, ps[0:QKH, 1, :]), "kvl_evicted")
            ch.then(dve.tensor_copy(ql.rearrange("p k t -> p (k t)"), ps[:, 2, :]), "kvl_evicted")
            dve.wait_ge(sem("lrms_ready"), 1)
            ch(dve.reciprocal(rsx, stx))
            ch.then(stt(kvl, kvl, col("kvn"), rsx, M, M), "kvl_normed")
            dve.wait_ge(sem("lrms_ready"), 2)
            ch(dve.reciprocal(rsx[:, 0:L], stx[:, 0:L]))
            ch(stt(ql[:, 0], ql[:, 0], col("qn", 0), rsx[:, 0:L], M, M))
            ch.then(stt(ql[:, 1], ql[:, 1], col("qn", 1), rsx[:, 0:L], M, M), "ql_normed")
            kbank = (0, 1, 2, 7)
            for h in range(HEADS):
                dve.wait_ge(sem("head_mm"), 4 + h + 1)
                ch.then(dve.tensor_copy(kh[0:NOPE, h], ps[0:NOPE, kbank[h % 4], :]), "kh_evicted")
            ch.then(dve.tensor_copy(kh[NOPE:QKH], krl[NOPE:QKH].unsqueeze(1).broadcast_to([ROPE, HEADS, 2 * L])), "kr_copied")
            dve.wait_ge(sem("qrms"), 1)
            ch.then(dve.reciprocal(rkq[:, 2 * L:3 * L], rkq[:, 2 * L:3 * L]), "qh_normed")
            dve.wait_ge(sem("qrms"), 2)
            ch.then(dve.reciprocal(rkq[:, 0:2 * L], rkq[:, 0:2 * L]), "kh_normed")
            for b in range(4):
                dve.wait_ge(sem("rot_mm"), 2 + b + 1)
                v = qh[:, 2 * b:2 * b + 2].rearrange("p h t -> p (h t)")
                ch.then(stt(v, v, col("qqk", rows=QKH), ps[0:QKH, 2 + b, :], M, M), "qh_normed")
            kr_bank = (0, 1, 6, 7)
            for h in range(HEADS):
                dve.wait_ge(sem("rot_mm"), 6 + h + 1)
                ch.then(stt(kh[:, h], kh[:, h], col("kqk", rows=QKH), ps[0:QKH, kr_bank[h % 4], :], M, M), "kh_normed")
            for first, banks, v in ((14, (2, 4), qh), (18, (0, 6), kh[:, :, L:2 * L])):
                dve.wait_ge(sem("rot_mm"), first + 4)
                tmp = sqk[:, 0:4].rearrange("p h t -> p (h t)").rearrange("p (h t) -> p h t", t=L)
                for i, b in enumerate(banks):
                    ch(tt(tmp[:, 4 * i:4 * i + 4], ps[0:QKH, b:b + 2, :].rearrange("p b (h t) -> p (b h) t", h=2),
                          cst("sin", QKH).unsqueeze(1).broadcast_to([QKH, HEADS // 2, L]), M))
                ch(tt(v, v, cst("cos", QKH).unsqueeze(1).broadcast_to([QKH, HEADS, L]), M))
                ch.then(tt(v, v, tmp, AD), "rope_done")

            def s5_out(i):
                dve.wait_ge(sem("y_mm"), 2 * i + 2)
                for b in range(2):
                    ch.then(dve.tensor_copy(ys[:, i].rearrange("p t (q b) c -> p b q t c", b=2)[:, b],
                                            ps[0:XCH, 5 + b, :].rearrange("p (q t c) -> p q t c", t=T5, c=C5)), "y_evicted")
            for n in range(2 * HEADS + 1):
                if n < 2 * HEADS:
                    dve.wait_ge(sem("scores_done"), n + 1)
                    ch(dve.tensor_reduce(at(r_st + 32, 1), ps[:, n % 2, :], AX.X, ALU.max))
                    ch.then(ts(at(r_st + n, 1), at(r_st + 32, 1), -QKH ** -0.5, None, M), "max_done")
                if n >= 1:
                    k = n - 1
                    dve.wait_ge(sem("exp_done"), k + 1)
                    ch(dve.reciprocal(at(r_st + 33, 1), at(r_st + 16 + k, 1)))
                    ch.then(ts(prob[:, k % 2], prob[:, k % 2], at(r_st + 33, 1), None, M), "prob_ready")
                if n >= 3 and n % 2 == 1:
                    attend_out(dve, ch, (n - 3) // 2)
                if n >= S5_AT + 2 and (n - S5_AT) % 2 == 0:
                    s5_out((n - S5_AT) // 2 - 1)
            attend_out(dve, ch, HEADS - 1)
            for i in range((2 * HEADS - S5_AT) // 2, 4):
                s5_out(i)
            for j in range(4):
                dve.wait_ge(sem("glu_sig"), j + 1)
                if j == 0:
                    dve.wait_ge(sem("glu_mm"), 4)
                ch.then(tt(zT[:, j], zT[:, j], yT.rearrange("p i t c -> p i (t c)")[:, j], M), "s5_out")
            for j in range(KD):
                dve.wait_ge(sem("mix_mm"), j // 2 * 2 + 2)
                ins = stt(xT[:, j], ps[:, j // 2, (j % 2) * L:(j % 2 + 1) * L], scol(0, 2, j), xT[:, j], M, AD)
                ch(ins) if j < KD - 1 else ch.then(ins, "x_mixed")

            def moe_dve(li):
                inv_rms(L)
                scaled(hX, xT, rsx[:, 0:L], li, 0, 3)
                ch.then(ts(at(rtb + 23 * 64, 1), at(r_eps, 1), 0.0, None, M), "moe_h")
                dve.wait_ge(sem("rexp"), li + 1)
                dve.wait_ge(sem("rw_in"), 48 * (li + 1))

                def T(i, n=1):
                    return at(rtb + NE * i, NE * n)
                ch(ts(T(2, 2), T(2, 2), 1.0, None, AD))
                ch(dve.reciprocal(T(2, 2), T(2, 2)))
                for t in range(2):
                    s_, b_, top, eq, cum = T(2 + t), T(4), at(rtb + NE * 5, 8), T(7), T(8)
                    gt, w_ = T(10 + t), T(12 + t)
                    need = at(rtb + NE * 9, 1)
                    ch(tt(b_, s_, T(0), AD))
                    ch(dve.max(top, b_))
                    ch(ts(gt, b_, top[:, TOPK - 1:TOPK], None, ALU.is_gt))
                    ch(ts(eq, b_, top[:, TOPK - 1:TOPK], None, ALU.is_equal))
                    ch(dve.tensor_reduce(need, gt, AX.X, AD))
                    ch(ts(need, need, -1.0, float(TOPK), M, AD))
                    ch(dve.tensor_tensor_scan(cum, eq, eq, 0.0, AD, ALU.bypass))
                    ch(ts(cum, cum, need, None, ALU.is_le))
                    ch(tt(eq, eq, cum, M))
                    ch.then(tt(gt, gt, eq, AD), "route")
                    ch(tt(w_, gt, s_, M))
                    ch(dve.tensor_reduce(need, w_, AX.X, AD))
                    ch(dve.reciprocal(need, need))
                    ch(ts(rt[:, t, :, 1], w_, need, ROUTE_SCALE, M, M))
                    ch(ts(rt[:, t, :, 0], gt, 0.0, mcst("tok", t, 1), M, AD))
                    ch(dve.tensor_tensor_scan(cum, gt, gt, 0.0, AD, ALU.bypass))
                    ch(tt(cum, cum, gt, SU))
                    ch(dve.tensor_copy(rparts[:, t, :, 1], cum))
                    ch(ts(rt[:, t, :, 2], cum, mcst("row", t, 1), None, AD))
                rest = T(21, 2).rearrange("p (t e) -> p t e", t=2)
                ch(dve.tensor_copy(rparts[:, :, :, 0], rt[:, :, :, 0]))
                ch(dve.tensor_copy(rparts[:, :, :, 2], rt[:, :, :, 1]))
                ch(tt(rest, rt[:, :, :, 1], rparts[:, :, :, 2], SU))
                ch(dve.tensor_copy(rparts[:, :, :, 3], rest))
                ch(tt(rest, rest, rparts[:, :, :, 3], SU))
                ch(dve.tensor_copy(rparts[:, :, :, 4], rest))
                dve.wait_ge(sem("pos_mm"), li + 1)
                for t in range(2):
                    ch(stt(pos[:, t], ps[:, 7, t * NE:(t + 1) * NE], 1.0, T(10 + t), AD, M))
                    ch(ts(pos[:, t], pos[:, t], -1.0, None, AD))
                ch(dve.tensor_reduce(at(rtb + NE * 9, 1), ps[:, 7, 2 * NE:3 * NE], AX.X, ALU.max))
                ch(dve.tensor_copy(flags[:, li:li + 1], at(rtb + NE * 9, 1, 1)))

                def one_hot(out, slots, e):
                    return tt(out, slots.unsqueeze(1).broadcast_to([P, 2, S]), pos[:, :, bass.ds(e, 1)].broadcast_to([P, 2, S]), ALU.is_equal)

                def one_hots(b, e):
                    for t in range(2):
                        ins = tt(selg[:, b, t], mcst("iota").unsqueeze(1).broadcast_to([P, SG, S]),
                                 pos[:, t, bass.ds(e, SG)].unsqueeze(2).broadcast_to([P, SG, S]), ALU.is_equal)
                    ins.then_inc(sem("sel_ready"), 1)

                NG = NE // SG
                for q in range(NG):
                    if q >= 2:
                        dve.wait_ge(sem("tab_mm"), li * NG + q - 1)
                    one_hots(q % 2, q * SG)
                dve.wait_ge(sem("tab_mm"), NG * (li + 1))

                def indices(gidx, sidx, weight, src, empty, step_):
                    step_(ts(empty, src[:, :, 0], 0.0, mcst("beyond")[0:S], ALU.is_equal, M))
                    step_(tt(empty, empty, src[:, :, 0], AD))
                    step_(ts(gidx, empty, -1.0, None, AD))
                    step_(ts(empty, src[:, :, 2], 0.0, mcst("beyond")[0:S], ALU.is_equal, M))
                    step_(tt(empty, empty, src[:, :, 2], AD))
                    step_(ts(sidx, empty, -1.0, None, AD))
                    step_(dve.tensor_copy(weight, src[:, :, 1]))
                tab = ps[0:S, 7, 0:NR * NE].rearrange("p (e c) -> p e c", c=NR)
                tok = T(14)[0:S]
                ch(ts(tok, tab[:, :, 0], 0.0, mcst("beyond")[0:S], ALU.is_equal, M))
                ch(tt(tok, tok, tab[:, :, 0], AD))
                ch(ts(idx[:, 0], tok, -1.0, None, AD))
                ch(ts(tok, tok, float(RPT), -float(RPT), M, AD))
                ch(tt(idx[:, 1], tok, tab[:, :, 1], AD))
                ch(dve.tensor_copy(wtab, tab[:, :, 2]))
                ch(tt(wtab, wtab, tab[:, :, 3], AD))
                ch(tt(wtab, wtab, tab[:, :, 4], AD))
                ch.then(dve.memset(T(15), 0.0), "idx_ready")

                def step(n, i):
                    def at_least(name, count, per=NB):
                        dve.wait_ge(sem(name), li * per + count + 4 * i)

                    def turned_next(m):
                        at_least("tx_mm", m - 1, NE)
                        if n - 1 >= 2:
                            at_least("gu_mm", n)
                        dve.tensor_copy(xgT[:, m % 2, 4:8].rearrange("p k t -> p (k t)"), ps[:, 1, 0:4 * S]).then_inc(sem("xt_dve"), 1)
                    if 3 <= n + 1 < NB:
                        turned_next(n + 1)
                    if n < NB:
                        at_least("sg_ready", n + 1)
                        if n >= 2:
                            at_least("ht_mm", n - 1)
                        if n < 2:
                            ins = tt(hh[:, n % 2], sg[:, n % 2], ps[:, 2 + n % 2, FF:2 * FF], M)
                        else:
                            ins = stt(hh[0:S, n % 2], sg[0:S, n % 2], wtab[:, bass.ds(n - 2 + 4 * i, 1)], ps[0:S, 2 + n % 2, FF:2 * FF], M, M)
                        ins.then_inc(sem("h_done"), 1)
                    if n >= 1:
                        at_least("dn_mm", n)
                        if n >= 7:
                            dve.wait_ge(sem(f"scat{(n - 1) % GD}"), 16 * (li * (NE // GD) + (n - 7) // GD + 1) + 16 * i)
                        dst = ysh[:, n - 1, 0:512] if n <= 2 else yb[0:S, (n - 1) % GD, 0:512]
                        dve.tensor_copy(dst, ps[0:rows_of(n - 1), 5, :]).then_inc(sem("y_dve"), 1)
                    if n == 1:
                        turned_next(2)
                steady(step, dve)
                for b in range(GD):
                    dve.wait_ge(sem(f"scat{b}"), 16 * (NE // GD) * (li + 1))
                def more(s, i):
                    ovd, ovp = sem(f"ov_d{li}"), sem(f"ov_p{li}")
                    base, own = NE * (s - 1), [0]

                    def oc(ins):
                        own[0] += 1
                        ins.then_inc(ovd, 1)
                        dve.wait_ge(ovd, i * OVD + OVD * base + own[0])
                    oc(one_hot(sel[:, 0], mcst("iota_more", (s - 1) * S, S), i))
                    oc(dve.tensor_copy(sel[:, 1, :, 0:3], rt[:, :, bass.ds(i, 1)].rearrange("p t e c -> p t (e c)")))
                    dve.wait_ge(ovp, i * 5 + 5 * base + 1)
                    indices(ib[:, 0:1], ib[:, GD:GD + 1], ov[:, 0:1], ps[0:S, 7, 0:3].rearrange("p (e c) -> p e c", c=3), ov[:, 1:2], oc)
                    oc(dve.memset(ov[:, 2:3], 0.0))
                    dve.wait_ge(ovp, i * 5 + 5 * base + 2)
                    oc(dve.tensor_copy(xgT[:, 0].rearrange("p (h k) t -> p h (k t)", h=2), ps[:, 0:2, 0:4 * S]))
                    dve.wait_ge(sem(f"ov_a{li}"), i + base + 1)
                    oc(stt(hh[0:S, 0], sg[0:S, 0], ov[:, 0:1], ps[0:S, 2, FF:2 * FF], M, M))
                    dve.wait_ge(ovp, i * 5 + 5 * base + 4)
                    oc(dve.tensor_copy(hT2[:, 0, :, 0:S], ps[:, 4, 0:2 * S].rearrange("p (f t) -> p f t", f=2)))
                    dve.wait_ge(ovp, i * 5 + 5 * base + 5)
                    oc(dve.tensor_copy(yb[0:S, 0], ps[0:S, 5:7, :].rearrange("p b n -> p (b n)")))
                    oc(dve.memset(ov[:, 2:3], 0.0))
                    dve.wait_ge(sem(f"ov_q{li}"), i * 32 + 32 * (base + 1))
                overflow(li, dve, more)
                for k in range(RPT):
                    for part, (k0, k1) in enumerate(ROW_PARTS):
                        if k == k0:
                            dve.wait_ge(sem(f"rows_in{part}"), 32 * (li + 1))
                    ins = tt(xg[:, 0], ysh[:, 0] if k == 0 else xg[:, 0], wring[:, 0, k * D:(k + 1) * D], AD)
                    ch(ins) if k < RPT - 1 else ch.then(ins, "sum_dve")
                dve.wait_ge(sem("out_mm"), 2 * (li + 1))
                for j in range(KD):
                    ins = stt(xT[:, j], ps[:, j // 2, (j % 2) * L:(j % 2 + 1) * L], scol(li, 5, j), xT[:, j], M, AD)
                    ch(ins) if j < KD - 1 else ch.then(ins, "moe_x")

            moe_dve(0)
            inv_rms(L)
            scaled(hX, xT, rsx[:, 0:L], 1, 0, 0)
            ch.then(ts(at(hsc, 1), at(r_eps, 1), 0.0, None, M), "hy_h")

            def filter_argument(i):
                dve.wait_ge(sem("filter_mm"), i + 1)
                if i == 1:
                    dve.wait_ge(sem("hid_ready"), 1)
                a, t = at(hsc + L, L, FH), at(hsc + 2 * L, L, FH)
                ch(ts(a, ps[0:FH, 4 + i, 0:L], col("fb1" if i == 0 else "fb2", rows=FH), col("freq", rows=FH), AD, M))
                reduced(at(hsc, L, FH), a, t, 0)
                ch.then(ts(t, t, 0.0, None, M), "hid_arg")

            def filter_decay(t):
                for j in range(4):
                    dve.wait_ge(sem("filter_mm"), 2 + 4 * t + j + 1)
                    ch.then(tt(hf[:, 2 * (j // 2) + t, (j % 2) * 512:(j % 2 + 1) * 512], ps[:, 4 + j, :],
                               hcst("decay")[:, t, (j % 2) * 512:(j % 2 + 1) * 512], M), "hf_ready")

            def filter_directions():
                dve.wait_ge(sem("squared"), 8 + 1)
                dve.wait_ge(sem("filter_mm"), 10 + 1)
                ch(tt(zs, hf[:, 0:2], hf[:, 2:4], SU))
                ch(tt(hf[:, 0:2], hf[:, 0:2], hf[:, 2:4], AD))
                ch.then(dve.tensor_copy(hf[:, 2:4], zs), "hf_comb")

            for i in range(6):
                dve.wait_ge(sem("hyp_evicted"), i + 1)
                for j in range(4):
                    c = 4 * i + j
                    p_in, o = pp[:, i % 2, j], xc[:, c]
                    ch(ts(o, p_in, col("convw", 24 + c), col("convb", c), M, AD))
                    ch(stt(o[:, 1:L], p_in[:, 0:L - 1], col("convw", c), o[:, 1:L], M, AD))
                    ins = stt(o[:, 0:L - 1], p_in[:, 1:L], col("convw", 48 + c), o[:, 0:L - 1], M, AD)
                    ch(ins) if j < 3 else ch.then(ins, "conv_done")
                if i < 2:
                    filter_argument(i)
                elif i < 4:
                    filter_decay(i - 2)
                elif i == 4:
                    filter_directions()
            dve.wait_ge(sem("hn_read"), 1)
            ch(dve.reciprocal(hns, hns))
            ch.then(tt(zt, xc[:, 8:16], xc[:, 16:24], M), "z_conv")
            dve.wait_ge(sem("Z_mm"), 8)
            ZR = ps[:, 0:4, :].rearrange("p (m c) n -> p m (c n)", m=2)
            ZS = ps[:, 4:8, :].rearrange("p (m c) n -> p m (c n)", m=2)
            ch(tt(YR, ZR, HR, M))
            ch(tt(ytmp, ZS, HS, M))
            ch(tt(YR, YR, ytmp, SU))
            ch(tt(YS, ZR, HS, M))
            ch(tt(ytmp, ZS, HR, M))
            ch.then(tt(YS, YS, ytmp, AD), "Y_ready")
            for j in range(KD):
                dve.wait_ge(sem("conv_mm"), j // 2 * 2 + 2)
                ch(ts(zt[:, j], zt[:, j], col("hybias", j), None, M))
                ch(stt(zt[:, j], ps[:, j // 2, (j % 2) * L:(j % 2 + 1) * L], hns[:, j:j + 1], zt[:, j], M, AD))
                ch.then(tt(zt[:, j], zt[:, j], xc[:, j], M), "yh_ready")
            for j in range(KD):
                dve.wait_ge(sem("mix_mm"), 8 + j // 2 * 2 + 2)
                ins = stt(xT[:, j], ps[:, 4 + j // 2, (j % 2) * L:(j % 2 + 1) * L], scol(1, 2, j), xT[:, j], M, AD)
                ch(ins) if j < KD - 1 else ch.then(ins, "x_mixed")
            moe_dve(1)


def tiles_of(w):
    k, n = w.shape
    return np.ascontiguousarray(w.reshape(k // P, P, n).transpose(1, 0, 2))


def columns(v):
    return v.reshape(-1, P).T


def constants():
    c = np.zeros((P, NCST), np.float32)

    def put(name, v):
        a, w = CST[name]
        c[:v.shape[0], a:a + w] = v
    put("ident", np.eye(P, dtype=np.float32))
    t = np.arange(L)
    nf = ROPE // 4
    inv = (10000.0 ** (-np.arange(nf, dtype=np.float32) / nf)).astype(np.float32)
    ang = np.concatenate([(t // 64).astype(np.float32)[:, None] * inv, (t % 64).astype(np.float32)[:, None] * inv], -1).T
    cos, sin = np.ones((QKH, L), np.float32), np.zeros((QKH, L), np.float32)
    cos[NOPE:] = np.repeat(np.cos(ang), 2, 0)
    sin[NOPE:] = np.repeat(np.sin(ang), 2, 0)
    swap = np.zeros((QKH, QKH), np.float32)
    for i in range(NOPE, QKH, 2):
        swap[i + 1, i] = -1.0
        swap[i, i + 1] = 1.0
    put("cos", cos)
    put("sin", sin)
    put("swap", swap)
    put("eye16", np.tile(np.eye(C5, dtype=np.float32), (2, 1)))
    put("pick", np.repeat(np.arange(2 * HEADS - 1, dtype=np.float32)[None] == HEADS - 1, P, 0))
    return c


def hyena_constants():
    c = np.zeros((P, NHCST), np.float32)

    def put(name, v):
        a, w = HCST[name]
        c[:v.shape[0], a:a + w] = v.reshape(v.shape[0], -1)
    n, k = np.arange(L, dtype=np.float64), np.arange(L) + 0.5
    w = 2 * np.pi / (2 * L) * np.outer(n, k)
    C, S = np.cos(w).astype(np.float32), np.sin(w).astype(np.float32)
    put("fc", tiles_of(C))
    put("fs", tiles_of(S))
    put("ic", tiles_of(np.ascontiguousarray(C.T) / np.float32(L)))
    put("is", tiles_of(np.ascontiguousarray(S.T) / np.float32(L)))
    t = np.linspace(0.0, 1.0, L, dtype=np.float32)[:, None]
    deltas = np.linspace(-math.log(1e-2) / 1.5, -math.log(1e-2) / 0.3, HYW, dtype=np.float32)
    put("decay", tiles_of(np.exp(-t * deltas).astype(np.float32)))
    ang = (2.0 * math.pi * np.arange(L, dtype=np.float32)[:, None] / L).astype(np.float32)
    bands = np.linspace(1e-4, (FE - 1) // 2 - 1, (FE - 1) // 2, dtype=np.float32)
    z = np.concatenate([t, np.cos(bands * ang), -np.sin(bands * ang)], -1).astype(np.float32)
    put("zemb", np.ascontiguousarray(z.T))
    return c


def routing_constants():
    c = np.zeros((P, NMCST), np.float32)
    p = np.arange(P, dtype=np.float32)[:, None]
    for name, v in (("tri", np.triu(np.ones((P, P)), 1)), ("iota", p.T[:, :S]), ("iota_more", np.arange(S, L)[None]), ("tok", p + [1, 1 + P]),
                    ("row", p * RPT + [1, 1 + P * RPT]), ("beyond", p + 1e6)):
        a, w = MCST[name]
        c[:, a:a + w] = v
    return c


def laid_out(i):
    i = {k: np.asarray(v) for k, v in i.items()}
    cols = np.zeros((P, NCOLS), np.float32)

    def put(name, v, rows=P):
        a, w = COLS[name]
        cols[:rows, a:a + w] = v
    put("ada_b", np.repeat(i["ada_b"].reshape(96, P).T[:, :, None], 2, 2).reshape(P, 192))
    put("c", np.stack([columns(i["c"][0]), columns(i["c_ctx"])], 2).reshape(P, 16))
    put("qn", columns(i["mla_q_norm"][0]))
    put("kvn", columns(i["mla_kv_norm"][0]))
    put("qqk", i["mla_q_qknorm"][0][:, None], QKH)
    put("kqk", i["mla_k_qknorm"][0][:, None], QKH)
    put("glub", columns(i["s5_glu_b"][0]))
    put("convw", i["hy_conv_w"][0].reshape(3 * 24, P).T)
    put("convb", columns(i["hy_conv_b"][0]))
    put("hybias", columns(i["hy_bias"][0]))
    put("fb1", i["hy_f_b1"][0][:, None], FH)
    put("fb2", i["hy_f_b2"][0][:, None], FH)
    put("freq", i["hy_f_freq"][0][:, None], FH)
    put("s5d", i["s5_d"][0].reshape(GP, 2 * C5).T, 2 * C5)
    s5p = np.zeros((P, NS5P), np.float32)

    def put5(name, v):
        a, w = S5P[name]
        v = v.reshape((2, GP, 2, N5) + v.shape[3:])
        v = np.moveaxis(v, (2, 3, 1, 0), (0, 1, 2, 3))
        s5p[:, a:a + w] = v.reshape(P, w)
    put5("lre", i["s5_lam_re"][0])
    put5("lim", i["s5_lam_im"][0])
    put5("lst", np.broadcast_to(i["s5_log_step"][0][:, :, None], (2, G5, N5)))
    put5("br", i["s5_b_re"][0])
    put5("bi", i["s5_b_im"][0])
    put5("cr", i["s5_c_re"][0].transpose(0, 1, 3, 2))
    put5("ci", i["s5_c_im"][0].transpose(0, 1, 3, 2))

    def weights(gate, up, down):
        lead = gate.shape[:-2]
        g, u = (w.reshape(lead + (KD, P, FF)) for w in (gate, up))
        d = down.reshape(lead + (FF // P, P, D))
        n = len(lead)
        gu = np.concatenate([g, u], -1)
        return np.concatenate([np.moveaxis(w, n, n + 1).reshape(lead + (P, -1)) for w in (gu, d)], -1)
    return {
        "cols": cols, "s5p": s5p, "cst": constants(), "hcst": hyena_constants(), "mcst": routing_constants(),
        "ada_w": np.ascontiguousarray(i["ada_w"].reshape(2, KD, P, 12, ADC).transpose(0, 3, 2, 1, 4)).reshape(NADC, P, KD, ADC),
        "xT": tiles_of(np.ascontiguousarray(i["x"][0].T)), "ctxT": tiles_of(np.ascontiguousarray(i["ctx"][0].T)),
        "w_in": tiles_of(i["ev_w_in"][0]), "w_uq": tiles_of(i["mla_w_uq"][0]), "w_ukv": i["mla_w_ukv"][0],
        "glu_w": tiles_of(i["s5_glu_w"][0]), "ev_w_out": tiles_of(i["ev_w_out"][0]),
        "hy_w_in": np.ascontiguousarray(i["hy_w_in"][0].reshape(KD, P, 6, 512).transpose(2, 1, 0, 3)),
        "hy_w_out": tiles_of(i["hy_w_out"][0]), "f_w1": i["hy_f_w1"][0], "f_w2": i["hy_f_w2"][0], "f_w3": i["hy_f_w3"][0],
        "router_w": np.ascontiguousarray(i["moe_router_w"].reshape(2, KD, P, NE).transpose(0, 2, 1, 3)),
        "router_b": i["moe_router_b"],
        "w_experts": weights(i["moe_w_gate"], i["moe_w_up"], i["moe_w_down"]),
        "w_shared": weights(i["moe_sh_gate"], i["moe_sh_up"], i["moe_sh_down"]),
    }


def kernel(**inputs):
    import concourse.bacc as bacc
    from concourse.bass_utils import run_bass_kernel_spmd

    nc = bacc.Bacc("TRN2", target_bir_lowering=False, num_devices=1)
    arrays = {f"in_{k}": np.ascontiguousarray(v) for k, v in laid_out(inputs).items()}
    A = {k[3:]: nc.dram_tensor(k, v.shape, mybir.dt.from_np(v.dtype), kind="ExternalInput").ap() for k, v in arrays.items()}
    A["out"] = nc.dram_tensor("out_x", (P, KD, L), F32, kind="ExternalOutput").ap()
    program(nc, A)
    r = run_bass_kernel_spmd(nc, [arrays], core_ids=[0])
    y = r.results[0]["out_x"]
    return np.ascontiguousarray(y.transpose(2, 1, 0).reshape(1, L, D))
```
